# Optimizing a Trainium2 kernel written in Bass

```python
import jax, jax.numpy as jnp
from jax import lax
import numpy as np

D_MODEL = 1024
BATCH = 1
SEQ = 1024
DEPTH = 1
DEC_BATCH = 1
DEC_SEQ = 1024
PAST_LEN = 128

N_HEADS_A = 8
HEAD_DIM_A = 64
DILATED_CONFIGS = ((128, 1), (512, 4), (2048, 16))
N_HEADS_B = 8
Q_LORA_RANK = 256
KV_LORA_RANK = 128
QK_NOPE_DIM = 64
QK_ROPE_DIM = 32
V_HEAD_DIM = 64

WIDTH_A = N_HEADS_A * HEAD_DIM_A
WIDTH_B = N_HEADS_B * V_HEAD_DIM
MIX_WIDTH = WIDTH_A + WIDTH_B
IN_PROJ_WIDTH = 3 * WIDTH_A + Q_LORA_RANK + KV_LORA_RANK + QK_ROPE_DIM
D_FF = 2816
CONV_WIDTH = 3

ROPE_THETA = 10000.0
EPS = 1e-6
Q_BLOCK = 128
NEG = -1e30

kernel_name = "hymba_dilated_mla_convffn_encoder"

def rmsnorm(x, g):
    xf = x.astype(jnp.float32)
    y = xf * lax.rsqrt(jnp.mean(xf * xf, axis=-1, keepdims=True) + EPS)
    return (y * g.astype(jnp.float32)).astype(x.dtype)

def rope(t):
    s, dim = t.shape[1], t.shape[-1]
    half = dim // 2
    inv_freq = ROPE_THETA ** (-jnp.arange(half, dtype=jnp.float32) * (2.0 / dim))
    ang = jnp.arange(s, dtype=jnp.float32)[:, None] * inv_freq[None, :]
    cos = jnp.cos(ang)[None, :, None, :]
    sin = jnp.sin(ang)[None, :, None, :]
    tf = t.astype(jnp.float32)
    t1, t2 = tf[..., :half], tf[..., half:]
    return jnp.concatenate([t1 * cos - t2 * sin, t2 * cos + t1 * sin], axis=-1).astype(t.dtype)

def window_attention(q, k, v, radius):
    n, l, h, hd = q.shape
    blk = radius
    nb = -(-l // blk)
    lp = nb * blk
    qb = jnp.pad(q, ((0, 0), (0, lp - l), (0, 0), (0, 0))).reshape(n, nb, blk, h, hd)
    pad_kv = ((0, 0), (blk, lp - l + blk), (0, 0), (0, 0))
    kp = jnp.pad(k, pad_kv).reshape(n, nb + 2, blk, h, hd)
    vp = jnp.pad(v, pad_kv).reshape(n, nb + 2, blk, h, hd)
    kb = jnp.concatenate([kp[:, :-2], kp[:, 1:-1], kp[:, 2:]], axis=2)
    vb = jnp.concatenate([vp[:, :-2], vp[:, 1:-1], vp[:, 2:]], axis=2)
    sc = jnp.einsum('nbqhd,nbkhd->nbhqk', qb, kb, preferred_element_type=jnp.float32) * (hd ** -0.5)
    qpos = jnp.arange(nb)[:, None] * blk + jnp.arange(blk)[None, :]
    kpos = jnp.arange(nb)[:, None] * blk - blk + jnp.arange(3 * blk)[None, :]
    rel = kpos[:, None, :] - qpos[:, :, None]
    valid = (jnp.abs(rel) <= radius) & (kpos[:, None, :] >= 0) & (kpos[:, None, :] < l)
    sc = jnp.where(valid[None, :, None], sc, NEG)
    m = jnp.max(sc, axis=-1, keepdims=True)
    p = jnp.exp(sc - m)
    den = jnp.sum(p, axis=-1)
    o = jnp.einsum('nbhqk,nbkhd->nbqhd', p, vb.astype(jnp.float32))
    o = o / jnp.transpose(den, (0, 1, 3, 2))[..., None]
    lse = jnp.transpose(m[..., 0] + jnp.log(den), (0, 1, 3, 2))
    return o.reshape(n, lp, h, hd)[:, :l], lse.reshape(n, lp, h)[:, :l]

def dilated_attention(q, k, v):
    b, s, h, hd = q.shape
    outs, lses = [], []
    for window, dil in DILATED_CONFIGS:
        radius = window // 2 // dil
        ls = s // dil

        def to_res(t):
            return t.reshape(b, ls, dil, h, hd).transpose(0, 2, 1, 3, 4).reshape(b * dil, ls, h, hd)

        o, lse = window_attention(to_res(q), to_res(k), to_res(v), radius)
        outs.append(o.reshape(b, dil, ls, h, hd).transpose(0, 2, 1, 3, 4).reshape(b, s, h, hd))
        lses.append(lse.reshape(b, dil, ls, h).transpose(0, 2, 1, 3).reshape(b, s, h))
    wts = jax.nn.softmax(jnp.stack(lses, axis=0), axis=0)
    out = jnp.sum(wts[..., None] * jnp.stack(outs, axis=0), axis=0)
    return out.astype(q.dtype)

def dense_attention(q, k, v):
    b, s, h, dk = q.shape
    dv = v.shape[-1]
    nb = s // Q_BLOCK
    qb = q.reshape(b, nb, Q_BLOCK, h, dk).transpose(1, 0, 2, 3, 4)
    scale = dk ** -0.5

    def one_block(qblk):
        sc = jnp.einsum('bqhd,bkhd->bhqk', qblk, k, preferred_element_type=jnp.float32) * scale
        p = jax.nn.softmax(sc, axis=-1)
        return jnp.einsum('bhqk,bkhd->bqhd', p.astype(v.dtype), v, preferred_element_type=jnp.float32)

    o = lax.map(one_block, qb)
    return o.transpose(1, 0, 2, 3, 4).reshape(b, s, h, dv).astype(q.dtype)

def depthwise_conv(u, w, bias):
    c = u.shape[-1]
    y = lax.conv_general_dilated(u, w[:, None, :], window_strides=(1,),
                                 padding=((CONV_WIDTH // 2, CONV_WIDTH // 2),),
                                 dimension_numbers=('NWC', 'WIO', 'NWC'),
                                 feature_group_count=c)
    return y + bias

def encoder_layer(x, g_attn, w_in, g_q_lora, w_uq, g_kv_lora, w_ukv, g_out_a, g_out_b, w_o,
                  g_ffn, w_up, w_conv, b_conv, w_down):
    b, s, _ = x.shape
    hn = rmsnorm(x, g_attn)
    proj = hn @ w_in
    splits = np.cumsum([WIDTH_A, WIDTH_A, WIDTH_A, Q_LORA_RANK, KV_LORA_RANK]).tolist()
    qa, ka, va, c_q, c_kv, k_rope = jnp.split(proj, splits, axis=-1)
    qa = rope(qa.reshape(b, s, N_HEADS_A, HEAD_DIM_A))
    ka = rope(ka.reshape(b, s, N_HEADS_A, HEAD_DIM_A))
    va = va.reshape(b, s, N_HEADS_A, HEAD_DIM_A)
    o_a = dilated_attention(qa, ka, va).reshape(b, s, WIDTH_A)
    qb = (rmsnorm(c_q, g_q_lora) @ w_uq).reshape(b, s, N_HEADS_B, QK_NOPE_DIM + QK_ROPE_DIM)
    q_nope, q_rot = qb[..., :QK_NOPE_DIM], rope(qb[..., QK_NOPE_DIM:])
    kv = (rmsnorm(c_kv, g_kv_lora) @ w_ukv).reshape(b, s, N_HEADS_B, QK_NOPE_DIM + V_HEAD_DIM)
    k_nope, vb = kv[..., :QK_NOPE_DIM], kv[..., QK_NOPE_DIM:]
    k_rot = jnp.broadcast_to(rope(k_rope[:, :, None, :]), (b, s, N_HEADS_B, QK_ROPE_DIM))
    o_b = dense_attention(jnp.concatenate([q_nope, q_rot], axis=-1),
                          jnp.concatenate([k_nope, k_rot], axis=-1), vb).reshape(b, s, WIDTH_B)
    mix = jnp.concatenate([rmsnorm(o_a, g_out_a), rmsnorm(o_b, g_out_b)], axis=-1) @ w_o
    x = x + mix
    u = depthwise_conv(rmsnorm(x, g_ffn) @ w_up, w_conv, b_conv)
    gate, val = u[..., :D_FF], u[..., D_FF:]
    x = x + (jax.nn.silu(gate) * val) @ w_down
    return x

def setup_inputs(seed: int = 0) -> dict:
    key = jax.random.key(seed)
    ks = jax.random.split(key, 20)
    f32 = jnp.float32

    def w(k, shape, fan_in):
        return jax.random.normal(k, shape, f32) * (fan_in ** -0.5)

    def gain(k, shape):
        return 1.0 + 0.1 * jax.random.normal(k, shape, f32)

    return {
        "x_prompt": jax.random.normal(ks[0], (BATCH, SEQ, D_MODEL), f32),
        "x_sample": jax.random.normal(ks[1], (DEC_BATCH, DEC_SEQ, D_MODEL), f32),
        "g_attn": gain(ks[2], (DEPTH, D_MODEL)),
        "w_in": w(ks[3], (DEPTH, D_MODEL, IN_PROJ_WIDTH), D_MODEL),
        "g_q_lora": gain(ks[4], (DEPTH, Q_LORA_RANK)),
        "w_uq": w(ks[5], (DEPTH, Q_LORA_RANK, N_HEADS_B * (QK_NOPE_DIM + QK_ROPE_DIM)), Q_LORA_RANK),
        "g_kv_lora": gain(ks[6], (DEPTH, KV_LORA_RANK)),
        "w_ukv": w(ks[7], (DEPTH, KV_LORA_RANK, N_HEADS_B * (QK_NOPE_DIM + V_HEAD_DIM)), KV_LORA_RANK),
        "g_out_a": gain(ks[8], (DEPTH, WIDTH_A)),
        "g_out_b": gain(ks[9], (DEPTH, WIDTH_B)),
        "w_o": w(ks[10], (DEPTH, MIX_WIDTH, D_MODEL), MIX_WIDTH),
        "g_ffn": gain(ks[11], (DEPTH, D_MODEL)),
        "w_up": w(ks[12], (DEPTH, D_MODEL, 2 * D_FF), D_MODEL),
        "w_conv": w(ks[13], (DEPTH, CONV_WIDTH, 2 * D_FF), CONV_WIDTH),
        "b_conv": 0.02 * jax.random.normal(ks[14], (DEPTH, 2 * D_FF), f32),
        "w_down": w(ks[15], (DEPTH, D_FF, D_MODEL), D_FF),
        "g_final": gain(ks[16], (D_MODEL,)),
    }

def reference(x_prompt, x_sample, g_attn, w_in, g_q_lora, w_uq, g_kv_lora, w_ukv, g_out_a, g_out_b,
              w_o, g_ffn, w_up, w_conv, b_conv, w_down, g_final):
    def trunk(x):
        for layer in range(DEPTH):
            x = encoder_layer(x, g_attn[layer], w_in[layer], g_q_lora[layer], w_uq[layer],
                              g_kv_lora[layer], w_ukv[layer], g_out_a[layer], g_out_b[layer],
                              w_o[layer], g_ffn[layer], w_up[layer], w_conv[layer], b_conv[layer],
                              w_down[layer])
        return rmsnorm(x, g_final)

    y_prompt = trunk(x_prompt)
    y_sample = trunk(x_sample)
    return (y_prompt, y_sample)


_drawn_inputs = setup_inputs


def setup_inputs(seed=0):
    import zlib

    import numpy as np

    out = dict(_drawn_inputs(seed))
    spreads = {}
    factors = {'b_conv': 5.052}
    for name, (base, spread) in spreads.items():
        noise = np.random.default_rng([zlib.crc32(name.encode()), seed]).standard_normal(out[name].shape)
        drawn = base * np.exp(spread * noise) if base else spread * noise
        out[name] = __import__('jax').numpy.asarray(drawn.astype(out[name].dtype))
    for name, factor in factors.items():
        out[name] = (out[name] * factor).astype(out[name].dtype)
    return out
```

```python
from contextlib import ExitStack

import concourse.bass as bass
from concourse import mybir

ALU = mybir.AluOpType
ACT = mybir.ActivationFunctionType
AXX = mybir.AxisListType.X
F32 = mybir.dt.float32
F32R = mybir.dt.float32r
BF16 = mybir.dt.bfloat16

P = 128
N_SEQ = 2
S = 1024
D = 1024
NT = S // P
NK = D // P
HEADS = 8
HA = 64
ROT = 32
HB = HA + ROT
WA = HEADS * HA
RQ, RKV = 256, 128
RC = RQ + RKV
F = 2816
NCH = F // (2 * P)
COL = 256
EPS = 1e-6
NEG_HUGE = -1e30
MASK_W = 2 * S - P
SCALE_A = float(HA) ** -0.5
SCALE_B = float(HB) ** -0.5

U_C, U_QK, U_V = 2, 4, 2
U_IN = U_C + U_QK + U_V
U_O = D // COL
U_ALL = U_IN + U_O
KV_COLS = RKV + ROT
EV_SEQ = (U_ALL - U_C) * NT
ROT_SEQ = (2 + U_QK) * NT

PHASES = 6
ENGINES = 4

LO_CREDIT = 2
EV_CREDIT = 4
YA_CREDIT = 2


def encoder_kernel(nc: bass.Bass, x_seqs, g_attn, w_in, g_q, w_uq, g_kv, w_ukv, g_out, w_o, g_ffn,
                   w_up, conv_wb, w_down, g_final, ident, stack_ident, cos_a, sin_a, cos_b, sin_b,
                   log_count, out):
    with ExitStack() as ctx:
        used = set()

        def place(name, shape, dt, offset_kb):
            return nc.alloc_sbuf_tensor_at(name, shape, dt, offset=BASE + int(offset_kb * 1024))

        def sem(name):
            return ctx.enter_context(nc.semaphore(name))

        BASE = 16512
        R_O, R_C, R_Q, R_X, R_REST = 3.5, 35.5, 67.5, 131.5, 195.5
        idn = place("idn", [P, P], F32, 0)
        stk = place("stk", [P, HA], F32, 0.5)
        cosb = place("cosb", [P, NT, ROT], F32, 0.75)
        sinb = place("sinb", [P, NT, ROT], F32, 1.75)
        ss = place("ss", [P, 32], F32, 2.75)
        sd = place("sd", [P, 32], F32, 2.875)
        rs = place("rs", [P, 32], F32, 3.0)
        mx = place("mx", [P, 4], F32, 3.125)
        nm = place("nm", [P, 4], F32, 3.15625)
        den = place("den", [P, 2, NT], F32, 3.1875)
        rden = place("rden", [P, 4], F32, 3.25)
        eps = place("eps", [P, 1], F32, 3.28125)
        cw = [place(f"cw{b}", [P, 4], F32, 3.3125 + b / 32) for b in range(4)]

        w_hi = [place(f"w_hi{i}", [P, NK, COL], F32R, R_O + 16 * i) for i in range(2)]
        w_lo = [place(f"w_lo{i}", [P, NK, COL], F32R, R_O + 16 * i + 8) for i in range(2)]
        ct_hi = place("ct_hi", [P, 3, S], F32R, R_C)
        ct_lo = place("ct_lo", [P, 3, S], F32R, R_C + 12)
        krot = place("krot", [P, NT, ROT], F32, R_C + 24)
        glora = place("glora", [P, RC], F32, R_C + 25)
        cr = [place(f"cr{i}", [P, RC + ROT], F32, R_C + 26.5 + 1.625 * i) for i in range(2)]
        junk = place("junk", [P, D], BF16, R_C + 29.75)
        qk = place("qk", [P, NT, 2 * WA], F32, R_Q)
        va = place("va", [P, NT, WA], F32, R_Q + 32)
        wst = place("wst", [P, NK, COL], F32, R_Q + 48)
        xt = [place(f"xt{i}", [P, D], F32, R_Q + 56 + 4 * i) for i in range(2)]
        at_hi = place("at_hi", [P, NK, S], F32R, R_X)
        at_lo = place("at_lo", [P, NK, S], F32R, R_X + 32)
        gin = place("gin", [P, D], F32, R_REST)
        cosa = place("cosa", [P, NT, HA], F32, R_REST + 4)
        sina = place("sina", [P, NT, HA], F32, R_REST + 6)
        pra = [place(f"pra{i}", [P, COL], F32, R_REST + 8 + 2 * i) for i in range(2)]
        prb = [place(f"prb{i}", [P, COL], F32, R_REST + 9 + 2 * i) for i in range(2)]

        o = place("o", [P, NT, D], F32, R_O)
        pt_hi = [place(f"pt_hi{i}", [P, NT, 2 * P], F32R, R_X + 16 * i) for i in range(2)]
        pt_lo = [place(f"pt_lo{i}", [P, NT, 2 * P], F32R, R_X + 16 * i + 8) for i in range(2)]
        q2 = [place(f"q2{i}", [P, S], F32R, R_X + 32 + 12 * i) for i in range(2)]
        khh = [place(f"khh{i}", [P, S], F32R, R_X + 36 + 12 * i) for i in range(2)]
        kll = [place(f"kll{i}", [P, S], F32R, R_X + 40 + 12 * i) for i in range(2)]
        logc = place("logc", [P, MASK_W], F32, R_X + 56)
        st_a = dict(q=place("stqa", [P, NT, P], F32, R_REST), k=place("stka", [P, NT, P], F32, R_REST + 4),
                    v=place("stva", [P, NT, HA], F32, R_C + 29))
        ot_a = place("ot_a", [P, 2 * P], F32, R_C + 31)
        v2_a = [place(f"v2a{i}", [P, NT, P], F32R, R_Q + 48 + 4 * i) for i in range(2)]
        pr_a = [place(f"pr_a{i}", [P, S], F32, R_Q + 56 + 4 * i) for i in range(2)]
        qh = [place(f"qh{i}", [P, S], F32R, R_X + 32 + 16 * i) for i in range(2)]
        ql = [place(f"ql{i}", [P, S], F32R, R_X + 36 + 16 * i) for i in range(2)]
        kh = [place(f"kh{i}", [P, S], F32R, R_X + 40 + 16 * i) for i in range(2)]
        kl = [place(f"kl{i}", [P, S], F32R, R_X + 44 + 16 * i) for i in range(2)]
        st_b = dict(q=place("stqb", [P, NT, HB], F32, R_C + 0), k=place("stkb", [P, NT, HB], F32, R_C + 3),
                    v=place("stvb", [P, NT, HA], F32, R_C + 6))
        ot_b = place("ot_b", [P, 2 * P], F32, R_C + 8)
        v2_b = [place(f"v2b{i}", [P, NT, P], F32R, R_C + 9 + 4 * i) for i in range(2)]
        pr_b = [place(f"pr_b{i}", [P, S], F32, R_C + 17 + 4 * i) for i in range(2)]

        qb = place("qb", [P, NT, HEADS * HB], F32, R_Q)
        kb = place("kb", [P, NT, HEADS * HB], F32, R_Q + 24)
        vb = place("vb", [P, NT, WA], F32, R_Q + 48)
        NUQ, NUKV = HEADS * HB, HEADS * 2 * HA
        uq_hi = place("uq_hi", [P, 2, NUQ], F32R, R_X)
        uq_lo = place("uq_lo", [P, 2, NUQ], F32R, R_X + 6)
        ukv_hi = place("ukv_hi", [P, NUKV], F32R, R_X + 12)
        ukv_lo = place("ukv_lo", [P, NUKV], F32R, R_X + 16)
        uq_st = place("uq_st", [P, 2, NUQ], F32, R_X + 20)
        ukv_st = place("ukv_st", [P, NUKV], F32, R_X + 26)
        pba = [place(f"pba{i}", [P, HEADS, ROT], F32, R_X + 30 + 2 * i) for i in range(2)]
        pbb = [place(f"pbb{i}", [P, HEADS, ROT], F32, R_X + 31 + 2 * i) for i in range(2)]

        x1 = place("x1", [P, NT, D], F32, R_C)
        wo_hi = [place(f"wo_hi{i}", [P, NK, COL], F32R, R_Q + 16 * i) for i in range(2)]
        wo_lo = [place(f"wo_lo{i}", [P, NK, COL], F32R, R_Q + 16 * i + 8) for i in range(2)]
        wost = place("wost", [P, NK, COL], F32, R_Q + 32)
        xn = [place(f"xn{i}", [P, D], F32, R_Q + 40 + 4 * i) for i in range(2)]
        gout = place("gout", [P, D], F32, R_Q + 48)
        gffn = place("gffn", [P, D], F32, R_Q + 52)
        junk2 = place("junk2", [P, D], BF16, R_Q + 56)

        wu_hi = [place(f"wu_hi{b}", [P, NK, P], F32R, R_Q + 8 * b) for b in range(4)]
        wu_lo = [place(f"wu_lo{b}", [P, NK, P], F32R, R_Q + 8 * b + 4) for b in range(4)]
        wd_hi = [place(f"wd_hi{f}", [P, D], F32R, R_Q + 32 + 8 * f) for f in range(2)]
        wd_lo = [place(f"wd_lo{f}", [P, D], F32R, R_Q + 36 + 8 * f) for f in range(2)]
        h_hi = [place(f"h_hi{f}", [P, S], F32R, R_Q + 48 + 8 * f) for f in range(2)]
        h_lo = [place(f"h_lo{f}", [P, S], F32R, R_Q + 52 + 8 * f) for f in range(2)]
        ust = [place(f"ust{i}", [P, D], F32, R_O + 4 * i) for i in range(3)]
        cg = place("cg", [P, S], F32, R_O + 12)
        cv = place("cv", [P, S], F32, R_O + 16)
        gfin = place("gfin", [P, D], F32, R_O + 20)
        junk3 = place("junk3", [P, D], BF16, R_O + 24)

        pair = [ctx.enter_context(nc.psum_tensor(f"pair{i}", [P, 2 * 512], F32)) for i in range(4)]

        def bank(i):
            return pair[i // 2][:, 512 * (i % 2):512 * (i % 2) + 512]

        s_phase, s_passed = sem("phase_ended"), sem("wait_passed")
        s_const, s_eps = sem("constants_landed"), sem("eps_set")
        s_x = [sem(f"x_tile_landed{i}") for i in range(2)]
        s_inw, s_wst, s_whi, s_wlo = sem("input_tables_landed"), sem("w_unit_landed"), sem("w_hi_split"), sem("w_lo_split")
        s_ss, s_std, s_rs, s_xn = sem("squares_summed"), sem("rms_ready"), sem("rrms_ready"), sem("tile_normalised")
        s_tr, s_ahi, s_alo = sem("tile_transposed"), sem("act_hi_split"), sem("act_lo_split")
        s_mm, s_eva, s_evd = sem("unit_product_ready"), sem("unit_evicted_by_act"), sem("unit_evicted_by_dve")
        s_css, s_cstd, s_crs, s_cn = sem("c_squares"), sem("c_rms"), sem("c_rrms"), sem("c_normalised")
        s_ctr, s_chi, s_clo, s_rot = sem("c_transposed"), sem("c_hi_split"), sem("c_lo_split"), sem("rotary_products")
        s_bw, s_bhi, s_blo = sem("b_weights_landed"), sem("b_weights_hi"), sem("b_weights_lo")
        s_bmm, s_bea, s_bed = sem("b_product_ready"), sem("b_evicted_by_act"), sem("b_evicted_by_dve")
        s_logc = sem("log_count_landed")
        s_st = {n: sem(f"head_{n}_staged") for n in "qkv"}
        s_sc, s_max, s_nm, s_pr = sem("scores_ready"), sem("row_max"), sem("minus_max_ready"), sem("probs_ready")
        s_pt, s_pthi, s_ptlo = sem("probs_transposed"), sem("pt_hi_split"), sem("pt_lo_split")
        s_pv, s_ot, s_rden = sem("pv_ready"), sem("ot_evicted"), sem("rden_ready")
        s_mi, s_mihi, s_mid = sem("misc_bank_filled"), sem("misc_hi_split"), sem("misc_bank_free")
        s_vhi, s_vlo = sem("v_hi_split"), sem("v_lo_split")
        s_x1, s_og = sem("residual_landed"), sem("output_gains_landed")
        s_ust = [sem(f"mlp_slot_landed{i}") for i in range(3)]
        s_cw = [sem(f"conv_taps_landed{b}") for b in range(4)]
        s_uhi, s_ulo = sem("mlp_w_hi_split"), sem("mlp_w_lo_split")
        s_up, s_ci, s_c0, s_cv = sem("up_ready"), sem("conv_middle"), sem("conv_left"), sem("conv_done")
        s_sg, s_h, s_hhi, s_hlo = sem("gate_silu"), sem("hidden_ready"), sem("hidden_hi"), sem("hidden_lo")
        s_dn, s_ya = sem("down_ready"), sem("down_added")
        s_gf, s_out = sem("final_gain_landed"), sem("output_written")

        block = ctx.enter_context(nc.Block())

        def await_(eng, semaphore, value):
            eng.wait_ge(semaphore, value)
            eng.sem_inc(s_passed, 1)

        def begin(eng, s, ph):
            eng.wait_ge(s_phase, s * (PHASES * ENGINES) + ph * ENGINES)

        def end(eng):
            eng.drain().then_inc(s_phase, 1)

        ROUND = {0: 0, 1: 1, 3: 2, 5: 3}
        OSUM = {2: 0, 4: 1, 6: 2, 7: 3}

        @block.sync
        def _(sp):
            def begin_sp(s, ph):
                begin(sp, s, ph)
                sp.sem_inc(s_passed, 1)

            sp.dma_start(idn[:], ident).then_inc(s_const, 16)
            sp.dma_start(stk[:], stack_ident).then_inc(s_const, 16)
            sp.dma_start(cosb[:], cos_b).then_inc(s_const, 16)
            sp.dma_start(sinb[:], sin_b).then_inc(s_const, 16)
            w_in_v = w_in.rearrange("(k p) n -> p k n", p=P)
            w_o_v = w_o.rearrange("(k p) n -> p k n", p=P)
            w_up_v = w_up.rearrange("(k p) n -> p k n", p=P)
            x_v = x_seqs.rearrange("(t p) n -> t p n", p=P)
            x_all = x_seqs.rearrange("(t p) n -> p t n", p=P)
            out_v = out.rearrange("(t p) n -> t p n", p=P)

            with sp.Fori(0, N_SEQ) as s:
                begin_sp(s, 0)
                for t in range(2):
                    sp.dma_start(xt[t][:], x_v[s * NT + t]).then_inc(s_x[t], 16)
                sp.dma_start(gin[:], g_attn.partition_broadcast(P)).then_inc(s_inw, 16)
                sp.dma_start(wst[:], w_in_v[:, :, 3 * WA:3 * WA + RQ]).then_inc(s_wst, 16)
                sp.dma_start(glora[:, 0:RQ], g_q.partition_broadcast(P)).then_inc(s_inw, 16)
                sp.dma_start(glora[:, RQ:RC], g_kv.partition_broadcast(P)).then_inc(s_inw, 16)
                sp.dma_start(cosa[:], cos_a).then_inc(s_inw, 16)
                sp.dma_start(sina[:], sin_a).then_inc(s_inw, 16)
                for t in range(2, NT):
                    await_(sp, s_tr, s * (3 * NT) + t - 1)
                    sp.dma_start(xt[t % 2][:], x_v[s * NT + t]).then_inc(s_x[t % 2], 16)
                    if t == 2:
                        await_(sp, s_wlo, s * U_ALL + 1)
                        sp.dma_start(wst[:, :, 0:KV_COLS], w_in_v[:, :, 3 * WA + RQ:3 * WA + RC + ROT]).then_inc(s_wst, 16)
                with sp.Fori(0, U_QK + U_V) as j:
                    await_(sp, s_wlo, s * U_ALL + j + U_C)
                    sp.dma_start(wst[:], w_in_v[:, :, bass.ds(j * COL, COL)]).then_inc(s_wst, 16)
                end(sp)

                def stage(h, src, dst, width, n):
                    if n == "v":
                        sp.dma_start(dst[n][:], src[:, :, bass.ds(h * width, width)]).then_inc(s_st[n], 16)
                        return
                    for i in range(2):
                        if width == HA:
                            to, t = dst[n][:, :, i * HA:(i + 1) * HA], slice(0, NT)
                        else:
                            t = slice(i * NT // 2, (i + 1) * NT // 2)
                            to = dst[n][:, t, :]
                        sp.dma_start(to, src[:, t, bass.ds(h * width, width)]).then_inc(s_st[n], 16)

                def attention(mixer, src_q, src_k, src_v, dst, width):
                    pr0 = s * HEADS + mixer * (HEADS // 2)
                    srcs = dict(q=(src_q, width), k=(src_k, width), v=(src_v, HA))
                    for n in "qkv":
                        stage(0, srcs[n][0], dst, srcs[n][1], n)
                    await_(sp, s_mi, pr0 * 16 + 2)
                    stage(1, srcs["q"][0], dst, srcs["q"][1], "q")
                    await_(sp, s_mi, pr0 * 16 + 4)
                    stage(1, srcs["k"][0], dst, srcs["k"][1], "k")
                    await_(sp, s_vlo, pr0 * 2 + 1)
                    stage(1, srcs["v"][0], dst, srcs["v"][1], "v")
                    with sp.Fori(0, HEADS // 2 - 1) as j:
                        for e in range(2):
                            h2 = j * 2 + e + 2
                            await_(sp, s_mi, (pr0 + j) * 16 + 4 + 8 * e + 2)
                            stage(h2, srcs["q"][0], dst, srcs["q"][1], "q")
                            await_(sp, s_vlo, (pr0 + j) * 2 + e + 2)
                            stage(h2, srcs["v"][0], dst, srcs["v"][1], "v")
                            await_(sp, s_mi, (pr0 + j) * 16 + 4 + 8 * e + 6)
                            stage(h2, srcs["k"][0], dst, srcs["k"][1], "k")

                begin_sp(s, 1)
                sp.dma_start(logc[:], log_count).then_inc(s_logc, 16)
                attention(0, qk, qk[:, :, WA:2 * WA], va, st_a, HA)
                end(sp)

                begin_sp(s, 2)
                sp.dma_start(uq_st[:], w_uq.rearrange("(k p) n -> p k n", p=P)).then_inc(s_bw, 16)
                sp.dma_start(ukv_st[:], w_ukv).then_inc(s_bw, 16)
                end(sp)

                begin_sp(s, 3)
                attention(1, qb, kb, vb, st_b, HB)
                end(sp)

                begin_sp(s, 4)
                sp.dma_start(gout[:], g_out.partition_broadcast(P)).then_inc(s_og, 16)
                sp.dma_start(gffn[:], g_ffn.partition_broadcast(P)).then_inc(s_og, 16)
                sp.dma_start(wost[:], w_o_v[:, :, 0:COL]).then_inc(s_wst, 16)
                sp.dma_start(x1[:], x_all[:, bass.ds(s * NT, NT), :]).then_inc(s_x1, 16)
                with sp.Fori(1, U_O) as j:
                    await_(sp, s_wlo, s * U_ALL + j + U_IN)
                    sp.dma_start(wost[:], w_o_v[:, :, bass.ds(j * COL, COL)]).then_inc(s_wst, 16)
                end(sp)

                begin_sp(s, 5)

                def slot_free(u):
                    await_(sp, s_ulo, s * (6 * NCH) + u - 2)

                def load_up(b, c, slot):
                    col = (b % 2) * F + (b // 2) * P
                    sp.dma_start(ust[slot][:].rearrange("p (k n) -> p k n", k=NK),
                                 w_up_v[:, :, bass.ds(c * (2 * P) + col, P)]).then_inc(s_ust[slot], 16)

                def load_taps(b, c):
                    sp.dma_start(cw[b][:], conv_wb[:, bass.ds(c * 16 + 4 * b, 4)]).then_inc(s_cw[b], 16)

                def load_down(f, c, slot):
                    sp.dma_start(ust[slot][:], w_down[bass.ds(c * (2 * P) + f * P, P), :]).then_inc(s_ust[slot], 16)

                for b in range(4):
                    if b == 3:
                        slot_free(b)
                    load_up(b, 0, b % 3)
                    load_taps(b, 0)
                sp.dma_start(gfin[:], g_final.partition_broadcast(P)).then_inc(s_gf, 16)
                with sp.Fori(0, NCH - 1) as c:
                    for k, what in enumerate(("u0", "d0", "d1", "u1", "u2", "u3")):
                        slot_free(c * 6 + 4 + k)
                        if what[0] == "u":
                            b = int(what[1])
                            load_up(b, c + 1, (4 + k) % 3)
                            await_(sp, s_cv, (s * NCH + c) * 4 + b + 1)
                            load_taps(b, c + 1)
                        else:
                            load_down(int(what[1]), c, (4 + k) % 3)
                for f in range(2):
                    slot_free(6 * NCH - 2 + f)
                    load_down(f, NCH - 1, (6 * NCH - 2 + f) % 3)
                for t in range(NT):
                    await_(sp, s_xn, s * (4 * NT) + 3 * NT + t + 1)
                    sp.dma_start(out_v[s * NT + t], x1[:, t, :]).then_inc(s_out, 16)
                await_(sp, s_out, s * (16 * NT) + 16 * NT)
                end(sp)

        @block.tensor
        def _(pe):
            def product(dst, passes):
                n = len(passes)
                for i, (lhs, rhs) in enumerate(passes):
                    mm = pe.matmul(dst, lhs, rhs, start=(i == 0), stop=(i == n - 1))
                return mm

            def transpose_tile(src, dst):
                for k in range(NK):
                    tr = pe.transpose(dst[:, k * P:(k + 1) * P], src[:, k * P:(k + 1) * P], idn[:])
                tr.then_inc(s_tr, 1)

            def unit(t, whi, wlo, n, dst):
                tok = slice(t * P, (t + 1) * P)
                passes = []
                for k in range(NK):
                    passes += [(at_hi[:, k, tok], whi[:, k, 0:n]), (at_hi[:, k, tok], wlo[:, k, 0:n]),
                               (at_lo[:, k, tok], whi[:, k, 0:n])]
                product(dst[:, 0:n], passes).then_inc(s_mm, 1)

            pe.wait_ge(s_const, 16 * 4)
            with pe.Fori(0, N_SEQ) as s:
                begin(pe, s, 0)
                pe.wait_ge(s_xn, s * (4 * NT) + 1)
                transpose_tile(xt[0], pair[2])
                for t in range(NT):
                    pe.wait_ge(s_alo, s * (3 * NT) + t + 1)
                    if t + 1 < NT:
                        pe.wait_ge(s_xn, s * (4 * NT) + t + 2)
                        transpose_tile(xt[(t + 1) % 2], pair[2])
                    for u in range(U_C):
                        if t == 0:
                            pe.wait_ge(s_wlo, s * U_ALL + u + 1)
                        if t >= 2:
                            pe.wait_ge(s_eva, s * (U_C * NT) + (t - 2) * U_C + u + 1)
                        unit(t, w_hi[u], w_lo[u], COL if u == 0 else KV_COLS, bank((t * U_C + u) % 4))
                    for tc in ([t - 1] if t >= 1 else []) + ([t] if t == NT - 1 else []):
                        pe.wait_ge(s_cn, s * NT + tc + 1)
                        if tc >= 1:
                            pe.wait_ge(s_clo, s * NT + tc)
                        for k in range(3):
                            tr = pe.transpose(bank(6)[:, k * P:(k + 1) * P], cr[tc % 2][:, k * P:(k + 1) * P], idn[:])
                        tr.then_inc(s_ctr, 1)
                with pe.Fori(0, (U_QK + U_V) // 2) as j:
                    for e in range(2):
                        pe.wait_ge(s_wlo, s * U_ALL + j * 2 + U_C + e + 1)
                        for t in range(NT):
                            if e == 0 and t == 0:
                                pe.wait_ge(s_eva, s * (U_C * NT) + U_C * NT)
                            pe.wait_ge(s_evd, s * EV_SEQ + j * (2 * NT) + e * NT + t - 3 + EV_CREDIT)
                            unit(t, w_hi[e], w_lo[e], COL, bank(t % 4))
                end(pe)

                def attention(mixer, prep_q, prep_k, score_passes, v2, ot, prob, st):
                    pr0 = s * HEADS + mixer * (HEADS // 2)

                    def scores(e, t):
                        q = slice(t * P, (t + 1) * P)
                        for half in range(2):
                            k = slice(half * 512, half * 512 + 512)
                            mm = product(pair[t % 2][:, k], score_passes(e, q, k))
                        mm.then_inc(s_sc, 1)

                    def round_(r, pr, m, heads_staged):
                        pe.wait_ge(s_mid, pr * 16 + m)
                        if r % 2 == 0:
                            pe.wait_ge(s_st["q" if r < 2 else "k"], heads_staged * 32)
                        (prep_q if r < 2 else prep_k)(r % 2)

                    def pv(e, g, pr):
                        i = 8 * e + 2 * g + 1
                        pe.wait_ge(s_ptlo, pr * 32 + 2 * i + 2 + LO_CREDIT)
                        if g == 0:
                            pe.wait_ge(s_vlo, pr * 2 + e + 1)
                        pe.wait_ge(s_ot, pr * 8 + 4 * e + g)
                        passes = []
                        for k in range(NT):
                            passes += [(v2[e][:, k, :], pt_hi[g % 2][:, k, :]), (v2[e][:, k, :], pt_lo[g % 2][:, k, :])]
                        product(bank(6)[:, 0:2 * P], passes).then_inc(s_pv, 1)

                    def osum(e, g, pr, m):
                        pe.wait_ge(s_ot, pr * 8 + 4 * e + g + 1)
                        pe.wait_ge(s_mid, pr * 16 + m)
                        for i in range(2):
                            mm = pe.matmul(bank(7)[:, i * HA:(i + 1) * HA], ot[:, i * P:(i + 1) * P], stk[:],
                                           start=True, stop=True)
                        mm.then_inc(s_mi, 1)

                    def head(e, pr, last):
                        m0 = 4 + 8 * e
                        for t in range(NT):
                            i = 8 * e + t
                            pe.wait_ge(s_pr, pr * 16 + i + 1)
                            for hb in range(2):
                                pe.wait_ge(s_ptlo, pr * 32 + 2 * i + hb - 1 + LO_CREDIT)
                                for k in range(4):
                                    c = (4 * hb + k) * P
                                    tr = pe.transpose(bank(4 + hb)[:, k * P:(k + 1) * P], prob[t % 2][:, c:c + P], idn[:])
                                tr.then_inc(s_pt, 1)
                            if t + 2 < NT:
                                scores(e, t + 2)
                            elif not last:
                                if t + 2 == NT:
                                    pe.wait_ge(s_mid, pr * 16 + m0 + 6)
                                scores(1 - e, t + 2 - NT)
                            if t in ROUND and not last:
                                round_(ROUND[t], pr, m0 + t, pr * 2 + e + 2)
                            if t % 2 == 1:
                                pv(e, t // 2, pr)
                            if t in OSUM:
                                m = m0 + (OSUM[t] if last else t)
                                osum(e, OSUM[t], pr, m)

                    def heads(pr, last):
                        head(0, pr, False)
                        head(1, pr, last)

                    for r in range(4):
                        round_(r, pr0, r, pr0 * 2 + 1)
                    pe.wait_ge(s_mid, pr0 * 16 + 4)
                    scores(0, 0)
                    scores(0, 1)
                    with pe.Fori(0, HEADS // 2 - 1) as j:
                        heads(pr0 + j, False)
                    heads(pr0 + (HEADS // 2 - 1), True)

                def prep(dst_rows, src):
                    def go(half):
                        for i in range(4):
                            tr = pe.transpose(bank(7)[0:dst_rows, i * P:(i + 1) * P], src[:, 4 * half + i, :], idn[:])
                        tr.then_inc(s_mi, 1)
                    return go

                begin(pe, s, 1)
                attention(0, prep(P, st_a["q"]), prep(P, st_a["k"]),
                          lambda e, q, k: [(q2[e][:, q], khh[e][:, k]), (q2[e][:, q], kll[e][:, k])],
                          v2_a, ot_a, pr_a, st_a)
                end(pe)

                begin(pe, s, 2)
                pe.wait_ge(s_blo, s * 2 + 2)
                for t in range(NT):
                    tok = slice(t * P, (t + 1) * P)
                    if t >= 2:
                        pe.wait_ge(s_bed, s * (2 * NT) + 2 * (t - 2) + 2)
                    for a, b in ((0, 512), (512, NUQ)):
                        passes = []
                        for k in range(2):
                            passes += [(ct_hi[:, k, tok], uq_hi[:, k, a:b]), (ct_hi[:, k, tok], uq_lo[:, k, a:b]),
                                       (ct_lo[:, k, tok], uq_hi[:, k, a:b])]
                        mm = product(pair[t % 2][:, a:b], passes)
                    mm.then_inc(s_bmm, 1)
                    for a, b in ((0, 512), (512, 1024)):
                        mm = product(pair[2 + t % 2][:, a:b], [
                            (ct_hi[:, 2, tok], ukv_hi[:, a:b]), (ct_hi[:, 2, tok], ukv_lo[:, a:b]),
                            (ct_lo[:, 2, tok], ukv_hi[:, a:b])])
                    mm.then_inc(s_bmm, 1)
                end(pe)

                begin(pe, s, 3)
                attention(1, prep(HB, st_b["q"]), prep(HB, st_b["k"]),
                          lambda e, q, k: [(qh[e][0:HB, q], kh[e][0:HB, k]), (qh[e][0:HB, q], kl[e][0:HB, k]),
                                           (ql[e][0:HB, q], kh[e][0:HB, k])],
                          v2_b, ot_b, pr_b, st_b)
                end(pe)

                begin(pe, s, 4)

                def mlp_input(t):
                    pe.wait_ge(s_xn, s * (4 * NT) + 2 * NT + t + 1)
                    if t >= 2:
                        pe.wait_ge(s_alo, s * (3 * NT) + 2 * NT + t - 1)
                    transpose_tile(xn[t % 2], pair[2 + t % 2])

                for t in range(NT):
                    pe.wait_ge(s_xn, s * (4 * NT) + NT + t + 1)
                    if t >= 2:
                        pe.wait_ge(s_alo, s * (3 * NT) + NT + t - 1)
                    transpose_tile(xn[t % 2], pair[2 + t % 2])
                for u in range(U_O):
                    pe.wait_ge(s_wlo, s * U_ALL + U_IN + u + 1)
                    for t in range(NT):
                        if u == 0:
                            pe.wait_ge(s_alo, s * (3 * NT) + NT + t + 1)
                        pe.wait_ge(s_evd, s * EV_SEQ + (U_QK + U_V + u) * NT + t - 3 + EV_CREDIT)
                        unit(t, wo_hi[u % 2], wo_lo[u % 2], COL, bank(t % 4))
                        if u == U_O - 1 and t >= 2:
                            mlp_input(t - 2)
                mlp_input(NT - 2)
                mlp_input(NT - 1)
                end(pe)

                begin(pe, s, 5)

                def up(b, c, first):
                    K = (s * NCH + c) * 4 + b
                    if first:
                        pe.wait_ge(s_ulo, s * (6 * NCH) + b + 1)
                        if b >= 2:
                            pe.wait_ge(s_cv, K - 1)
                    else:
                        pe.wait_ge(s_ulo, s * (6 * NCH) + (c - 1) * 6 + 5 + (0, 3, 4, 5)[b])
                        pe.wait_ge(s_cv, K - 1)
                    for half in range(2):
                        tok = slice(half * 512, half * 512 + 512)
                        passes = []
                        for k in range(NK):
                            passes += [(wu_hi[b][:, k, :], at_hi[:, k, tok]), (wu_hi[b][:, k, :], at_lo[:, k, tok]),
                                       (wu_lo[b][:, k, :], at_hi[:, k, tok])]
                        mm = product(pair[b % 2][:, tok], passes)
                    mm.then_inc(s_up, 1)

                def down(c, tail):
                    n = 6 * NCH if tail else (c * 6 + 7)
                    pe.wait_ge(s_ulo, s * (6 * NCH) + n)
                    pe.wait_ge(s_hlo, (s * NCH + c) * 2 + 2)
                    for t in range(NT):
                        tok = slice(t * P, (t + 1) * P)
                        pe.wait_ge(s_ya, (s * NCH + c) * NT + t - 1 + YA_CREDIT)
                        for half in range(2):
                            col = slice(half * 512, half * 512 + 512)
                            passes = []
                            for f in range(2):
                                passes += [(h_hi[f][:, tok], wd_hi[f][:, col]), (h_hi[f][:, tok], wd_lo[f][:, col]),
                                           (h_lo[f][:, tok], wd_hi[f][:, col])]
                            mm = product(pair[2 + t % 2][:, col], passes)
                        mm.then_inc(s_dn, 1)

                for b in range(4):
                    up(b, 0, True)
                with pe.Fori(1, NCH) as c:
                    up(0, c, False)
                    down(c - 1, False)
                    for b in range(1, 4):
                        up(b, c, False)
                down(NCH - 1, True)
                end(pe)


        @block.scalar
        def _(act):
            def squares(src, n_cols, junk_buf, col, done, j0=0):
                act.activation(junk_buf[:, j0:j0 + n_cols], src, ACT.Square, accum_out=ss[:, col:col + 1]).then_inc(done, 1)

            def rms(col, n, n_cols, done, inc=True):
                op = act.activation(sd[:, col:col + n], ss[:, col:col + n], ACT.Sqrt, bias=eps[:, 0:1], scale=1.0 / n_cols)
                if inc:
                    op.then_inc(done, 1)

            def act_hi(t, src, idx):
                act.wait_ge(s_tr, idx + 1)
                act.copy(at_hi[:, :, t * P:(t + 1) * P], src[:].rearrange("p (k n) -> p k n", k=NK)).then_inc(s_ahi, 1)

            act.wait_ge(s_eps, 1)
            act.wait_ge(s_const, 16 * 4)
            with act.Fori(0, N_SEQ) as s:
                begin(act, s, 0)
                xb = s * (4 * NT)
                tb = s * (3 * NT)

                def stats(t):
                    act.wait_ge(s_x[t % 2], s * (16 * NT // 2) + 16 * (t // 2 + 1))
                    squares(xt[t % 2][:], D, junk, 2 * t, s_ss)
                    act.wait_ge(s_ss, xb + t + 1)
                    rms(2 * t, 1, D, s_std)

                def w_split(u, src, dst):
                    act.wait_ge(s_wst, (s * U_ALL + u + 1) * 16)
                    act.copy(dst, src).then_inc(s_whi, 1)

                stats(0)
                w_split(0, wst[:], w_hi[0][:])
                act_hi(0, pair[2], tb)
                stats(1)
                w_split(1, wst[:, :, 0:KV_COLS], w_hi[1][:, :, 0:KV_COLS])
                for t in range(NT):
                    if t + 1 < NT:
                        act_hi(t + 1, pair[2], tb + t + 1)
                    if t + 2 < NT:
                        stats(t + 2)
                    c = cr[t % 2]
                    if t >= 2:
                        act.wait_ge(s_ctr, s * NT + t - 1)
                    act.wait_ge(s_mm, s * (U_ALL * NT) + 2 * t + 1)
                    act.copy(c[:, 0:RQ], bank(2 * t % 4)[:, 0:RQ]).then_inc(s_eva, 1)
                    act.wait_ge(s_mm, s * (U_ALL * NT) + 2 * t + 2)
                    act.copy(c[:, RQ:RC + ROT], bank((2 * t + 1) % 4)[:, 0:KV_COLS]).then_inc(s_eva, 1)
                    act.wait_ge(s_eva, s * (U_C * NT) + 2 * t + 2)
                    squares(c[:, 0:RQ], RQ, junk, 16 + 2 * t, s_css)
                    squares(c[:, RQ:RC], RKV, junk, 17 + 2 * t, s_css, RQ)
                    act.wait_ge(s_css, s * (2 * NT) + 2 * t + 2)
                    rms(16 + 2 * t, 1, RQ, s_cstd)
                    rms(17 + 2 * t, 1, RKV, s_cstd)
                    for tc in ([t - 1] if t >= 1 else []) + ([t] if t == NT - 1 else []):
                        act.wait_ge(s_ctr, s * NT + tc + 1)
                        act.copy(ct_hi[:, :, tc * P:(tc + 1) * P],
                                 bank(6)[:, 0:3 * P].rearrange("p (k n) -> p k n", k=3)).then_inc(s_chi, 1)
                act.wait_ge(s_mm, s * (U_ALL * NT) + 2 * NT)
                for e in range(2):
                    w_split(2 + e, wst[:], w_hi[e][:])
                with act.Fori(0, U_QK // 2) as j:
                    for e in range(2):
                        act.wait_ge(s_mm, s * (U_ALL * NT) + j * (2 * NT) + (U_C + e + 1) * NT)
                        w_split(j * 2 + 4 + e, wst[:], w_hi[e][:])
                end(act)

                def attention(mixer, hi_q, hi_k, v2, ot, prob, st, scale):
                    pr0 = s * HEADS + mixer * (HEADS // 2)

                    def prob_tile(e, t, pr):
                        i = 8 * e + t
                        act.wait_ge(s_nm, pr * 16 + i + 1)
                        act.activation(prob[t % 2][:], pair[t % 2][:], ACT.Exp, bias=nm[:, t % 4:t % 4 + 1],
                                       scale=scale, accum_out=den[:, e % 2, t:t + 1]).then_inc(s_pr, 1)

                    def round_(r, pr, m, e):
                        act.wait_ge(s_mi, pr * 16 + m + 1)
                        (hi_q if r < 2 else hi_k)(e, r % 2)

                    def v_split(e, heads_staged):
                        act.wait_ge(s_st["v"], heads_staged * 16)
                        act.copy(v2[e][:, :, 0:HA], st["v"][:]).then_inc(s_vhi, 1)

                    def head(e, pr, last):
                        m0 = 4 + 8 * e
                        for t in range(NT):
                            i = 8 * e + t
                            for hb in range(2):
                                act.wait_ge(s_pt, pr * 32 + 2 * i + hb + 1)
                                act.copy(pt_hi[t // 2 % 2][:, 4 * hb:4 * hb + 4, t % 2 * P:(t % 2 + 1) * P],
                                         bank(4 + hb).rearrange("p (k n) -> p k n", k=4)).then_inc(s_pthi, 1)
                            if t + 1 < NT:
                                prob_tile(e, t + 1, pr)
                            elif not last:
                                prob_tile(1, 0, pr) if e == 0 else prob_tile_next(pr)
                            if t in ROUND and not last:
                                round_(ROUND[t], pr, m0 + t, 1 - e)
                                if t == 0:
                                    v_split(1 - e, pr * 2 + e + 2)
                            if t % 2 == 1:
                                act.wait_ge(s_pv, pr * 8 + 4 * e + t // 2 + 1)
                                act.copy(ot[:], bank(6)[:, 0:2 * P]).then_inc(s_ot, 1)

                    def prob_tile_next(pr):
                        act.wait_ge(s_nm, pr * 16 + 17)
                        act.activation(prob[0][:], pair[0][:], ACT.Exp, bias=nm[:, 0:1],
                                       scale=scale, accum_out=den[:, 0, 0:1]).then_inc(s_pr, 1)

                    for r in range(4):
                        round_(r, pr0, r, 0)
                    v_split(0, pr0 * 2 + 1)
                    prob_tile(0, 0, pr0)
                    with act.Fori(0, HEADS // 2 - 1) as j:
                        head(0, pr0 + j, False)
                        head(1, pr0 + j, False)
                    head(0, pr0 + (HEADS // 2 - 1), False)
                    head(1, pr0 + (HEADS // 2 - 1), True)

                def hi_of(dst, rows):
                    def go(e, half):
                        act.copy(dst[e][0:rows, half * 512:half * 512 + 512], bank(7)[0:rows, :]).then_inc(s_mihi, 1)
                    return go

                begin(act, s, 1)
                attention(0, hi_of(q2, P), hi_of(khh, P), v2_a, ot_a, pr_a, st_a, SCALE_A)
                end(act)

                begin(act, s, 2)
                act.wait_ge(s_bw, (s * 2 + 2) * 16)
                act.copy(uq_hi[:], uq_st[:]).then_inc(s_bhi, 1)
                act.copy(ukv_hi[:], ukv_st[:]).then_inc(s_bhi, 1)
                for t in range(NT):
                    act.wait_ge(s_bmm, s * (2 * NT) + 2 * t + 1)
                    act.copy(qb[:, t, :].rearrange("p (h x) -> p h x", x=HB)[:, :, 0:HA],
                             pair[t % 2][:, 0:NUQ].rearrange("p (h x) -> p h x", x=HB)[:, :, 0:HA]).then_inc(s_bea, 1)
                    act.wait_ge(s_bmm, s * (2 * NT) + 2 * t + 2)
                    act.copy(kb[:, t, :].rearrange("p (h x) -> p h x", x=HB)[:, :, 0:HA],
                             pair[2 + t % 2][:].rearrange("p (h x) -> p h x", x=2 * HA)[:, :, 0:HA]).then_inc(s_bea, 1)
                end(act)

                begin(act, s, 3)
                attention(1, hi_of(qh, HB), hi_of(kh, HB), v2_b, ot_b, pr_b, st_b, SCALE_B)
                end(act)

                begin(act, s, 4)

                def o_stats(t):
                    act.activation(junk2[:, 0:WA], o[:, t, 0:WA], ACT.Square, accum_out=ss[:, 2 * t:2 * t + 1])
                    act.activation(junk2[:, WA:D], o[:, t, WA:D], ACT.Square, accum_out=ss[:, 2 * t + 1:2 * t + 2]).then_inc(s_ss, 1)
                    act.wait_ge(s_ss, xb + NT + t + 1)
                    rms(2 * t, 2, WA, s_std)

                o_stats(0)
                o_stats(1)
                w_split(U_IN, wost[:], wo_hi[0][:])
                for t in range(NT):
                    if t + 2 < NT:
                        o_stats(t + 2)
                    act_hi(t, pair[2 + t % 2], tb + NT + t)
                w_split(U_IN + 1, wost[:], wo_hi[1][:])
                for u in range(2, U_O):
                    act.wait_ge(s_mm, s * (U_ALL * NT) + (U_IN + u - 1) * NT)
                    w_split(U_IN + u, wost[:], wo_hi[u % 2][:])

                def x1_stats(t, base):
                    squares(x1[:, t, :], D, junk2 if base == 2 * NT else junk3, 2 * t, s_ss)
                    act.wait_ge(s_ss, xb + base + t + 1)
                    rms(2 * t, 1, D, s_std)

                for t in range(NT):
                    act.wait_ge(s_evd, s * EV_SEQ + (U_ALL - U_C - 1) * NT + t + 1 + EV_CREDIT)
                    x1_stats(t, 2 * NT)
                    if t >= 1:
                        act_hi(t - 1, pair[2 + (t - 1) % 2], tb + 2 * NT + t - 1)
                act_hi(NT - 1, pair[2 + (NT - 1) % 2], tb + 3 * NT - 1)
                end(act)

                begin(act, s, 5)

                def split(u3, slot, dst):
                    act.wait_ge(s_ust[slot], (s * (2 * NCH) + u3) * 16)
                    act.copy(dst, ust[slot][:]).then_inc(s_uhi, 1)

                def split_up(b, c_next, u3, slot):
                    split(u3, slot, wu_hi[b][:].rearrange("p k n -> p (k n)"))

                def conv(b, c):
                    K = (s * NCH + c) * 4 + b
                    act.wait_ge(s_up, K + 1)
                    act.wait_ge(s_cw[b], (s * NCH + c + 1) * 16)
                    dst = cg if b % 2 == 0 else cv
                    if b == 3:
                        act.wait_ge(s_hlo, (s * NCH + c) * 2 + 1)
                    if b == 1:
                        act.wait_ge(s_hlo, (s * NCH + c) * 2)
                    act.activation(dst[:], pair[b % 2][:], ACT.Identity, bias=cw[b][:, 3:4], scale=cw[b][:, 1:2]).then_inc(s_ci, 1)

                def silu(f, c):
                    act.wait_ge(s_cv, (s * NCH + c) * 4 + 2 * f + 1)
                    act.activation(cg[:], cg[:], ACT.Silu).then_inc(s_sg, 1)

                def hidden_hi(f, c):
                    act.wait_ge(s_h, (s * NCH + c) * 2 + f + 1)
                    act.copy(h_hi[f][:], cv[:]).then_inc(s_hhi, 1)

                def chunk(c, first, last):
                    def next_up(b, k):
                        if not last:
                            split_up(b, c + 1, c * 2 + (4 + k) // 3 + 1, (4 + k) % 3)
                    conv(0, c)
                    next_up(0, 0)
                    silu(0, c)
                    if not first:
                        act.wait_ge(s_dn, (s * NCH + c) * NT)
                    for f in range(2):
                        k = f if last else f + 1
                        split(c * 2 + (4 + k) // 3 + 1, (4 + k) % 3, wd_hi[f][:])
                    conv(1, c)
                    hidden_hi(0, c)
                    next_up(1, 3)
                    conv(2, c)
                    next_up(2, 4)
                    silu(1, c)
                    conv(3, c)
                    hidden_hi(1, c)
                    next_up(3, 5)

                for b in range(4):
                    split_up(b, 0, b // 3 + 1, b % 3)
                chunk(0, True, False)
                with act.Fori(1, NCH - 1) as c:
                    chunk(c, False, False)
                chunk(NCH - 1, False, True)
                for t in range(NT):
                    act.wait_ge(s_ya, (s * NCH + NCH - 1) * NT + t + 1 + YA_CREDIT)
                    x1_stats(t, 3 * NT)
                end(act)

        @block.vector
        def _(dve):
            def normalise(dst, src, gain, col, idx, halves=1):
                dve.wait_ge(s_std, idx + 1)
                dve.reciprocal(rs[:, col:col + halves], sd[:, col:col + halves]).then_inc(s_rs, 1)
                dve.wait_ge(s_rs, idx + 1)
                w = D // halves
                for i in range(halves):
                    c = slice(i * w, (i + 1) * w)
                    op = dve.scalar_tensor_tensor(dst[:, c], src[:, c], rs[:, col + i:col + i + 1], gain[:, c], ALU.mult, ALU.mult)
                op.then_inc(s_xn, 1)

            def act_lo(t, src, idx):
                dve.wait_ge(s_ahi, idx + 1)
                tok = slice(t * P, (t + 1) * P)
                dve.tensor_tensor(at_lo[:, :, tok], src[:].rearrange("p (k n) -> p k n", k=NK),
                                  at_hi[:, :, tok].bitcast(F32), ALU.subtract).then_inc(s_alo, 1)

            def rotate(dst, src, cos, sin, heads, width, ta, tb_, idx, done):
                h = width // 2
                bc = lambda a, n: a.unsqueeze(1).to_broadcast([P, heads, n])
                dve.tensor_tensor(ta, src, bc(cos, width), ALU.mult)
                dve.tensor_tensor(tb_[:, :, 0:h], src[:, :, h:width], bc(sin[:, 0:h], h), ALU.mult)
                dve.tensor_tensor(tb_[:, :, h:width], src[:, :, 0:h], bc(sin[:, h:width], h), ALU.mult).then_inc(s_rot, 1)
                dve.wait_ge(s_rot, idx + 1)
                dve.tensor_tensor(dst, ta, tb_, ALU.add).then_inc(done, 1)

            dve.memset(eps[:], EPS).then_inc(s_eps, 1)
            for s_free, n in ((s_ptlo, LO_CREDIT), (s_evd, EV_CREDIT), (s_ya, YA_CREDIT)):
                for _ in range(n):
                    dve.sem_inc(s_free, 1)
            dve.wait_ge(s_const, 16 * 4)
            with dve.Fori(0, N_SEQ) as s:
                begin(dve, s, 0)
                xb = s * (4 * NT)
                tb = s * (3 * NT)

                def w_split(u, src, hi, lo):
                    dve.wait_ge(s_whi, s * U_ALL + u + 1)
                    dve.tensor_tensor(lo, src, hi.bitcast(F32), ALU.subtract).then_inc(s_wlo, 1)

                def xnorm(t):
                    normalise(xt[t % 2][:], xt[t % 2][:], gin[:], 2 * t, xb + t)

                dve.wait_ge(s_inw, (s + 1) * 80)
                xnorm(0)
                w_split(0, wst[:], w_hi[0][:], w_lo[0][:])
                xnorm(1)
                act_lo(0, pair[2], tb)
                w_split(1, wst[:, :, 0:KV_COLS], w_hi[1][:, :, 0:KV_COLS], w_lo[1][:, :, 0:KV_COLS])
                for t in range(NT):
                    if t + 1 < NT:
                        act_lo(t + 1, pair[2], tb + t + 1)
                    if t + 2 < NT:
                        xnorm(t + 2)
                    c = cr[t % 2]
                    q0 = 16 + 2 * t
                    dve.wait_ge(s_cstd, s * (2 * NT) + 2 * t + 2)
                    dve.reciprocal(rs[:, q0:q0 + 2], sd[:, q0:q0 + 2]).then_inc(s_crs, 1)
                    dve.wait_ge(s_crs, s * NT + t + 1)
                    dve.scalar_tensor_tensor(c[:, 0:RQ], c[:, 0:RQ], rs[:, q0:q0 + 1], glora[:, 0:RQ], ALU.mult, ALU.mult)
                    dve.scalar_tensor_tensor(c[:, RQ:RC], c[:, RQ:RC], rs[:, q0 + 1:q0 + 2], glora[:, RQ:RC], ALU.mult, ALU.mult)
                    rotate(krot[:, t, :].unsqueeze(1), c[:, RC:RC + ROT].unsqueeze(1), cosb[:, t, :], sinb[:, t, :], 1, ROT,
                           pra[t % 2][:, 0:ROT].unsqueeze(1), prb[t % 2][:, 0:ROT].unsqueeze(1), s * ROT_SEQ + t, s_cn)
                    for tc in ([t - 1] if t >= 1 else []) + ([t] if t == NT - 1 else []):
                        dve.wait_ge(s_chi, s * NT + tc + 1)
                        tok = slice(tc * P, (tc + 1) * P)
                        dve.tensor_tensor(ct_lo[:, :, tok], bank(6)[:, 0:3 * P].rearrange("p (k n) -> p k n", k=3),
                                          ct_hi[:, :, tok].bitcast(F32), ALU.subtract).then_inc(s_clo, 1)
                for e in range(2):
                    w_split(2 + e, wst[:], w_hi[e][:], w_lo[e][:])
                heads4 = lambda a: a.rearrange("p (h x) -> p h x", x=HA)
                with dve.Fori(0, U_QK // 2) as j:
                    for e in range(2):
                        for t in range(NT):
                            dve.wait_ge(s_mm, s * (U_ALL * NT) + j * (2 * NT) + (U_C + e) * NT + t + 1)
                            rotate(heads4(qk[:, t, bass.ds(j * (2 * COL) + e * COL, COL)]), heads4(bank(t % 4)[:, 0:COL]),
                                   cosa[:, t, :], sina[:, t, :], COL // HA, HA, heads4(pra[t % 2][:]), heads4(prb[t % 2][:]),
                                   s * ROT_SEQ + j * (2 * NT) + (e + 1) * NT + t, s_evd)
                        w_split(j * 2 + 4 + e, wst[:], w_hi[e][:], w_lo[e][:])
                for u in range(U_V):
                    for t in range(NT):
                        dve.wait_ge(s_mm, s * (U_ALL * NT) + (U_C + U_QK + u) * NT + t + 1)
                        dve.tensor_copy(va[:, t, u * COL:(u + 1) * COL], bank(t % 4)[:, 0:COL]).then_inc(s_evd, 1)
                end(dve)

                def attention(mixer, lo_q, lo_k, v2, st, scale):
                    pr0 = s * HEADS + mixer * (HEADS // 2)

                    def row_max(t, idx):
                        m, n = mx[:, t % 4:t % 4 + 1], nm[:, t % 4:t % 4 + 1]
                        sc = pair[t % 2][:]
                        if mixer == 0:
                            await_(dve, s_sc, idx + 1)
                            u0 = (NT - 1 - t) * P
                            dve.tensor_tensor_reduce(sc, sc, logc[:, u0:u0 + S], 1.0, -3e38, ALU.add, ALU.max, m).then_inc(s_max, 1)
                        else:
                            dve.wait_ge(s_sc, idx + 1)
                            dve.tensor_reduce(m, sc, AXX, ALU.max).then_inc(s_max, 1)
                        dve.wait_ge(s_max, idx + 1)
                        dve.tensor_scalar(n, m, -scale, None, ALU.mult).then_inc(s_nm, 1)

                    def round_(r, m, e, idx):
                        dve.wait_ge(s_mihi, idx + 1)
                        (lo_q if r < 2 else lo_k)(e, r % 2)

                    def v_split(e, idx):
                        dve.wait_ge(s_vhi, idx + 1)
                        dve.tensor_tensor(v2[e][:, :, HA:P], st["v"][:], v2[e][:, :, 0:HA].bitcast(F32), ALU.subtract).then_inc(s_vlo, 1)

                    def head(e, pr, h, last):
                        m0 = 4 + 8 * e
                        for t in range(NT):
                            i = 8 * e + t
                            for hb in range(2):
                                dve.wait_ge(s_pthi, pr * 32 + 2 * i + hb + 1)
                                dst = (slice(None), slice(4 * hb, 4 * hb + 4), slice(t % 2 * P, (t % 2 + 1) * P))
                                dve.tensor_tensor(pt_lo[t // 2 % 2][dst], bank(4 + hb).rearrange("p (k n) -> p k n", k=4),
                                                  pt_hi[t // 2 % 2][dst].bitcast(F32), ALU.subtract).then_inc(s_ptlo, 1)
                            if t in ROUND and not last:
                                round_(ROUND[t], m0 + t, 1 - e, pr * 8 + 4 + 4 * e + ROUND[t])
                                if t == 0:
                                    v_split(1 - e, pr * 2 + e + 1)
                            if t in OSUM:
                                g = OSUM[t]
                                m = m0 + (g if last else t)
                                gi = pr * 8 + 4 * e + g
                                r2 = slice(g % 2 * 2, g % 2 * 2 + 2)
                                dve.wait_ge(s_mi, pr * 16 + m + 1)
                                dve.reciprocal(rden[:, r2], den[:, e, 2 * g:2 * g + 2]).then_inc(s_rden, 1)
                                dve.wait_ge(s_rden, gi + 1)
                                dve.tensor_tensor(o[:, 2 * g:2 * g + 2, bass.ds(h, HA)],
                                                  bank(7)[:, 0:2 * HA].rearrange("p (i x) -> p i x", i=2),
                                                  rden[:, r2].unsqueeze(2).to_broadcast([P, 2, HA]), ALU.mult).then_inc(s_mid, 1)
                            if t + 2 < NT or not last:
                                row_max((t + 2) % NT, pr * 16 + i + 2)

                    for r in range(4):
                        round_(r, r, 0, pr0 * 8 + r)
                    v_split(0, pr0 * 2)
                    row_max(0, pr0 * 16)
                    row_max(1, pr0 * 16 + 1)
                    with dve.Fori(0, HEADS // 2 - 1) as j:
                        for e in range(2):
                            head(e, pr0 + j, j * (2 * HA) + (mixer * WA + e * HA), False)
                    for e in range(2):
                        head(e, pr0 + (HEADS // 2 - 1), mixer * WA + (HEADS - 2 + e) * HA, e == 1)

                def lo_of(dst, hi, r0, r1):
                    def go(e, half):
                        c = slice(half * 512, half * 512 + 512)
                        dve.tensor_tensor(dst[e][r0:r1, c], bank(7)[r0:r1, :], hi[e][r0:r1, c].bitcast(F32),
                                          ALU.subtract).then_inc(s_mid, 1)
                    return go

                begin(dve, s, 1)
                dve.wait_ge(s_logc, (s + 1) * 16)
                attention(0, lo_of(q2, q2, HA, P), lo_of(kll, khh, 0, P), v2_a, st_a, SCALE_A)
                end(dve)

                begin(dve, s, 2)
                dve.wait_ge(s_bhi, s * 2 + 1)
                dve.tensor_tensor(uq_lo[:], uq_st[:], uq_hi[:].bitcast(F32), ALU.subtract).then_inc(s_blo, 1)
                dve.wait_ge(s_bhi, s * 2 + 2)
                dve.tensor_tensor(ukv_lo[:], ukv_st[:], ukv_hi[:].bitcast(F32), ALU.subtract).then_inc(s_blo, 1)
                for t in range(NT):
                    by_head = lambda a, x: a.rearrange("p (h x) -> p h x", x=x)
                    dve.wait_ge(s_bea, s * (2 * NT) + 2 * t + 1)
                    rotate(by_head(qb[:, t, :], HB)[:, :, HA:HB], by_head(pair[t % 2][:, 0:NUQ], HB)[:, :, HA:HB],
                           cosb[:, t, :], sinb[:, t, :], HEADS, ROT, pba[t % 2][:], pbb[t % 2][:],
                           s * ROT_SEQ + (1 + U_QK) * NT + t, s_bed)
                    dve.tensor_copy(by_head(kb[:, t, :], HB)[:, :, HA:HB], krot[:, t, :].unsqueeze(1).to_broadcast([P, HEADS, ROT]))
                    dve.wait_ge(s_bea, s * (2 * NT) + 2 * t + 2)
                    dve.tensor_copy(by_head(vb[:, t, :], HA), by_head(pair[2 + t % 2][:], 2 * HA)[:, :, HA:2 * HA]).then_inc(s_bed, 1)
                end(dve)

                begin(dve, s, 3)
                attention(1, lo_of(ql, qh, 0, HB), lo_of(kl, kh, 0, HB), v2_b, st_b, SCALE_B)
                end(dve)

                begin(dve, s, 4)

                def onorm(t):
                    if t >= 2:
                        dve.wait_ge(s_tr, tb + NT + t - 1)
                    normalise(xn[t % 2], o[:, t, :], gout, 2 * t, xb + NT + t, halves=2)

                dve.wait_ge(s_og, (s * 2 + 2) * 16)
                onorm(0)
                onorm(1)
                w_split(U_IN, wost[:], wo_hi[0][:], wo_lo[0][:])
                for t in range(NT):
                    act_lo(t, pair[2 + t % 2], tb + NT + t)
                    if t + 2 < NT:
                        onorm(t + 2)
                w_split(U_IN + 1, wost[:], wo_hi[1][:], wo_lo[1][:])

                def xnorm2(t):
                    dve.wait_ge(s_tr, tb + (2 * NT + t - 1 if t >= 2 else 2 * NT))
                    normalise(xn[t % 2], x1[:, t, :], gffn, 2 * t, xb + 2 * NT + t)

                dve.wait_ge(s_x1, (s + 1) * 16)
                for u in range(U_O):
                    for t in range(NT):
                        dve.wait_ge(s_mm, s * (U_ALL * NT) + (U_IN + u) * NT + t + 1)
                        col = slice(u * COL, (u + 1) * COL)
                        dve.tensor_tensor(x1[:, t, col], bank(t % 4)[:, 0:COL], x1[:, t, col], ALU.add).then_inc(s_evd, 1)
                        if u == U_O - 1 and t >= 1:
                            xnorm2(t - 1) if t == 1 else (act_lo(t - 2, pair[2 + t % 2], tb + 2 * NT + t - 2), xnorm2(t - 1))
                    if u + 2 < U_O:
                        w_split(U_IN + u + 2, wost[:], wo_hi[u % 2][:], wo_lo[u % 2][:])
                xnorm2(NT - 1)
                act_lo(NT - 2, pair[2 + NT % 2], tb + 3 * NT - 2)
                act_lo(NT - 1, pair[2 + (NT - 1) % 2], tb + 3 * NT - 1)
                end(dve)

                begin(dve, s, 5)

                def split(u, slot, hi, lo):
                    dve.wait_ge(s_uhi, s * (6 * NCH) + u + 1)
                    dve.tensor_tensor(lo, ust[slot][:], hi.bitcast(F32), ALU.subtract).then_inc(s_ulo, 1)

                def split_up(b, u, slot):
                    split(u, slot, wu_hi[b][:].rearrange("p k n -> p (k n)"), wu_lo[b][:].rearrange("p k n -> p (k n)"))

                def conv(b, c):
                    K = (s * NCH + c) * 4 + b
                    buf, u = (cg if b % 2 == 0 else cv), pair[b % 2]
                    dve.wait_ge(s_ci, K + 1)
                    dve.scalar_tensor_tensor(buf[:, 1:S], u[:, 0:S - 1], cw[b][:, 0:1], buf[:, 1:S], ALU.mult, ALU.add).then_inc(s_c0, 1)
                    dve.wait_ge(s_c0, K + 1)
                    dve.scalar_tensor_tensor(buf[:, 0:S - 1], u[:, 1:S], cw[b][:, 2:3], buf[:, 0:S - 1], ALU.mult, ALU.add).then_inc(s_cv, 1)

                def hidden(f, c):
                    i = (s * NCH + c) * 2 + f
                    dve.wait_ge(s_sg, i + 1)
                    dve.wait_ge(s_cv, (s * NCH + c) * 4 + 2 * f + 2)
                    dve.tensor_tensor(cv[:], cg[:], cv[:], ALU.mult).then_inc(s_h, 1)
                    dve.wait_ge(s_hhi, i + 1)
                    dve.tensor_tensor(h_lo[f][:], cv[:], h_hi[f][:].bitcast(F32), ALU.subtract).then_inc(s_hlo, 1)

                def add_down(t, c):
                    dve.wait_ge(s_dn, (s * NCH + c) * NT + t + 1)
                    dve.tensor_tensor(x1[:, t, :], pair[2 + t % 2][:], x1[:, t, :], ALU.add).then_inc(s_ya, 1)

                def chunk(c, first, last):
                    def next_up(b, k):
                        if not last:
                            split_up(b, c * 6 + 4 + k, (4 + k) % 3)
                    conv(0, c)
                    next_up(0, 0)
                    if not first:
                        for t in range(NT):
                            add_down(t, c - 1)
                    for f in range(2):
                        k = f if last else f + 1
                        split(c * 6 + 4 + k, (4 + k) % 3, wd_hi[f][:], wd_lo[f][:])
                    conv(1, c)
                    hidden(0, c)
                    next_up(1, 3)
                    conv(2, c)
                    next_up(2, 4)
                    conv(3, c)
                    hidden(1, c)
                    next_up(3, 5)

                for b in range(4):
                    split_up(b, b, b % 3)
                chunk(0, True, False)
                with dve.Fori(1, NCH - 1) as c:
                    chunk(c, False, False)
                chunk(NCH - 1, False, True)
                dve.wait_ge(s_gf, (s + 1) * 16)
                for t in range(NT):
                    add_down(t, NCH - 1)
                    if t >= 1:
                        normalise(x1[:, t - 1, :], x1[:, t - 1, :], gfin, 2 * (t - 1), xb + 3 * NT + t - 1)
                normalise(x1[:, NT - 1, :], x1[:, NT - 1, :], gfin, 2 * (NT - 1), xb + 4 * NT - 1)
                end(dve)


def tables():
    import numpy as np

    def rotary(width):
        half = width // 2
        inv = (np.float32(10000.0) ** (-np.arange(half, dtype=np.float32) * np.float32(2.0 / width))).astype(np.float32)
        ang = np.arange(S, dtype=np.float32)[:, None] * inv[None, :]
        cos, sin = np.cos(ang).astype(np.float32), np.sin(ang).astype(np.float32)
        per_tile = lambda a: np.ascontiguousarray(a.reshape(NT, P, width).transpose(1, 0, 2))
        return per_tile(np.concatenate([cos, cos], 1)), per_tile(np.concatenate([-sin, sin], 1))

    ca, sa = rotary(HA)
    cb, sb = rotary(ROT)
    d = np.arange(MASK_W)[None, :] - (S - P) - np.arange(P)[:, None]
    count = sum(((np.abs(d) <= window // 2) & (d % dil == 0)).astype(np.int64)
                for window, dil in ((128, 1), (512, 4), (2048, 16)))
    logc = np.where(count > 0, np.log(np.maximum(count, 1)) / SCALE_A, NEG_HUGE).astype(np.float32)
    eye = np.eye(P, dtype=np.float32)
    return dict(ident=eye, stack_ident=np.concatenate([np.eye(HA, dtype=np.float32)] * 2, 0),
                cos_a=ca, sin_a=sa, cos_b=cb, sin_b=sb, log_count=logc)


def kernel(x_prompt, x_sample, g_attn, w_in, g_q_lora, w_uq, g_kv_lora, w_ukv, g_out_a, g_out_b, w_o,
           g_ffn, w_up, w_conv, b_conv, w_down, g_final):
    import numpy as np
    import concourse.bacc as bacc
    from concourse.bass_utils import run_bass_kernel_spmd

    a = lambda v: np.ascontiguousarray(v)
    conv = np.concatenate([np.asarray(w_conv)[0], np.asarray(b_conv)], 0).reshape(4, 2, NCH, 2, P)
    conv = conv.transpose(4, 2, 3, 1, 0).reshape(P, NCH * 16)
    arrays = dict(
        x_seqs=np.concatenate([np.asarray(x_prompt).reshape(S, D), np.asarray(x_sample).reshape(S, D)], 0),
        g_attn=np.asarray(g_attn)[0], w_in=np.asarray(w_in)[0], g_q=np.asarray(g_q_lora)[0],
        w_uq=np.asarray(w_uq)[0], g_kv=np.asarray(g_kv_lora)[0], w_ukv=np.asarray(w_ukv)[0],
        g_out=np.concatenate([np.asarray(g_out_a)[0], np.asarray(g_out_b)[0]], 0),
        w_o=np.asarray(w_o)[0], g_ffn=np.asarray(g_ffn)[0], w_up=np.asarray(w_up)[0], conv_wb=conv,
        w_down=np.asarray(w_down)[0], g_final=np.asarray(g_final), **tables())
    nc = bacc.Bacc("TRN2", target_bir_lowering=False, num_devices=1)
    args = {}
    for name, v in arrays.items():
        arrays[name] = v = a(v)
        args[name] = nc.dram_tensor(f"in_{name}", v.shape, mybir.dt.from_np(v.dtype), kind="ExternalInput").ap()
    args["out"] = nc.dram_tensor("out_y", (N_SEQ * S, D), F32, kind="ExternalOutput").ap()
    encoder_kernel(nc, **args)
    r = run_bass_kernel_spmd(nc, [{f"in_{k}": v for k, v in arrays.items()}], core_ids=[0])
    y = r.results[0]["out_y"]
    return y[0:S].reshape(np.asarray(x_prompt).shape), y[S:].reshape(np.asarray(x_sample).shape)
```

```python
from contextlib import ExitStack

import concourse.bass as bass
from concourse import mybir

ALU = mybir.AluOpType
ACT = mybir.ActivationFunctionType
AXX = mybir.AxisListType.X
F32 = mybir.dt.float32
F32R = mybir.dt.float32r
BF16 = mybir.dt.bfloat16

P = 128
N_SEQ = 2
S = 1024
D = 1024
NT = S // P
NK = D // P
HEADS = 8
HA = 64
ROT = 32
HB = HA + ROT
WA = HEADS * HA
RQ, RKV = 256, 128
RC = RQ + RKV
F = 2816
NCH = F // (2 * P)
COL = 256
EPS = 1e-6
NEG_HUGE = -1e30
MASK_W = 2 * S - P
SCALE_A = float(HA) ** -0.5
SCALE_B = float(HB) ** -0.5

U_C, U_QK, U_V = 2, 4, 2
U_IN = U_C + U_QK + U_V
U_O = D // COL
U_ALL = U_IN + U_O
KV_COLS = RKV + ROT
EV_SEQ = (U_ALL - U_C) * NT
ROT_SEQ = (2 + U_QK) * NT

PHASES = 6
ENGINES = 4

LO_CREDIT = 2
EV_CREDIT = 4
YA_CREDIT = 2
ONE = 1


def encoder_kernel(nc: bass.Bass, x_seqs, g_attn, w_in, g_q, w_uq, g_kv, w_ukv, g_out, w_o, g_ffn,
                   w_up, conv_wb, w_down, g_final, ident, stack_ident, cos_a, sin_a, cos_b, sin_b,
                   log_count, out):
    with ExitStack() as ctx:
        used = set()

        def place(name, shape, dt, offset_kb):
            return nc.alloc_sbuf_tensor_at(name, shape, dt, offset=BASE + int(offset_kb * 1024))

        def sem(name):
            return ctx.enter_context(nc.semaphore(name))

        BASE = 16512
        R_O, R_C, R_Q, R_X, R_REST = 3.5, 35.5, 67.5, 131.5, 195.5
        idn = place("idn", [P, P], F32, 0)
        stk = place("stk", [P, HA], F32, 0.5)
        cosb = place("cosb", [P, NT, ROT], F32, 0.75)
        sinb = place("sinb", [P, NT, ROT], F32, 1.75)
        ss = place("ss", [P, 32], F32, 2.75)
        sd = place("sd", [P, 32], F32, 2.875)
        rs = place("rs", [P, 32], F32, 3.0)
        mx = place("mx", [P, 4], F32, 3.125)
        nm = place("nm", [P, 4], F32, 3.15625)
        den = place("den", [P, 2, NT], F32, 3.1875)
        rden = place("rden", [P, 4], F32, 3.25)
        eps = place("eps", [P, 1], F32, 3.28125)
        cw = [place(f"cw{b}", [P, 4], F32, 3.3125 + b / 32) for b in range(4)]

        wc_hi = [place(f"wc_hi{i}", [P, NK, COL if i == 0 else KV_COLS], F32R, R_Q + 16 * i) for i in range(2)]
        wc_lo = [place(f"wc_lo{i}", [P, NK, COL if i == 0 else KV_COLS], F32R, R_Q + 8 + 16 * i) for i in range(2)]
        w_hi = [place(f"w_hi{i}", [P, NK, COL], F32R, R_O + 16 * i) for i in range(2)]
        w_lo = [place(f"w_lo{i}", [P, NK, COL], F32R, R_O + 16 * i + 8) for i in range(2)]
        ct_hi = place("ct_hi", [P, 3, S], F32R, R_C)
        ct_lo = place("ct_lo", [P, 3, S], F32R, R_C + 12)
        krot = place("krot", [P, NT, ROT], F32, R_C + 24)
        glora = place("glora", [P, RC], F32, R_C + 25)
        cr = [place(f"cr{i}", [P, RC + ROT], F32, R_C + 26.5 + 1.625 * i) for i in range(2)]
        junk = place("junk", [P, D], BF16, R_C + 29.75)
        qk = place("qk", [P, NT, 2 * WA], F32, R_Q)
        va = place("va", [P, NT, WA], F32, R_Q + 32)
        wst = place("wst", [P, NK, COL], F32, R_Q + 48)
        xt = [place(f"xt{i}", [P, D], F32, R_REST + 4 * i) for i in range(2)]
        at_hi = place("at_hi", [P, NK, S], F32R, R_X)
        at_lo = place("at_lo", [P, NK, S], F32R, R_X + 32)
        gin = place("gin", [P, D], F32, R_REST + 8)
        cosa = place("cosa", [P, NT, HA], F32, R_Q + 56)
        sina = place("sina", [P, NT, HA], F32, R_Q + 58)
        pra = [place(f"pra{i}", [P, COL], F32, R_Q + 60 + 2 * i) for i in range(2)]
        prb = [place(f"prb{i}", [P, COL], F32, R_Q + 61 + 2 * i) for i in range(2)]

        o = place("o", [P, NT, D], F32, R_O)
        pt_hi_a = [place(f"pt_hi_a{i}", [P, NT, 2 * P], F32R, R_X + 16 * i) for i in range(2)]
        pt_lo_a = [place(f"pt_lo_a{i}", [P, NT, 2 * P], F32R, R_X + 16 * i + 8) for i in range(2)]
        pt_hi_b = [place(f"pt_hi_b{i}", [P, NT, 2 * P], F32R, R_Q + 16 * i) for i in range(2)]
        pt_lo_b = [place(f"pt_lo_b{i}", [P, NT, 2 * P], F32R, R_Q + 16 * i + 8) for i in range(2)]
        q2 = [place(f"q2{i}", [P, S], F32R, R_X + 32 + 12 * i) for i in range(2)]
        khh = [place(f"khh{i}", [P, S], F32R, R_X + 36 + 12 * i) for i in range(2)]
        kll = [place(f"kll{i}", [P, S], F32R, R_X + 40 + 12 * i) for i in range(2)]
        logc = place("logc", [P, MASK_W], F32, R_Q + 56)
        st_a = dict(q=place("stqa", [P, NT, P], F32, R_REST), k=place("stka", [P, NT, P], F32, R_REST + 4),
                    v=place("stva", [P, NT, HA], F32, R_C + 29))
        ot_a = place("ot_a", [P, 2 * P], F32, R_C + 31)
        v2_a = [place(f"v2a{i}", [P, NT, P], F32R, R_Q + 48 + 4 * i) for i in range(2)]
        pr_a = [place(f"pr_a{i}", [P, S], F32, R_X + 56 + 4 * i) for i in range(2)]
        qh = [place(f"qh{i}", [P, S], F32R, R_Q + 32 + 16 * i) for i in range(2)]
        ql = [place(f"ql{i}", [P, S], F32R, R_Q + 36 + 16 * i) for i in range(2)]
        kh = [place(f"kh{i}", [P, S], F32R, R_Q + 40 + 16 * i) for i in range(2)]
        kl = [place(f"kl{i}", [P, S], F32R, R_Q + 44 + 16 * i) for i in range(2)]
        st_b = dict(q=place("stqb", [P, NT, HB], F32, R_REST), k=place("stkb", [P, NT, HB], F32, R_REST + 3),
                    v=place("stvb", [P, NT, HA], F32, R_REST + 6))
        ot_b = place("ot_b", [P, 2 * P], F32, R_C + 15)
        v2_b = [place(f"v2b{i}", [P, NT, P], F32R, R_C + 16 + 4 * i) for i in range(2)]
        pr_b = [place(f"pr_b{i}", [P, S], F32, R_C + 24 + 4 * i) for i in range(2)]

        qb = place("qb", [P, NT, HEADS * HB], F32, R_X)
        kb = place("kb", [P, NT, HEADS * HB], F32, R_X + 24)
        vb = place("vb", [P, NT, WA], F32, R_X + 48)
        NUQ, NUKV = HEADS * HB, HEADS * 2 * HA
        uq_hi = place("uq_hi", [P, 2, NUQ], F32R, R_Q)
        uq_lo = place("uq_lo", [P, 2, NUQ], F32R, R_Q + 6)
        ukv_hi = place("ukv_hi", [P, NUKV], F32R, R_Q + 12)
        ukv_lo = place("ukv_lo", [P, NUKV], F32R, R_Q + 16)
        uq_st = place("uq_st", [P, 2, NUQ], F32, R_Q + 20)
        ukv_st = place("ukv_st", [P, NUKV], F32, R_Q + 26)
        pba = [place(f"pba{i}", [P, HEADS, ROT], F32, R_Q + 30 + 2 * i) for i in range(2)]
        pbb = [place(f"pbb{i}", [P, HEADS, ROT], F32, R_Q + 31 + 2 * i) for i in range(2)]

        x1 = place("x1", [P, NT, D], F32, R_C)
        at2_hi = place("at2_hi", [P, NK, S], F32R, R_Q)
        at2_lo = place("at2_lo", [P, NK, S], F32R, R_Q + 32)
        wo_hi = [place(f"wo_hi{i}", [P, NK, COL], F32R, R_X + 32 + 16 * i) for i in range(2)]
        wo_lo = [place(f"wo_lo{i}", [P, NK, COL], F32R, R_X + 40 + 16 * i) for i in range(2)]
        wost = place("wost", [P, NK, COL], F32, R_REST)
        gout = place("gout", [P, D], F32, R_REST + 8)
        xn = [place(f"xn{i}", [P, D], F32, R_X + 16 + 4 * i) for i in range(2)]
        gffn = place("gffn", [P, D], F32, R_X + 24)
        junk2 = place("junk2", [P, D], BF16, R_X + 28)

        wu_hi = [place(f"wu_hi{b}", [P, NK, P], F32R, R_X + 8 * b) for b in range(4)]
        wu_lo = [place(f"wu_lo{b}", [P, NK, P], F32R, R_X + 8 * b + 4) for b in range(4)]
        wd_hi = [place(f"wd_hi{f}", [P, D], F32R, R_X + 32 + 8 * f) for f in range(2)]
        wd_lo = [place(f"wd_lo{f}", [P, D], F32R, R_X + 36 + 8 * f) for f in range(2)]
        h_hi = [place(f"h_hi{f}", [P, S], F32R, R_X + 48 + 8 * f) for f in range(2)]
        h_lo = [place(f"h_lo{f}", [P, S], F32R, R_X + 52 + 8 * f) for f in range(2)]
        ust = [place(f"ust{i}", [P, D], F32, R_O + 4 * i) for i in range(3)]
        cg = place("cg", [P, S], F32, R_O + 12)
        cv = place("cv", [P, S], F32, R_O + 16)
        gfin = place("gfin", [P, D], F32, R_O + 20)
        junk3 = place("junk3", [P, D], BF16, R_O + 24)

        pair = [ctx.enter_context(nc.psum_tensor(f"pair{i}", [P, 2 * 512], F32)) for i in range(4)]

        def bank(i):
            return pair[i // 2][:, 512 * (i % 2):512 * (i % 2) + 512]

        s_phase, s_passed = sem("phase_ended"), sem("wait_passed")
        s_const, s_eps = sem("constants_landed"), sem("eps_set")
        s_x = [sem(f"x_tile_landed{i}") for i in range(2)]
        s_inw, s_gin, s_wst, s_whi, s_wlo = sem("input_tables_landed"), sem("input_gain_landed"), sem("w_unit_landed"), sem("w_hi_split"), sem("w_lo_split")
        s_ss, s_std, s_rs, s_xn = sem("squares_summed"), sem("rms_ready"), sem("rrms_ready"), sem("tile_normalised")
        s_tr, s_ahi, s_alo = sem("tile_transposed"), sem("act_hi_split"), sem("act_lo_split")
        s_mm, s_eva, s_evd = sem("unit_product_ready"), sem("unit_evicted_by_act"), sem("unit_evicted_by_dve")
        s_css, s_cstd, s_crs, s_cn = sem("c_squares"), sem("c_rms"), sem("c_rrms"), sem("c_normalised")
        s_ctr, s_chi, s_clo, s_rot = sem("c_transposed"), sem("c_hi_split"), sem("c_lo_split"), sem("rotary_products")
        s_bw, s_bhi, s_blo = sem("b_weights_landed"), sem("b_weights_hi"), sem("b_weights_lo")
        s_bmm, s_bea, s_bed = sem("b_product_ready"), sem("b_evicted_by_act"), sem("b_evicted_by_dve")
        s_logc = sem("log_count_landed")
        s_st = {n: sem(f"head_{n}_staged") for n in "qkv"}
        s_sc, s_max, s_nm, s_pr = sem("scores_ready"), sem("row_max"), sem("minus_max_ready"), sem("probs_ready")
        s_pt, s_pthi, s_ptlo = sem("probs_transposed"), sem("pt_hi_split"), sem("pt_lo_split")
        s_pv, s_ot, s_rden = sem("pv_ready"), sem("ot_evicted"), sem("rden_ready")
        s_mi, s_mihi, s_mid = sem("misc_bank_filled"), sem("misc_hi_split"), sem("misc_bank_free")
        s_vhi, s_vlo = sem("v_hi_split"), sem("v_lo_split")
        s_x1 = [sem(f"residual_landed{i}") for i in range(3)]
        s_og, s_gf2 = sem("output_gain_landed"), sem("mlp_gain_landed")
        s_ust = [sem(f"mlp_slot_landed{i}") for i in range(3)]
        s_cw = [sem(f"conv_taps_landed{b}") for b in range(4)]
        s_uhi, s_ulo = sem("mlp_w_hi_split"), sem("mlp_w_lo_split")
        s_up, s_ci, s_c0, s_cv = sem("up_ready"), sem("conv_middle"), sem("conv_left"), sem("conv_done")
        s_sg, s_h, s_hhi, s_hlo = sem("gate_silu"), sem("hidden_ready"), sem("hidden_hi"), sem("hidden_lo")
        s_dn, s_ya = sem("down_ready"), sem("down_added")
        s_gf, s_out = sem("final_gain_landed"), sem("output_written")

        block = ctx.enter_context(nc.Block())

        def await_(eng, semaphore, value):
            eng.wait_ge(semaphore, value)
            eng.sem_inc(s_passed, 1)

        def begin(eng, s, ph):
            eng.wait_ge(s_phase, s * (PHASES * ENGINES) + (ph * ENGINES + ONE))

        def end(eng):
            eng.drain().then_inc(s_phase, 1)

        BODY = [(0, 3, "round", 3), (0, 4, "osum", 0), (0, 5, "round", 0), (0, 6, "osum", 1),
                (0, 7, "round", 1), (1, 0, "osum", 2), (1, 1, "round", 2), (1, 2, "osum", 3)]
        FIRST = 7

        HEAD0 = (0, 2, 3, 1)

        def steps(n, left):
            m = n * 8 + (FIRST if left else FIRST - 3)
            for off, t, use, a in BODY:
                here = left >= (1 if a == 3 else 2) if use == "round" else True
                if here or left or not off:
                    yield off, t, use if here else None, a, m
                if here:
                    m = m + 1

        @block.sync
        def _(sp):
            def begin_sp(s, ph):
                begin(sp, s, ph)
                sp.sem_inc(s_passed, 1)

            w_in_v = w_in.rearrange("(k p) n -> p k n", p=P)
            w_o_v = w_o.rearrange("(k p) n -> p k n", p=P)
            w_up_v = w_up.rearrange("(k p) n -> p k n", p=P)
            x_v = x_seqs.rearrange("(t p) n -> t p n", p=P)
            x_all = x_seqs.rearrange("(t p) n -> p t n", p=P)
            out_v = out.rearrange("(t p) n -> t p n", p=P)

            def stage(h, src, dst, width, n):
                if n == "v":
                    sp.dma_start(dst[n][:], src[:, :, bass.ds(h * width, width)]).then_inc(s_st[n], 16)
                    return
                for i in range(2):
                    if width == HA:
                        to, t = dst[n][:, :, i * HA:(i + 1) * HA], slice(0, NT)
                    else:
                        t = slice(i * NT // 2, (i + 1) * NT // 2)
                        to = dst[n][:, t, :]
                    sp.dma_start(to, src[:, t, bass.ds(h * width, width)]).then_inc(s_st[n], 16)

            def load_first(row):
                for t in range(2):
                    sp.dma_start(xt[t][:], x_v[row + t]).then_inc(s_x[t], 16)
                sp.dma_start(gin[:], g_attn.partition_broadcast(P)).then_inc(s_gin, 16)

            load_first(0)
            sp.dma_start(idn[:], ident).then_inc(s_const, 16)
            sp.dma_start(stk[:], stack_ident).then_inc(s_const, 16)
            sp.dma_start(cosb[:], cos_b).then_inc(s_const, 16)
            sp.dma_start(sinb[:], sin_b).then_inc(s_const, 16)

            with sp.Fori(0, N_SEQ) as s:
                begin_sp(s, 0)
                sp.dma_start(wst[:], w_in_v[:, :, 3 * WA:3 * WA + RQ]).then_inc(s_wst, 16)
                sp.dma_start(glora[:, 0:RQ], g_q.partition_broadcast(P)).then_inc(s_inw, 16)
                sp.dma_start(glora[:, RQ:RC], g_kv.partition_broadcast(P)).then_inc(s_inw, 16)
                sp.dma_start(cosa[:], cos_a).then_inc(s_inw, 16)
                sp.dma_start(sina[:], sin_a).then_inc(s_inw, 16)
                for t in range(2, NT):
                    await_(sp, s_tr, s * (3 * NT) + t - 1)
                    sp.dma_start(xt[t % 2][:], x_v[s * NT + t]).then_inc(s_x[t % 2], 16)
                    if t in (2, 4, 6):
                        u = t // 2
                        await_(sp, s_wlo, s * U_ALL + u)
                        if u == 1:
                            sp.dma_start(wst[:, :, 0:KV_COLS], w_in_v[:, :, 3 * WA + RQ:3 * WA + RC + ROT]).then_inc(s_wst, 16)
                        else:
                            sp.dma_start(wst[:], w_in_v[:, :, (u - 2) * COL:(u - 1) * COL]).then_inc(s_wst, 16)
                with sp.Fori(2, U_QK + U_V) as j:
                    await_(sp, s_wlo, s * U_ALL + j + U_C)
                    sp.dma_start(wst[:], w_in_v[:, :, bass.ds(j * COL, COL)]).then_inc(s_wst, 16)
                for i, n in enumerate("qkv"):
                    await_(sp, s_evd, s * EV_SEQ + (2 * (i + 1) if i < 2 else 2 * i + 1) * NT + EV_CREDIT)
                    if n == "v":
                        sp.dma_start(logc[:], log_count).then_inc(s_logc, 16)
                    stage(0, va if n == "v" else qk[:, :, i * WA:(i + 1) * WA], st_a, HA, n)
                end(sp)

                def attention(mixer, src_q, src_k, src_v, dst, width):
                    n0 = s * (2 * HEADS) + mixer * HEADS
                    srcs = dict(q=(src_q, width), k=(src_k, width), v=(src_v, HA))
                    if mixer == 0:
                        await_(sp, s_mi, n0 * 8 + 4)
                    for n in "qk":
                        stage(1, srcs[n][0], dst, srcs[n][1], n)
                    if mixer == 0:
                        await_(sp, s_vlo, n0 + 1)
                    stage(1, srcs["v"][0], dst, srcs["v"][1], "v")
                    with sp.Fori(0, HEADS - 2) as h:
                        n = n0 + h
                        await_(sp, s_mi, n * 8 + (FIRST - 1))
                        stage(h + 2, srcs["q"][0], dst, srcs["q"][1], "q")
                        await_(sp, s_vlo, n + 2)
                        stage(h + 2, srcs["v"][0], dst, srcs["v"][1], "v")
                        await_(sp, s_mi, n * 8 + (FIRST + 1))
                        stage(h + 2, srcs["k"][0], dst, srcs["k"][1], "k")

                def heads_landed(mixer):
                    for n, k in (("q", 32), ("k", 32), ("v", 16)):
                        await_(sp, s_st[n], (s * (2 * HEADS) + (mixer + 1) * HEADS) * k)

                begin_sp(s, 1)
                attention(0, qk, qk[:, :, WA:2 * WA], va, st_a, HA)
                heads_landed(0)
                sp.dma_start(uq_st[:], w_uq.rearrange("(k p) n -> p k n", p=P)).then_inc(s_bw, 16)
                sp.dma_start(ukv_st[:], w_ukv).then_inc(s_bw, 16)
                end(sp)

                begin_sp(s, 2)
                end(sp)

                begin_sp(s, 3)
                for n, k in (("q", 32), ("k", 32), ("v", 16)):
                    sp.sem_inc(s_st[n], k)
                for i in range(3):
                    sp.dma_start(x1[:, i, :], x_v[s * NT + i]).then_inc(s_x1[i], 16)
                sp.dma_start(gout[:], g_out.partition_broadcast(P)).then_inc(s_og, 16)
                attention(1, qb, kb, vb, st_b, HB)
                heads_landed(1)
                await_(sp, s_mi, (s * (2 * HEADS) + (2 * HEADS - 1)) * 8 + (FIRST - 3))
                await_(sp, s_vlo, s * (2 * HEADS) + 2 * HEADS)
                sp.dma_start(wost[:], w_o_v[:, :, 0:COL]).then_inc(s_wst, 16)
                end(sp)

                begin_sp(s, 4)
                sp.dma_start(gffn[:], g_ffn.partition_broadcast(P)).then_inc(s_gf2, 16)
                for i in range(3, NT):
                    sp.dma_start(x1[:, i, :], x_v[s * NT + i]).then_inc(s_x1[i % 3], 16)
                with sp.Fori(1, U_O) as j:
                    await_(sp, s_wlo, s * U_ALL + j + U_IN)
                    sp.dma_start(wost[:], w_o_v[:, :, bass.ds(j * COL, COL)]).then_inc(s_wst, 16)

                def slot_free(u):
                    await_(sp, s_ulo, s * (6 * NCH) + u - 2)

                def load_up(b, c, slot):
                    col = (b % 2) * F + (b // 2) * P
                    sp.dma_start(ust[slot][:].rearrange("p (k n) -> p k n", k=NK),
                                 w_up_v[:, :, bass.ds(c * (2 * P) + col, P)]).then_inc(s_ust[slot], 16)

                def load_taps(b, c):
                    sp.dma_start(cw[b][:], conv_wb[:, bass.ds(c * 16 + 4 * b, 4)]).then_inc(s_cw[b], 16)

                def load_down(f, c, slot):
                    sp.dma_start(ust[slot][:], w_down[bass.ds(c * (2 * P) + f * P, P), :]).then_inc(s_ust[slot], 16)

                await_(sp, s_xn, s * (4 * NT) + 2 * NT)
                for b in range(3):
                    load_up(b, 0, b % 3)
                    load_taps(b, 0)
                end(sp)

                begin_sp(s, 5)
                slot_free(3)
                load_up(3, 0, 0)
                load_taps(3, 0)
                sp.dma_start(gfin[:], g_final.partition_broadcast(P)).then_inc(s_gf, 16)
                with sp.Fori(0, NCH - 1) as c:
                    for k, what in enumerate(("u0", "d0", "d1", "u1", "u2", "u3")):
                        slot_free(c * 6 + 4 + k)
                        if what[0] == "u":
                            b = int(what[1])
                            load_up(b, c + 1, (4 + k) % 3)
                            await_(sp, s_cv, (s * NCH + c) * 4 + b + 1)
                            load_taps(b, c + 1)
                        else:
                            load_down(int(what[1]), c, (4 + k) % 3)
                load_first(s * (-NT) + NT)
                for f in range(2):
                    slot_free(6 * NCH - 2 + f)
                    load_down(f, NCH - 1, (6 * NCH - 2 + f) % 3)
                for t in range(NT):
                    await_(sp, s_xn, s * (4 * NT) + 3 * NT + t + 1)
                    sp.dma_start(out_v[s * NT + t], x1[:, t, :]).then_inc(s_out, 16)
                await_(sp, s_out, s * (16 * NT) + 16 * NT)
                end(sp)
            for t in range(2):
                sp.wait_ge(s_x[t], 16 * (N_SEQ * NT // 2 + 1))
            sp.wait_ge(s_gin, 16 * (N_SEQ + 1))

        @block.tensor
        def _(pe):
            def product(dst, passes):
                n = len(passes)
                for i, (lhs, rhs) in enumerate(passes):
                    mm = pe.matmul(dst, lhs, rhs, start=(i == 0), stop=(i == n - 1))
                return mm

            def transpose_tile(src, dst):
                for k in range(NK):
                    tr = pe.transpose(dst[:, k * P:(k + 1) * P], src[:, k * P:(k + 1) * P], idn[:])
                tr.then_inc(s_tr, 1)

            def unit(t, whi, wlo, n, dst, at_hi, at_lo):
                tok = slice(t * P, (t + 1) * P)
                passes = []
                for k in range(NK):
                    passes += [(at_hi[:, k, tok], whi[:, k, 0:n]), (at_hi[:, k, tok], wlo[:, k, 0:n]),
                               (at_lo[:, k, tok], whi[:, k, 0:n])]
                product(dst[:, 0:n], passes).then_inc(s_mm, 1)

            pe.wait_ge(s_const, 16 * 4)
            with pe.Fori(0, N_SEQ) as s:
                begin(pe, s, 0)
                pe.wait_ge(s_xn, s * (4 * NT) + 1)
                transpose_tile(xt[0], pair[2])
                for t in range(NT):
                    pe.wait_ge(s_alo, s * (3 * NT) + t + 1)
                    if t + 1 < NT:
                        pe.wait_ge(s_xn, s * (4 * NT) + t + 2)
                        transpose_tile(xt[(t + 1) % 2], pair[2])
                    for u in range(U_C):
                        if t == 0:
                            pe.wait_ge(s_wlo, s * U_ALL + u + 1)
                        if t >= 2:
                            pe.wait_ge(s_eva, s * (U_C * NT) + (t - 2) * U_C + u + 1)
                        unit(t, wc_hi[u], wc_lo[u], COL if u == 0 else KV_COLS, bank((t * U_C + u) % 4), at_hi, at_lo)
                    for tc in ([t - 1] if t >= 1 else []) + ([t] if t == NT - 1 else []):
                        pe.wait_ge(s_cn, s * NT + tc + 1)
                        if tc >= 1:
                            pe.wait_ge(s_clo, s * NT + tc)
                        for k in range(3):
                            tr = pe.transpose(bank(6)[:, k * P:(k + 1) * P], cr[tc % 2][:, k * P:(k + 1) * P], idn[:])
                        tr.then_inc(s_ctr, 1)
                with pe.Fori(0, (U_QK + U_V) // 2) as j:
                    for e in range(2):
                        pe.wait_ge(s_wlo, s * U_ALL + j * 2 + U_C + e + 1)
                        for t in range(NT):
                            if e == 0 and t == 0:
                                pe.wait_ge(s_eva, s * (U_C * NT) + U_C * NT)
                            pe.wait_ge(s_evd, s * EV_SEQ + j * (2 * NT) + e * NT + t - 3 + EV_CREDIT)
                            unit(t, w_hi[e], w_lo[e], COL, bank(t % 4), at_hi, at_lo)

                def first_rounds(src_q, src_k):
                    for i, r in enumerate(HEAD0):
                        src = src_q if r < 2 else src_k
                        for k in range(4):
                            tile = src[:, 4 * (r % 2) + k, 0:P] if src is st_a["q"] or src is st_a["k"] else src[:, 4 * (r % 2) + k, 0:HB]
                            rows = P if tile.shape[-1] == P else HB
                            tr = pe.transpose(bank(4 + i)[0:rows, k * P:(k + 1) * P], tile, idn[:])
                        tr.then_inc(s_mi, 1)

                for n in "qk":
                    pe.wait_ge(s_st[n], s * (2 * HEADS * 32) + 32)
                first_rounds(st_a["q"], st_a["k"])
                end(pe)

                def attention(mixer, prep_q, prep_k, score_passes, v2, ot, prob, st, pt_hi, pt_lo):
                    n0 = s * (2 * HEADS) + mixer * HEADS

                    def scores(e, t):
                        q = slice(t * P, (t + 1) * P)
                        for half in range(2):
                            k = slice(half * 512, half * 512 + 512)
                            mm = product(pair[t % 2][:, k], score_passes(e, q, k))
                        mm.then_inc(s_sc, 1)

                    def round_(r, m, heads_staged):
                        pe.wait_ge(s_mid, m + ONE)
                        if r % 2 == 0:
                            pe.wait_ge(s_st["q" if r < 2 else "k"], heads_staged * 32)
                        (prep_q if r < 2 else prep_k)(r % 2)

                    def pv(e, n, g, half):
                        if half != 1:
                            pe.wait_ge(s_ptlo, n * 16 + 4 * g + 4 + LO_CREDIT)
                            if g == 0:
                                pe.wait_ge(s_vlo, n + 1)
                            pe.wait_ge(s_ot, n * 4 + (g + ONE))
                        keys = range(NT) if half is None else range(half * NT // 2, (half + 1) * NT // 2)
                        for k in keys:
                            pe.matmul(bank(6)[:, 0:2 * P], v2[e][:, k, :], pt_hi[g % 2][:, k, :],
                                      start=(k == 0), stop=False)
                            mm = pe.matmul(bank(6)[:, 0:2 * P], v2[e][:, k, :], pt_lo[g % 2][:, k, :],
                                           start=False, stop=(k == NT - 1))
                        if half != 0:
                            mm.then_inc(s_pv, 1)

                    def osum(n, g, m):
                        pe.wait_ge(s_ot, n * 4 + (g + 1 + ONE))
                        pe.wait_ge(s_mid, m + ONE)
                        for i in range(2):
                            mm = pe.matmul(bank(7)[:, i * HA:(i + 1) * HA], ot[:, i * P:(i + 1) * P], stk[:],
                                           start=True, stop=True)
                        mm.then_inc(s_mi, 1)

                    def step(e, n, t, left):
                        pe.wait_ge(s_pr, n * 8 + t + 1)
                        for hb in range(2):
                            pe.wait_ge(s_ptlo, n * 16 + 2 * t + hb - 1 + LO_CREDIT)
                            for k in range(4):
                                c = (4 * hb + k) * P
                                tr = pe.transpose(bank(4 + hb)[:, k * P:(k + 1) * P], prob[t % 2][:, c:c + P], idn[:])
                            tr.then_inc(s_pt, 1)
                        if t + 3 < NT or left:
                            pe.wait_ge(s_pr, n * 8 + t + 2)
                        if t + 3 < NT:
                            scores(e, t + 3)
                        elif left:
                            if t + 3 == NT:
                                pe.wait_ge(s_mid, n * 8 + (FIRST + 1 + ONE))
                            scores(1 - e, t + 3 - NT)

                    def body(e, n, left):
                        for off, t, use, a, m in steps(n, left):
                            if left or not off:
                                step((e + off) % 2, n + off, t, left - off)
                            if use == "round":
                                round_(a, m, n + (2 if a == 3 else 3))
                            if use == "osum":
                                osum(n, a, m)
                            if off == 0:
                                pv(e, n, t // 2 - 1, t % 2)
                            elif t < 2 and left:
                                pv(e, n, 3, t)
                            elif t < 2:
                                pv(e, n, 3, None)
                            elif left:
                                pv(1 - e, n + 1, 0, 0)

                    pe.wait_ge(s_mid, n0 * 8 + (3 + ONE))
                    scores(0, 0)
                    scores(0, 1)
                    pe.wait_ge(s_pr, n0 * 8 + 1)
                    scores(0, 2)
                    for t in range(3):
                        step(0, n0, t, HEADS - 1)
                        round_(t, n0 * 8 + 4 + t, n0 + 2)
                    pv(0, n0, 0, 0)
                    with pe.Fori(0, HEADS // 2 - 1) as j:
                        for e in range(2):
                            body(e, j * 2 + (n0 + e), 2)
                    body(0, n0 + (HEADS - 2), 1)
                    body(1, n0 + (HEADS - 1), 0)

                def prep(dst_rows, src):
                    def go(half):
                        for i in range(4):
                            tr = pe.transpose(bank(7)[0:dst_rows, i * P:(i + 1) * P], src[:, 4 * half + i, :], idn[:])
                        tr.then_inc(s_mi, 1)
                    return go

                begin(pe, s, 1)
                attention(0, prep(P, st_a["q"]), prep(P, st_a["k"]),
                          lambda e, q, k: [(q2[e][:, q], khh[e][:, k]), (q2[e][:, q], kll[e][:, k])],
                          v2_a, ot_a, pr_a, st_a, pt_hi_a, pt_lo_a)
                end(pe)

                begin(pe, s, 2)
                pe.wait_ge(s_blo, s * 2 + 2)
                for t in range(NT):
                    tok = slice(t * P, (t + 1) * P)
                    if t >= 2:
                        pe.wait_ge(s_bed, s * (2 * NT) + 2 * (t - 2) + 2)
                    for a, b in ((0, 512), (512, NUQ)):
                        passes = []
                        for k in range(2):
                            passes += [(ct_hi[:, k, tok], uq_hi[:, k, a:b]), (ct_hi[:, k, tok], uq_lo[:, k, a:b]),
                                       (ct_lo[:, k, tok], uq_hi[:, k, a:b])]
                        mm = product(pair[t % 2][:, a:b], passes)
                    mm.then_inc(s_bmm, 1)
                    for a, b in ((0, 512), (512, 1024)):
                        mm = product(pair[2 + t % 2][:, a:b], [
                            (ct_hi[:, 2, tok], ukv_hi[:, a:b]), (ct_hi[:, 2, tok], ukv_lo[:, a:b]),
                            (ct_lo[:, 2, tok], ukv_hi[:, a:b])])
                    mm.then_inc(s_bmm, 1)
                pe.wait_ge(s_bed, s * (2 * NT) + 2 * NT)
                first_rounds(qb, kb)
                end(pe)

                begin(pe, s, 3)
                attention(1, prep(HB, st_b["q"]), prep(HB, st_b["k"]),
                          lambda e, q, k: [(qh[e][0:HB, q], kh[e][0:HB, k]), (qh[e][0:HB, q], kl[e][0:HB, k]),
                                           (ql[e][0:HB, q], kh[e][0:HB, k])],
                          v2_b, ot_b, pr_b, st_b, pt_hi_b, pt_lo_b)
                end(pe)

                begin(pe, s, 4)

                def mlp_input(t):
                    pe.wait_ge(s_xn, s * (4 * NT) + 2 * NT + t + 1)
                    if t >= 2:
                        pe.wait_ge(s_alo, s * (3 * NT) + 2 * NT + t - 1)
                    transpose_tile(xn[t % 2], pair[2 + t % 2])

                def wo_input(t):
                    pe.wait_ge(s_xn, s * (4 * NT) + NT + t + 1)
                    if t >= 2:
                        pe.wait_ge(s_alo, s * (3 * NT) + NT + t - 1)
                    transpose_tile(xn[t % 2], pair[2 + t % 2])

                wo_input(0)
                for u in range(U_O):
                    pe.wait_ge(s_wlo, s * U_ALL + U_IN + u + 1)
                    for t in range(NT):
                        if u == 0:
                            if t + 1 < NT:
                                wo_input(t + 1)
                            pe.wait_ge(s_alo, s * (3 * NT) + NT + t + 1)
                        pe.wait_ge(s_evd, s * EV_SEQ + (U_QK + U_V + u) * NT + t - 3 + EV_CREDIT)
                        unit(t, wo_hi[u % 2], wo_lo[u % 2], COL, bank(t % 4), at2_hi, at2_lo)
                        if u == U_O - 1 and t >= 2:
                            mlp_input(t - 2)
                mlp_input(NT - 2)
                mlp_input(NT - 1)
                end(pe)

                begin(pe, s, 5)

                def up(b, c, first):
                    K = (s * NCH + c) * 4 + b
                    if first:
                        pe.wait_ge(s_ulo, s * (6 * NCH) + b + 1)
                        if b >= 2:
                            pe.wait_ge(s_cv, K - 1)
                    else:
                        pe.wait_ge(s_ulo, s * (6 * NCH) + (c - 1) * 6 + 5 + (0, 3, 4, 5)[b])
                        pe.wait_ge(s_cv, K - 1)
                    for half in range(2):
                        tok = slice(half * 512, half * 512 + 512)
                        passes = []
                        for k in range(NK):
                            passes += [(wu_hi[b][:, k, :], at2_hi[:, k, tok]), (wu_hi[b][:, k, :], at2_lo[:, k, tok]),
                                       (wu_lo[b][:, k, :], at2_hi[:, k, tok])]
                        mm = product(pair[b % 2][:, tok], passes)
                    mm.then_inc(s_up, 1)

                def down(c, tail):
                    n = 6 * NCH if tail else (c * 6 + 7)
                    pe.wait_ge(s_ulo, s * (6 * NCH) + n)
                    pe.wait_ge(s_hlo, (s * NCH + c) * 2 + (2 + ONE))
                    for t in range(NT):
                        tok = slice(t * P, (t + 1) * P)
                        pe.wait_ge(s_ya, (s * NCH + c) * NT + t - 1 + YA_CREDIT)
                        for half in range(2):
                            col = slice(half * 512, half * 512 + 512)
                            passes = []
                            for f in range(2):
                                passes += [(h_hi[f][:, tok], wd_hi[f][:, col]), (h_hi[f][:, tok], wd_lo[f][:, col]),
                                           (h_lo[f][:, tok], wd_hi[f][:, col])]
                            mm = product(pair[2 + t % 2][:, col], passes)
                        mm.then_inc(s_dn, 1)

                for b in range(4):
                    up(b, 0, True)
                with pe.Fori(1, NCH) as c:
                    up(0, c, False)
                    down(c - 1, False)
                    for b in range(1, 4):
                        up(b, c, False)
                down(NCH - 1, True)
                end(pe)


        @block.scalar
        def _(act):
            def squares(src, n_cols, junk_buf, col, done, j0=0):
                act.activation(junk_buf[:, j0:j0 + n_cols], src, ACT.Square, accum_out=ss[:, col:col + 1]).then_inc(done, 1)

            def rms(col, n, n_cols, done, inc=True):
                op = act.activation(sd[:, col:col + n], ss[:, col:col + n], ACT.Sqrt, bias=eps[:, 0:1], scale=1.0 / n_cols)
                if inc:
                    op.then_inc(done, 1)

            def act_hi(t, src, idx, at_hi):
                act.wait_ge(s_tr, idx + 1)
                act.copy(at_hi[:, :, t * P:(t + 1) * P], src[:].rearrange("p (k n) -> p k n", k=NK)).then_inc(s_ahi, 1)

            act.wait_ge(s_eps, 1)
            act.wait_ge(s_const, 16 * 4)
            with act.Fori(0, N_SEQ) as s:
                begin(act, s, 0)
                xb = s * (4 * NT)
                tb = s * (3 * NT)

                def stats(t):
                    act.wait_ge(s_x[t % 2], s * (16 * NT // 2) + 16 * (t // 2 + 1))
                    squares(xt[t % 2][:], D, junk, 2 * t, s_ss)
                    act.wait_ge(s_ss, xb + t + 1)
                    rms(2 * t, 1, D, s_std)

                def w_split(u, src, dst):
                    act.wait_ge(s_wst, (s * U_ALL + u + 1) * 16)
                    act.copy(dst, src).then_inc(s_whi, 1)

                stats(0)
                stats(1)
                w_split(0, wst[:], wc_hi[0][:])
                act_hi(0, pair[2], tb, at_hi)
                w_split(1, wst[:, :, 0:KV_COLS], wc_hi[1][:])
                for t in range(NT):
                    if t + 1 < NT:
                        act_hi(t + 1, pair[2], tb + t + 1, at_hi)
                    if t + 2 < NT:
                        stats(t + 2)
                    c = cr[t % 2]
                    if t >= 2:
                        act.wait_ge(s_ctr, s * NT + t - 1)
                    act.wait_ge(s_mm, s * (U_ALL * NT) + 2 * t + 1)
                    act.copy(c[:, 0:RQ], bank(2 * t % 4)[:, 0:RQ]).then_inc(s_eva, 1)
                    act.wait_ge(s_mm, s * (U_ALL * NT) + 2 * t + 2)
                    act.copy(c[:, RQ:RC + ROT], bank((2 * t + 1) % 4)[:, 0:KV_COLS]).then_inc(s_eva, 1)
                    act.wait_ge(s_eva, s * (U_C * NT) + 2 * t + 2)
                    squares(c[:, 0:RQ], RQ, junk, 16 + 2 * t, s_css)
                    squares(c[:, RQ:RC], RKV, junk, 17 + 2 * t, s_css, RQ)
                    act.wait_ge(s_css, s * (2 * NT) + 2 * t + 2)
                    rms(16 + 2 * t, 1, RQ, s_cstd)
                    rms(17 + 2 * t, 1, RKV, s_cstd)
                    if t in (3, 5):
                        w_split(t // 2 + 1, wst[:], w_hi[t // 2 - 1][:])
                    for tc in ([t - 1] if t >= 1 else []) + ([t] if t == NT - 1 else []):
                        act.wait_ge(s_ctr, s * NT + tc + 1)
                        act.copy(ct_hi[:, :, tc * P:(tc + 1) * P],
                                 bank(6)[:, 0:3 * P].rearrange("p (k n) -> p k n", k=3)).then_inc(s_chi, 1)
                with act.Fori(0, U_QK // 2) as j:
                    for e in range(2):
                        act.wait_ge(s_mm, s * (U_ALL * NT) + j * (2 * NT) + (U_C + e + 1) * NT)
                        w_split(j * 2 + 4 + e, wst[:], w_hi[e][:])
                end(act)

                def attention(mixer, hi_q, hi_k, v2, ot, prob, st, scale, pt_hi, v_first, between):
                    n0 = s * (2 * HEADS) + mixer * HEADS

                    def prob_tile(e, n, t):
                        act.wait_ge(s_nm, n * 8 + t + 1)
                        act.activation(prob[t % 2][:], pair[t % 2][:], ACT.Exp, bias=nm[:, t % 4:t % 4 + 1],
                                       scale=scale, accum_out=den[:, e, t:t + 1]).then_inc(s_pr, 1)

                    def round_(r, m, e):
                        act.wait_ge(s_mi, m + 1)
                        (hi_q if r < 2 else hi_k)(e, r % 2)

                    def v_split(e, heads_staged):
                        act.wait_ge(s_st["v"], heads_staged * 16)
                        act.copy(v2[e][:, :, 0:HA], st["v"][:]).then_inc(s_vhi, 1)

                    def first_round(i, r):
                        act.wait_ge(s_mi, n0 * 8 + i + 1)
                        (hi_q if r < 2 else hi_k)(0, r % 2, bank(4 + i))

                    def evict(n, g):
                        act.wait_ge(s_pv, n * 4 + g + 1)
                        act.copy(ot[:], bank(6)[:, 0:2 * P]).then_inc(s_ot, 1)

                    def next_probs(e, n, t, left):
                        if t + 1 < NT:
                            prob_tile(e, n, t + 1)
                        elif left:
                            prob_tile(1 - e, n + 1, 0)

                    def step(n, t):
                        for hb in range(2):
                            act.wait_ge(s_pt, n * 16 + 2 * t + hb + 1)
                            act.copy(pt_hi[t // 2 % 2][:, 4 * hb:4 * hb + 4, t % 2 * P:(t % 2 + 1) * P],
                                     bank(4 + hb).rearrange("p (k n) -> p k n", k=4)).then_inc(s_pthi, 1)

                    def body(e, n, left):
                        for off, t, use, a, m in steps(n, left):
                            if left or not off:
                                next_probs((e + off) % 2, n + off, t, left - off)
                            if use == "osum":
                                evict(n, a)
                            if left or not off:
                                step(n + off, t)
                            if use == "round":
                                round_(a, m, 1 - e if a == 3 else e)
                            if off and t == 2 and left > 1:
                                v_split(e, n + 3)

                    for i, r in enumerate(HEAD0):
                        first_round(i, r)
                    act.copy(v2[0][:, :, 0:HA], v_first).then_inc(s_vhi, 1)
                    prob_tile(0, n0, 0)
                    for t in range(3):
                        prob_tile(0, n0, t + 1)
                        step(n0, t)
                        round_(t, n0 * 8 + 4 + t, 1)
                    v_split(1, n0 + 2)
                    with act.Fori(0, HEADS // 2 - 1) as j:
                        for e in range(2):
                            body(e, j * 2 + (n0 + e), 2)
                    body(0, n0 + (HEADS - 2), 1)
                    between()
                    body(1, n0 + (HEADS - 1), 0)

                def hi_of(dst, rows):
                    def go(e, half, src=bank(7)):
                        act.copy(dst[e][0:rows, half * 512:half * 512 + 512], src[0:rows, :]).then_inc(s_mihi, 1)
                    return go

                begin(act, s, 1)
                act.wait_ge(s_st["v"], s * (2 * HEADS * 16) + 16)

                def b_weights_hi():
                    act.wait_ge(s_bw, (s * 2 + 2) * 16)
                    act.copy(uq_hi[:], uq_st[:]).then_inc(s_bhi, 1)
                    act.copy(ukv_hi[:], ukv_st[:]).then_inc(s_bhi, 1)

                attention(0, hi_of(q2, P), hi_of(khh, P), v2_a, ot_a, pr_a, st_a, SCALE_A, pt_hi_a, st_a["v"][:],
                          b_weights_hi)
                end(act)

                begin(act, s, 2)
                for t in range(NT):
                    act.wait_ge(s_bmm, s * (2 * NT) + 2 * t + 1)
                    act.copy(qb[:, t, :].rearrange("p (h x) -> p h x", x=HB)[:, :, 0:HA],
                             pair[t % 2][:, 0:NUQ].rearrange("p (h x) -> p h x", x=HB)[:, :, 0:HA]).then_inc(s_bea, 1)
                    act.wait_ge(s_bmm, s * (2 * NT) + 2 * t + 2)
                    act.copy(kb[:, t, :].rearrange("p (h x) -> p h x", x=HB)[:, :, 0:HA],
                             pair[2 + t % 2][:].rearrange("p (h x) -> p h x", x=2 * HA)[:, :, 0:HA]).then_inc(s_bea, 1)
                end(act)

                begin(act, s, 3)
                attention(1, hi_of(qh, HB), hi_of(kh, HB), v2_b, ot_b, pr_b, st_b, SCALE_B, pt_hi_b, vb[:, :, 0:HA],
                          lambda: None)
                w_split(U_IN, wost[:], wo_hi[0][:])
                end(act)

                begin(act, s, 4)

                def o_stats(t):
                    act.activation(junk2[:, 0:WA], o[:, t, 0:WA], ACT.Square, accum_out=ss[:, 2 * t:2 * t + 1])
                    act.activation(junk2[:, WA:D], o[:, t, WA:D], ACT.Square, accum_out=ss[:, 2 * t + 1:2 * t + 2]).then_inc(s_ss, 1)
                    act.wait_ge(s_ss, xb + NT + t + 1)
                    rms(2 * t, 2, WA, s_std)

                o_stats(0)
                o_stats(1)
                for t in range(NT):
                    act_hi(t, pair[2 + t % 2], tb + NT + t, at2_hi)
                    if t + 2 < NT:
                        o_stats(t + 2)
                    if t == 3:
                        w_split(U_IN + 1, wost[:], wo_hi[1][:])
                for u in range(2, U_O):
                    act.wait_ge(s_mm, s * (U_ALL * NT) + (U_IN + u - 1) * NT)
                    w_split(U_IN + u, wost[:], wo_hi[u % 2][:])

                def split(u3, slot, dst):
                    act.wait_ge(s_ust[slot], (s * (2 * NCH) + u3) * 16)
                    act.copy(dst, ust[slot][:]).then_inc(s_uhi, 1)

                def split_up(b, c_next, u3, slot):
                    split(u3, slot, wu_hi[b][:].rearrange("p k n -> p (k n)"))

                for b in range(2):
                    split_up(b, 0, 1, b)

                def x1_stats(t, base):
                    squares(x1[:, t, :], D, junk2 if base == 2 * NT else junk3, 2 * t, s_ss)
                    act.wait_ge(s_ss, xb + base + t + 1)
                    rms(2 * t, 1, D, s_std)

                for t in range(NT):
                    act.wait_ge(s_evd, s * EV_SEQ + (U_ALL - U_C - 1) * NT + t + 1 + EV_CREDIT)
                    x1_stats(t, 2 * NT)
                    if t >= 2:
                        act_hi(t - 2, pair[2 + t % 2], tb + 2 * NT + t - 2, at2_hi)
                for t in range(NT - 2, NT):
                    act_hi(t, pair[2 + t % 2], tb + 2 * NT + t, at2_hi)
                end(act)

                begin(act, s, 5)

                def conv(b, c):
                    K = (s * NCH + c) * 4 + b
                    act.wait_ge(s_up, K + 1)
                    act.wait_ge(s_cw[b], (s * NCH + c + 1) * 16)
                    dst = cg if b % 2 == 0 else cv
                    if b == 3:
                        act.wait_ge(s_hlo, (s * NCH + c) * 2 + (1 + ONE))
                    if b == 1:
                        act.wait_ge(s_hlo, (s * NCH + c) * 2 + ONE)
                    act.activation(dst[:], pair[b % 2][:], ACT.Identity, bias=cw[b][:, 3:4], scale=cw[b][:, 1:2]).then_inc(s_ci, 1)

                def silu(f, c):
                    act.wait_ge(s_cv, (s * NCH + c) * 4 + 2 * f + 1)
                    act.activation(cg[:], cg[:], ACT.Silu).then_inc(s_sg, 1)

                def hidden_hi(f, c):
                    act.wait_ge(s_h, (s * NCH + c) * 2 + f + 1)
                    act.copy(h_hi[f][:], cv[:]).then_inc(s_hhi, 1)

                def chunk(c, first, last):
                    def next_up(b, k):
                        if not last:
                            split_up(b, c + 1, c * 2 + (4 + k) // 3 + 1, (4 + k) % 3)
                    conv(0, c)
                    next_up(0, 0)
                    silu(0, c)
                    if not first:
                        act.wait_ge(s_dn, (s * NCH + c) * NT)
                    for f in range(2):
                        k = f if last else f + 1
                        split(c * 2 + (4 + k) // 3 + 1, (4 + k) % 3, wd_hi[f][:])
                    conv(1, c)
                    hidden_hi(0, c)
                    next_up(1, 3)
                    conv(2, c)
                    next_up(2, 4)
                    silu(1, c)
                    conv(3, c)
                    hidden_hi(1, c)
                    next_up(3, 5)

                for b in range(2, 4):
                    split_up(b, 0, b // 3 + 1, b % 3)
                chunk(0, True, False)
                with act.Fori(1, NCH - 1) as c:
                    chunk(c, False, False)
                chunk(NCH - 1, False, True)
                for t in range(NT):
                    act.wait_ge(s_ya, (s * NCH + NCH - 1) * NT + t + 1 + YA_CREDIT)
                    x1_stats(t, 3 * NT)
                end(act)

        @block.vector
        def _(dve):
            def normalise(dst, src, gain, col, idx, halves=1):
                dve.wait_ge(s_std, idx + 1)
                dve.reciprocal(rs[:, col:col + halves], sd[:, col:col + halves]).then_inc(s_rs, 1)
                dve.wait_ge(s_rs, idx + 1)
                w = D // halves
                for i in range(halves):
                    c = slice(i * w, (i + 1) * w)
                    op = dve.scalar_tensor_tensor(dst[:, c], src[:, c], rs[:, col + i:col + i + 1], gain[:, c], ALU.mult, ALU.mult)
                op.then_inc(s_xn, 1)

            def act_lo(t, src, idx, at_hi, at_lo):
                dve.wait_ge(s_ahi, idx + 1)
                tok = slice(t * P, (t + 1) * P)
                dve.tensor_tensor(at_lo[:, :, tok], src[:].rearrange("p (k n) -> p k n", k=NK),
                                  at_hi[:, :, tok].bitcast(F32), ALU.subtract).then_inc(s_alo, 1)

            def rotate(dst, src, cos, sin, heads, width, ta, tb_, idx, done):
                h = width // 2
                bc = lambda a, n: a.unsqueeze(1).to_broadcast([P, heads, n])
                dve.tensor_tensor(ta, src, bc(cos, width), ALU.mult)
                dve.tensor_tensor(tb_[:, :, 0:h], src[:, :, h:width], bc(sin[:, 0:h], h), ALU.mult)
                dve.tensor_tensor(tb_[:, :, h:width], src[:, :, 0:h], bc(sin[:, h:width], h), ALU.mult).then_inc(s_rot, 1)
                dve.wait_ge(s_rot, idx + 1)
                dve.tensor_tensor(dst, ta, tb_, ALU.add).then_inc(done, 1)

            dve.memset(eps[:], EPS).then_inc(s_eps, 1)
            for s_free, n in ((s_ptlo, LO_CREDIT), (s_evd, EV_CREDIT), (s_ya, YA_CREDIT), (s_mid, ONE), (s_ot, ONE),
                              (s_hlo, ONE), (s_phase, ONE)):
                for _ in range(n):
                    dve.sem_inc(s_free, 1)
            dve.wait_ge(s_const, 16 * 4)
            with dve.Fori(0, N_SEQ) as s:
                begin(dve, s, 0)
                xb = s * (4 * NT)
                tb = s * (3 * NT)

                def w_split(u, src, hi, lo):
                    dve.wait_ge(s_whi, s * U_ALL + u + 1)
                    dve.tensor_tensor(lo, src, hi.bitcast(F32), ALU.subtract).then_inc(s_wlo, 1)

                def xnorm(t):
                    normalise(xt[t % 2][:], xt[t % 2][:], gin[:], 2 * t, xb + t)

                dve.wait_ge(s_gin, (s + 1) * 16)
                xnorm(0)
                xnorm(1)
                w_split(0, wst[:], wc_hi[0][:], wc_lo[0][:])
                act_lo(0, pair[2], tb, at_hi, at_lo)
                w_split(1, wst[:, :, 0:KV_COLS], wc_hi[1][:], wc_lo[1][:])
                dve.wait_ge(s_inw, (s + 1) * 64)
                for t in range(NT):
                    if t + 1 < NT:
                        act_lo(t + 1, pair[2], tb + t + 1, at_hi, at_lo)
                    if t + 2 < NT:
                        xnorm(t + 2)
                    c = cr[t % 2]
                    q0 = 16 + 2 * t
                    dve.wait_ge(s_cstd, s * (2 * NT) + 2 * t + 2)
                    dve.reciprocal(rs[:, q0:q0 + 2], sd[:, q0:q0 + 2]).then_inc(s_crs, 1)
                    dve.wait_ge(s_crs, s * NT + t + 1)
                    dve.scalar_tensor_tensor(c[:, 0:RQ], c[:, 0:RQ], rs[:, q0:q0 + 1], glora[:, 0:RQ], ALU.mult, ALU.mult)
                    dve.scalar_tensor_tensor(c[:, RQ:RC], c[:, RQ:RC], rs[:, q0 + 1:q0 + 2], glora[:, RQ:RC], ALU.mult, ALU.mult)
                    rotate(krot[:, t, :].unsqueeze(1), c[:, RC:RC + ROT].unsqueeze(1), cosb[:, t, :], sinb[:, t, :], 1, ROT,
                           pra[t % 2][:, 0:ROT].unsqueeze(1), prb[t % 2][:, 0:ROT].unsqueeze(1), s * ROT_SEQ + t, s_cn)
                    if t in (3, 5):
                        w_split(t // 2 + 1, wst[:], w_hi[t // 2 - 1][:], w_lo[t // 2 - 1][:])
                    for tc in ([t - 1] if t >= 1 else []) + ([t] if t == NT - 1 else []):
                        dve.wait_ge(s_chi, s * NT + tc + 1)
                        tok = slice(tc * P, (tc + 1) * P)
                        dve.tensor_tensor(ct_lo[:, :, tok], bank(6)[:, 0:3 * P].rearrange("p (k n) -> p k n", k=3),
                                          ct_hi[:, :, tok].bitcast(F32), ALU.subtract).then_inc(s_clo, 1)
                heads4 = lambda a: a.rearrange("p (h x) -> p h x", x=HA)
                with dve.Fori(0, U_QK // 2) as j:
                    for e in range(2):
                        for t in range(NT):
                            dve.wait_ge(s_mm, s * (U_ALL * NT) + j * (2 * NT) + (U_C + e) * NT + t + 1)
                            rotate(heads4(qk[:, t, bass.ds(j * (2 * COL) + e * COL, COL)]), heads4(bank(t % 4)[:, 0:COL]),
                                   cosa[:, t, :], sina[:, t, :], COL // HA, HA, heads4(pra[t % 2][:]), heads4(prb[t % 2][:]),
                                   s * ROT_SEQ + j * (2 * NT) + (e + 1) * NT + t, s_evd)
                        w_split(j * 2 + 4 + e, wst[:], w_hi[e][:], w_lo[e][:])
                for u in range(U_V):
                    for t in range(NT):
                        dve.wait_ge(s_mm, s * (U_ALL * NT) + (U_C + U_QK + u) * NT + t + 1)
                        dve.tensor_copy(va[:, t, u * COL:(u + 1) * COL], bank(t % 4)[:, 0:COL]).then_inc(s_evd, 1)
                end(dve)

                def attention(mixer, lo_q, lo_k, v2, st, scale, pt_hi, pt_lo, v_first, between):
                    n0 = s * (2 * HEADS) + mixer * HEADS

                    def row_max(t, idx):
                        m, n = mx[:, t % 4:t % 4 + 1], nm[:, t % 4:t % 4 + 1]
                        sc = pair[t % 2][:]
                        if mixer == 0:
                            await_(dve, s_sc, idx + 1)
                            u0 = (NT - 1 - t) * P
                            dve.tensor_tensor_reduce(sc, sc, logc[:, u0:u0 + S], 1.0, -3e38, ALU.add, ALU.max, m).then_inc(s_max, 1)
                        else:
                            dve.wait_ge(s_sc, idx + 1)
                            dve.tensor_reduce(m, sc, AXX, ALU.max).then_inc(s_max, 1)
                        dve.wait_ge(s_max, idx + 1)
                        dve.tensor_scalar(n, m, -scale, None, ALU.mult).then_inc(s_nm, 1)

                    def round_(r, e, idx):
                        dve.wait_ge(s_mihi, idx + 1)
                        (lo_q if r < 2 else lo_k)(e, r % 2)

                    def v_split(e, idx):
                        dve.wait_ge(s_vhi, idx + 1)
                        dve.tensor_tensor(v2[e][:, :, HA:P], st["v"][:], v2[e][:, :, 0:HA].bitcast(F32), ALU.subtract).then_inc(s_vlo, 1)

                    def sums(e, g):
                        dve.reciprocal(rden[:, g % 2 * 2:g % 2 * 2 + 2], den[:, e, 2 * g:2 * g + 2]).then_inc(s_rden, 1)

                    def osum(e, n, g, col, m):
                        r2 = slice(g % 2 * 2, g % 2 * 2 + 2)
                        dve.wait_ge(s_mi, m + 1)
                        dve.wait_ge(s_rden, n * 4 + g + 1)
                        dve.tensor_tensor(o[:, 2 * g:2 * g + 2, bass.ds(col, HA)],
                                          bank(7)[:, 0:2 * HA].rearrange("p (i x) -> p i x", i=2),
                                          rden[:, r2].unsqueeze(2).to_broadcast([P, 2, HA]), ALU.mult).then_inc(s_mid, 1)

                    def step(n, t):
                        for hb in range(2):
                            dve.wait_ge(s_pthi, n * 16 + 2 * t + hb + 1)
                            dst = (slice(None), slice(4 * hb, 4 * hb + 4), slice(t % 2 * P, (t % 2 + 1) * P))
                            dve.tensor_tensor(pt_lo[t // 2 % 2][dst], bank(4 + hb).rearrange("p (k n) -> p k n", k=4),
                                              pt_hi[t // 2 % 2][dst].bitcast(F32), ALU.subtract).then_inc(s_ptlo, 1)

                    def body(e, n, col, left):
                        for off, t, use, a, m in steps(n, left):
                            if use == "osum":
                                sums(e, a)
                            if left or not off:
                                step(n + off, t)
                                if t + 3 < NT or left - off:
                                    row_max((t + 3) % NT, (n + off) * 8 + t + 3)
                            if use == "round":
                                round_(a, 1 - e if a == 3 else e, n * 4 + (7 if a == 3 else 8 + a))
                            if use == "osum":
                                osum(e, n, a, col, m)
                            if off and t == 2 and left > 1:
                                v_split(e, n + 2)

                    def first_round(i, r):
                        dve.wait_ge(s_mihi, n0 * 4 + i + 1)
                        (lo_q if r < 2 else lo_k)(0, r % 2, bank(4 + i))

                    for i, r in enumerate(HEAD0[:3]):
                        first_round(i, r)
                    row_max(0, n0 * 8)
                    first_round(3, HEAD0[3])
                    row_max(1, n0 * 8 + 1)
                    dve.wait_ge(s_vhi, n0 + 1)
                    dve.tensor_tensor(v2[0][:, :, HA:P], v_first, v2[0][:, :, 0:HA].bitcast(F32), ALU.subtract).then_inc(s_vlo, 1)
                    row_max(2, n0 * 8 + 2)
                    for t in range(3):
                        step(n0, t)
                        row_max(t + 3, n0 * 8 + t + 3)
                        round_(t, 1, n0 * 4 + 4 + t)
                    v_split(1, n0 + 1)
                    with dve.Fori(0, HEADS // 2 - 1) as j:
                        for e in range(2):
                            body(e, j * 2 + (n0 + e), j * (2 * HA) + (mixer * WA + e * HA), 2)
                    body(0, n0 + (HEADS - 2), mixer * WA + (HEADS - 2) * HA, 1)
                    between()
                    body(1, n0 + (HEADS - 1), mixer * WA + (HEADS - 1) * HA, 0)

                def lo_of(dst, hi, r0, r1):
                    def go(e, half, src=bank(7)):
                        c = slice(half * 512, half * 512 + 512)
                        dve.tensor_tensor(dst[e][r0:r1, c], src[r0:r1, :], hi[e][r0:r1, c].bitcast(F32),
                                          ALU.subtract).then_inc(s_mid, 1)
                    return go

                begin(dve, s, 1)
                dve.wait_ge(s_logc, (s + 1) * 16)

                def b_weights_lo():
                    dve.wait_ge(s_bhi, s * 2 + 1)
                    dve.tensor_tensor(uq_lo[:], uq_st[:], uq_hi[:].bitcast(F32), ALU.subtract).then_inc(s_blo, 1)
                    dve.wait_ge(s_bhi, s * 2 + 2)
                    dve.tensor_tensor(ukv_lo[:], ukv_st[:], ukv_hi[:].bitcast(F32), ALU.subtract).then_inc(s_blo, 1)

                attention(0, lo_of(q2, q2, HA, P), lo_of(kll, khh, 0, P), v2_a, st_a, SCALE_A, pt_hi_a, pt_lo_a,
                          st_a["v"][:], b_weights_lo)
                end(dve)

                begin(dve, s, 2)
                for t in range(NT):
                    by_head = lambda a, x: a.rearrange("p (h x) -> p h x", x=x)
                    dve.wait_ge(s_bea, s * (2 * NT) + 2 * t + 1)
                    rotate(by_head(qb[:, t, :], HB)[:, :, HA:HB], by_head(pair[t % 2][:, 0:NUQ], HB)[:, :, HA:HB],
                           cosb[:, t, :], sinb[:, t, :], HEADS, ROT, pba[t % 2][:], pbb[t % 2][:],
                           s * ROT_SEQ + (1 + U_QK) * NT + t, s_bed)
                    dve.tensor_copy(by_head(kb[:, t, :], HB)[:, :, HA:HB], krot[:, t, :].unsqueeze(1).to_broadcast([P, HEADS, ROT]))
                    dve.wait_ge(s_bea, s * (2 * NT) + 2 * t + 2)
                    dve.tensor_copy(by_head(vb[:, t, :], HA), by_head(pair[2 + t % 2][:], 2 * HA)[:, :, HA:2 * HA]).then_inc(s_bed, 1)
                end(dve)

                begin(dve, s, 3)
                attention(1, lo_of(ql, qh, 0, HB), lo_of(kl, kh, 0, HB), v2_b, st_b, SCALE_B, pt_hi_b, pt_lo_b,
                          vb[:, :, 0:HA], lambda: None)
                w_split(U_IN, wost[:], wo_hi[0][:], wo_lo[0][:])
                end(dve)

                begin(dve, s, 4)

                def onorm(t):
                    if t >= 2:
                        dve.wait_ge(s_tr, tb + NT + t - 1)
                    normalise(xn[t % 2], o[:, t, :], gout, 2 * t, xb + NT + t, halves=2)

                def add_unit(u, t):
                    if u == 0:
                        dve.wait_ge(s_x1[t % 3], (s * len(range(t % 3, NT, 3)) + t // 3 + 1) * 16)
                    dve.wait_ge(s_mm, s * (U_ALL * NT) + (U_IN + u) * NT + t + 1)
                    col = slice(u * COL, (u + 1) * COL)
                    dve.tensor_tensor(x1[:, t, col], bank(t % 4)[:, 0:COL], x1[:, t, col], ALU.add).then_inc(s_evd, 1)

                def split(u, slot, hi, lo):
                    dve.wait_ge(s_uhi, s * (6 * NCH) + u + 1)
                    dve.tensor_tensor(lo, ust[slot][:], hi.bitcast(F32), ALU.subtract).then_inc(s_ulo, 1)

                def split_up(b, u, slot):
                    split(u, slot, wu_hi[b][:].rearrange("p k n -> p (k n)"), wu_lo[b][:].rearrange("p k n -> p (k n)"))

                dve.wait_ge(s_og, (s + 1) * 16)
                onorm(0)
                onorm(1)
                for t in range(NT):
                    act_lo(t, pair[2 + t % 2], tb + NT + t, at2_hi, at2_lo)
                    if t + 2 < NT:
                        onorm(t + 2)
                    if t >= 1:
                        add_unit(0, t - 1)
                    if t == 3:
                        w_split(U_IN + 1, wost[:], wo_hi[1][:], wo_lo[1][:])
                add_unit(0, NT - 1)
                w_split(U_IN + 2, wost[:], wo_hi[0][:], wo_lo[0][:])

                def xnorm2(t):
                    dve.wait_ge(s_tr, tb + (2 * NT + t - 1 if t >= 2 else 2 * NT))
                    normalise(xn[t % 2], x1[:, t, :], gffn, 2 * t, xb + 2 * NT + t)

                for t in range(NT):
                    add_unit(1, t)
                w_split(U_IN + 3, wost[:], wo_hi[1][:], wo_lo[1][:])
                for b in range(2):
                    split_up(b, b, b)
                for t in range(NT):
                    add_unit(2, t)
                dve.wait_ge(s_gf2, (s + 1) * 16)
                for t in range(NT):
                    add_unit(3, t)
                    if t >= 2:
                        act_lo(t - 2, pair[2 + t % 2], tb + 2 * NT + t - 2, at2_hi, at2_lo)
                    xnorm2(t)
                for t in range(NT - 2, NT):
                    act_lo(t, pair[2 + t % 2], tb + 2 * NT + t, at2_hi, at2_lo)
                end(dve)

                begin(dve, s, 5)

                def conv(b, c):
                    K = (s * NCH + c) * 4 + b
                    buf, u = (cg if b % 2 == 0 else cv), pair[b % 2]
                    dve.wait_ge(s_ci, K + 1)
                    dve.scalar_tensor_tensor(buf[:, 1:S], u[:, 0:S - 1], cw[b][:, 0:1], buf[:, 1:S], ALU.mult, ALU.add).then_inc(s_c0, 1)
                    dve.wait_ge(s_c0, K + 1)
                    dve.scalar_tensor_tensor(buf[:, 0:S - 1], u[:, 1:S], cw[b][:, 2:3], buf[:, 0:S - 1], ALU.mult, ALU.add).then_inc(s_cv, 1)

                def hidden(f, c):
                    i = (s * NCH + c) * 2 + f
                    dve.wait_ge(s_sg, i + 1)
                    dve.wait_ge(s_cv, (s * NCH + c) * 4 + 2 * f + 2)
                    dve.tensor_tensor(cv[:], cg[:], cv[:], ALU.mult).then_inc(s_h, 1)
                    dve.wait_ge(s_hhi, i + 1)
                    dve.tensor_tensor(h_lo[f][:], cv[:], h_hi[f][:].bitcast(F32), ALU.subtract).then_inc(s_hlo, 1)

                def add_down(t, c):
                    dve.wait_ge(s_dn, (s * NCH + c) * NT + t + 1)
                    dve.tensor_tensor(x1[:, t, :], pair[2 + t % 2][:], x1[:, t, :], ALU.add).then_inc(s_ya, 1)

                def chunk(c, first, last):
                    def next_up(b, k):
                        if not last:
                            split_up(b, c * 6 + 4 + k, (4 + k) % 3)
                    conv(0, c)
                    for t in range(NT):
                        if not first:
                            add_down(t, c - 1)
                        if t == 2:
                            next_up(0, 0)
                    for f in range(2):
                        k = f if last else f + 1
                        split(c * 6 + 4 + k, (4 + k) % 3, wd_hi[f][:], wd_lo[f][:])
                    conv(1, c)
                    hidden(0, c)
                    next_up(1, 3)
                    conv(2, c)
                    next_up(2, 4)
                    conv(3, c)
                    hidden(1, c)
                    next_up(3, 5)

                for b in range(2, 4):
                    split_up(b, b, b % 3)
                chunk(0, True, False)
                with dve.Fori(1, NCH - 1) as c:
                    chunk(c, False, False)
                chunk(NCH - 1, False, True)
                dve.wait_ge(s_gf, (s + 1) * 16)
                for t in range(NT):
                    add_down(t, NCH - 1)
                    if t >= 1:
                        normalise(x1[:, t - 1, :], x1[:, t - 1, :], gfin, 2 * (t - 1), xb + 3 * NT + t - 1)
                normalise(x1[:, NT - 1, :], x1[:, NT - 1, :], gfin, 2 * (NT - 1), xb + 4 * NT - 1)
                end(dve)


def tables():
    import numpy as np

    def rotary(width):
        half = width // 2
        inv = (np.float32(10000.0) ** (-np.arange(half, dtype=np.float32) * np.float32(2.0 / width))).astype(np.float32)
        ang = np.arange(S, dtype=np.float32)[:, None] * inv[None, :]
        cos, sin = np.cos(ang).astype(np.float32), np.sin(ang).astype(np.float32)
        per_tile = lambda a: np.ascontiguousarray(a.reshape(NT, P, width).transpose(1, 0, 2))
        return per_tile(np.concatenate([cos, cos], 1)), per_tile(np.concatenate([-sin, sin], 1))

    ca, sa = rotary(HA)
    cb, sb = rotary(ROT)
    d = np.arange(MASK_W)[None, :] - (S - P) - np.arange(P)[:, None]
    count = sum(((np.abs(d) <= window // 2) & (d % dil == 0)).astype(np.int64)
                for window, dil in ((128, 1), (512, 4), (2048, 16)))
    logc = np.where(count > 0, np.log(np.maximum(count, 1)) / SCALE_A, NEG_HUGE).astype(np.float32)
    eye = np.eye(P, dtype=np.float32)
    return dict(ident=eye, stack_ident=np.concatenate([np.eye(HA, dtype=np.float32)] * 2, 0),
                cos_a=ca, sin_a=sa, cos_b=cb, sin_b=sb, log_count=logc)


def kernel(x_prompt, x_sample, g_attn, w_in, g_q_lora, w_uq, g_kv_lora, w_ukv, g_out_a, g_out_b, w_o,
           g_ffn, w_up, w_conv, b_conv, w_down, g_final):
    import numpy as np
    import concourse.bacc as bacc
    from concourse.bass_utils import run_bass_kernel_spmd

    a = lambda v: np.ascontiguousarray(v)
    conv = np.concatenate([np.asarray(w_conv)[0], np.asarray(b_conv)], 0).reshape(4, 2, NCH, 2, P)
    conv = conv.transpose(4, 2, 3, 1, 0).reshape(P, NCH * 16)
    arrays = dict(
        x_seqs=np.concatenate([np.asarray(x_prompt).reshape(S, D), np.asarray(x_sample).reshape(S, D)], 0),
        g_attn=np.asarray(g_attn)[0], w_in=np.asarray(w_in)[0], g_q=np.asarray(g_q_lora)[0],
        w_uq=np.asarray(w_uq)[0], g_kv=np.asarray(g_kv_lora)[0], w_ukv=np.asarray(w_ukv)[0],
        g_out=np.concatenate([np.asarray(g_out_a)[0], np.asarray(g_out_b)[0]], 0),
        w_o=np.asarray(w_o)[0], g_ffn=np.asarray(g_ffn)[0], w_up=np.asarray(w_up)[0], conv_wb=conv,
        w_down=np.asarray(w_down)[0], g_final=np.asarray(g_final), **tables())
    nc = bacc.Bacc("TRN2", target_bir_lowering=False, num_devices=1)
    args = {}
    for name, v in arrays.items():
        arrays[name] = v = a(v)
        args[name] = nc.dram_tensor(f"in_{name}", v.shape, mybir.dt.from_np(v.dtype), kind="ExternalInput").ap()
    args["out"] = nc.dram_tensor("out_y", (N_SEQ * S, D), F32, kind="ExternalOutput").ap()
    encoder_kernel(nc, **args)
    r = run_bass_kernel_spmd(nc, [{f"in_{k}": v for k, v in arrays.items()}], core_ids=[0])
    y = r.results[0]["out_y"]
    return y[0:S].reshape(np.asarray(x_prompt).shape), y[S:].reshape(np.asarray(x_sample).shape)
```

```python
from contextlib import ExitStack

import concourse.bass as bass
from concourse import mybir

ALU = mybir.AluOpType
ACT = mybir.ActivationFunctionType
AXX = mybir.AxisListType.X
F32 = mybir.dt.float32
F32R = mybir.dt.float32r
BF16 = mybir.dt.bfloat16

P = 128
N_SEQ = 2
S = 1024
D = 1024
NT = S // P
NK = D // P
HEADS = 8
HA = 64
ROT = 32
HB = HA + ROT
WA = HEADS * HA
RQ, RKV = 256, 128
RC = RQ + RKV
F = 2816
NCH = F // (2 * P)
COL = 256
EPS = 1e-6
NEG_HUGE = -1e30
MASK_W = 2 * S - P
SCALE_A = float(HA) ** -0.5
SCALE_B = float(HB) ** -0.5

U_C, U_QK, U_V = 2, 4, 2
U_IN = U_C + U_QK + U_V
U_O = D // COL
U_ALL = U_IN + U_O
KV_COLS = RKV + ROT
EV_SEQ = (U_ALL - U_C) * NT
ROT_SEQ = (2 + U_QK) * NT

PHASES = 6
ENGINES = 4

LO_CREDIT = 2
EV_CREDIT = 4
YA_CREDIT = 2
ONE = 1


def encoder_kernel(nc: bass.Bass, x_seqs, g_attn, w_in, g_q, w_uq, g_kv, w_ukv, g_out, w_o, g_ffn,
                   w_up, conv_wb, w_down, g_final, ident, stack_ident, cos_a, sin_a, cos_b, sin_b,
                   log_count, out):
    with ExitStack() as ctx:
        used = set()

        def place(name, shape, dt, offset_kb):
            return nc.alloc_sbuf_tensor_at(name, shape, dt, offset=BASE + int(offset_kb * 1024))

        def sem(name):
            return ctx.enter_context(nc.semaphore(name))

        BASE = 16512
        R_O, R_C, R_Q, R_X, R_REST = 3.5, 35.5, 67.5, 131.5, 195.5
        idn = place("idn", [P, P], F32, 0)
        stk = place("stk", [P, HA], F32, 0.5)
        cosb = place("cosb", [P, NT, ROT], F32, 0.75)
        sinb = place("sinb", [P, NT, ROT], F32, 1.75)
        ss = place("ss", [P, 32], F32, 2.75)
        sd = place("sd", [P, 32], F32, 2.875)
        rs = place("rs", [P, 32], F32, 3.0)
        mx = place("mx", [P, 4], F32, 3.125)
        nm = place("nm", [P, 4], F32, 3.15625)
        den = place("den", [P, 2, NT], F32, 3.1875)
        rden = place("rden", [P, 4], F32, 3.25)
        eps = place("eps", [P, 1], F32, 3.28125)
        warm = place("warm", [P, 1], F32, 3.4375)
        cw = [place(f"cw{b}", [P, 4], F32, 3.3125 + b / 32) for b in range(4)]

        wc_hi = [place(f"wc_hi{i}", [P, NK, COL if i == 0 else KV_COLS], F32R, R_Q + 16 * i) for i in range(2)]
        wc_lo = [place(f"wc_lo{i}", [P, NK, COL if i == 0 else KV_COLS], F32R, R_Q + 8 + 16 * i) for i in range(2)]
        w_hi = [place(f"w_hi{i}", [P, NK, COL], F32R, R_O + 16 * i) for i in range(2)]
        w_lo = [place(f"w_lo{i}", [P, NK, COL], F32R, R_O + 16 * i + 8) for i in range(2)]
        ct_hi = place("ct_hi", [P, 3, S], F32R, R_C)
        ct_lo = place("ct_lo", [P, 3, S], F32R, R_C + 12)
        krot = place("krot", [P, NT, ROT], F32, R_C + 24)
        glora = place("glora", [P, RC], F32, R_C + 25)
        cr = [place(f"cr{i}", [P, RC + ROT], F32, R_C + 26.5 + 1.625 * i) for i in range(2)]
        junk = place("junk", [P, D], BF16, R_Q + 46)
        qk = place("qk", [P, NT, 2 * WA], F32, R_Q)
        va = place("va", [P, NT, WA], F32, R_Q + 32)
        wst = place("wst", [P, NK, COL], F32, R_Q + 48)
        xt = [place(f"xt{i}", [P, D], F32, R_REST + 4 * i) for i in range(2)]
        at_hi = place("at_hi", [P, NK, S], F32R, R_X)
        at_lo = place("at_lo", [P, NK, S], F32R, R_X + 32)
        gin = place("gin", [P, D], F32, R_REST + 8)
        cosa = place("cosa", [P, NT, HA], F32, R_Q + 56)
        sina = place("sina", [P, NT, HA], F32, R_Q + 58)
        pra = [place(f"pra{i}", [P, COL], F32, R_Q + 60 + 2 * i) for i in range(2)]
        prb = [place(f"prb{i}", [P, COL], F32, R_Q + 61 + 2 * i) for i in range(2)]

        o = place("o", [P, NT, D], F32, R_O)
        pt_hi_a = [place(f"pt_hi_a{i}", [P, NT, 2 * P], F32R, R_X + 16 * i) for i in range(2)]
        pt_lo_a = [place(f"pt_lo_a{i}", [P, NT, 2 * P], F32R, R_X + 16 * i + 8) for i in range(2)]
        pt_hi_b = [place(f"pt_hi_b{i}", [P, NT, 2 * P], F32R, R_Q + 16 * i) for i in range(2)]
        pt_lo_b = [place(f"pt_lo_b{i}", [P, NT, 2 * P], F32R, R_Q + 16 * i + 8) for i in range(2)]
        q2 = [place(f"q2{i}", [P, S], F32R, R_X + 32 + 12 * i) for i in range(2)]
        khh = [place(f"khh{i}", [P, S], F32R, R_X + 36 + 12 * i) for i in range(2)]
        kll = [place(f"kll{i}", [P, S], F32R, R_X + 40 + 12 * i) for i in range(2)]
        logc = place("logc", [P, MASK_W], F32, R_Q + 56)
        st_a = dict(q=place("stqa", [P, NT, P], F32, R_REST), k=place("stka", [P, NT, P], F32, R_REST + 4),
                    v=place("stva", [P, NT, HA], F32, R_C + 29.75))
        ot_a = place("ot_a", [P, 2 * P], F32, R_C + 25)
        v2_a = [place(f"v2a{i}", [P, NT, P], F32R, R_Q + 48 + 4 * i) for i in range(2)]
        pr_a = [place(f"pr_a{i}", [P, S], F32, R_X + 56 + 4 * i) for i in range(2)]
        qh = [place(f"qh{i}", [P, S], F32R, R_Q + 32 + 16 * i) for i in range(2)]
        ql = [place(f"ql{i}", [P, S], F32R, R_Q + 36 + 16 * i) for i in range(2)]
        kh = [place(f"kh{i}", [P, S], F32R, R_Q + 40 + 16 * i) for i in range(2)]
        kl = [place(f"kl{i}", [P, S], F32R, R_Q + 44 + 16 * i) for i in range(2)]
        st_b = dict(q=place("stqb", [P, NT, HB], F32, R_REST), k=place("stkb", [P, NT, HB], F32, R_REST + 3),
                    v=place("stvb", [P, NT, HA], F32, R_REST + 6))
        ot_b = place("ot_b", [P, 2 * P], F32, R_C + 15)
        v2_b = [place(f"v2b{i}", [P, NT, P], F32R, R_C + 16 + 4 * i) for i in range(2)]
        pr_b = [place(f"pr_b{i}", [P, S], F32, R_C + 24 + 4 * i) for i in range(2)]

        qb = place("qb", [P, NT, HEADS * HB], F32, R_X)
        kb = place("kb", [P, NT, HEADS * HB], F32, R_X + 24)
        vb = place("vb", [P, NT, WA], F32, R_X + 48)
        NUQ, NUKV = HEADS * HB, HEADS * 2 * HA
        uq_hi = place("uq_hi", [P, 2, NUQ], F32R, R_Q)
        uq_lo = place("uq_lo", [P, 2, NUQ], F32R, R_Q + 6)
        ukv_hi = place("ukv_hi", [P, NUKV], F32R, R_Q + 12)
        ukv_lo = place("ukv_lo", [P, NUKV], F32R, R_Q + 16)
        uq_st = place("uq_st", [P, 2, NUQ], F32, R_Q + 20)
        ukv_st = place("ukv_st", [P, NUKV], F32, R_Q + 26)
        pba = [place(f"pba{i}", [P, HEADS, ROT], F32, R_C + 26 + 2 * i) for i in range(2)]
        pbb = [place(f"pbb{i}", [P, HEADS, ROT], F32, R_C + 27 + 2 * i) for i in range(2)]

        x1 = place("x1", [P, NT, D], F32, R_C)
        at2_hi = place("at2_hi", [P, NK, S], F32R, R_Q)
        at2_lo = place("at2_lo", [P, NK, S], F32R, R_Q + 32)
        wo_hi = [place(f"wo_hi{i}", [P, NK, COL], F32R, R_X + 32 + 16 * i) for i in range(2)]
        wo_lo = [place(f"wo_lo{i}", [P, NK, COL], F32R, R_X + 40 + 16 * i) for i in range(2)]
        wost = place("wost", [P, NK, COL], F32, R_REST)
        gout = place("gout", [P, D], F32, R_REST + 8)
        xn = [place(f"xn{i}", [P, D], F32, R_X + 16 + 4 * i) for i in range(2)]
        gffn = place("gffn", [P, D], F32, R_X + 24)
        junk2 = place("junk2", [P, D], BF16, R_X + 28)

        wu_hi = [place(f"wu_hi{b}", [P, NK, P], F32R, R_X + 8 * b) for b in range(4)]
        wu_lo = [place(f"wu_lo{b}", [P, NK, P], F32R, R_X + 8 * b + 4) for b in range(4)]
        wd_hi = [place(f"wd_hi{f}", [P, D], F32R, R_X + 32 + 8 * f) for f in range(2)]
        wd_lo = [place(f"wd_lo{f}", [P, D], F32R, R_X + 36 + 8 * f) for f in range(2)]
        h_hi = [place(f"h_hi{f}", [P, S], F32R, R_X + 48 + 8 * f) for f in range(2)]
        h_lo = [place(f"h_lo{f}", [P, S], F32R, R_X + 52 + 8 * f) for f in range(2)]
        ust = [place(f"ust{i}", [P, D], F32, R_O + 4 * i) for i in range(3)]
        cg = place("cg", [P, S], F32, R_O + 12)
        cv = place("cv", [P, S], F32, R_O + 16)
        gfin = place("gfin", [P, D], F32, R_O + 20)
        junk3 = place("junk3", [P, D], BF16, R_O + 24)

        pair = [ctx.enter_context(nc.psum_tensor(f"pair{i}", [P, 2 * 512], F32)) for i in range(4)]

        def bank(i):
            return pair[i // 2][:, 512 * (i % 2):512 * (i % 2) + 512]

        s_phase, s_passed = sem("phase_ended"), sem("wait_passed")
        s_idn, s_const, s_eps = sem("identity_landed"), sem("constants_landed"), sem("eps_set")
        s_x = [sem(f"x_tile_landed{i}") for i in range(2)]
        s_inw, s_gin, s_wst, s_whi, s_wlo = sem("input_tables_landed"), sem("input_gain_landed"), sem("w_unit_landed"), sem("w_hi_split"), sem("w_lo_split")
        s_ss, s_std, s_rs, s_xn = sem("squares_summed"), sem("rms_ready"), sem("rrms_ready"), sem("tile_normalised")
        s_tr, s_ahi, s_alo = sem("tile_transposed"), sem("act_hi_split"), sem("act_lo_split")
        s_mm, s_eva, s_evd = sem("unit_product_ready"), sem("unit_evicted_by_act"), sem("unit_evicted_by_dve")
        s_css, s_cstd, s_crs, s_cn = sem("c_squares"), sem("c_rms"), sem("c_rrms"), sem("c_normalised")
        s_ctr, s_chi, s_clo, s_rot = sem("c_transposed"), sem("c_hi_split"), sem("c_lo_split"), sem("rotary_products")
        s_bw, s_bhi, s_blo = sem("b_weights_landed"), sem("b_weights_hi"), sem("b_weights_lo")
        s_bmm, s_bea, s_bed = sem("b_product_ready"), sem("b_evicted_by_act"), sem("b_evicted_by_dve")
        s_logc = sem("log_count_landed")
        s_st = {n: sem(f"head_{n}_staged") for n in "qkv"}
        s_sc, s_max, s_nm, s_pr = sem("scores_ready"), sem("row_max"), sem("minus_max_ready"), sem("probs_ready")
        s_pt, s_pthi, s_ptlo = sem("probs_transposed"), sem("pt_hi_split"), sem("pt_lo_split")
        s_pv, s_ot, s_rden = sem("pv_ready"), sem("ot_evicted"), sem("rden_ready")
        s_mi, s_mihi, s_mid = sem("misc_bank_filled"), sem("misc_hi_split"), sem("misc_bank_free")
        s_vhi, s_vlo = sem("v_hi_split"), sem("v_lo_split")
        s_x1 = [sem(f"residual_landed{i}") for i in range(NT)]
        s_og, s_gf2 = sem("output_gain_landed"), sem("mlp_gain_landed")
        s_ust = [sem(f"mlp_slot_landed{i}") for i in range(3)]
        s_cw = [sem(f"conv_taps_landed{b}") for b in range(4)]
        s_uhi, s_ulo = sem("mlp_w_hi_split"), sem("mlp_w_lo_split")
        s_up, s_ci, s_c0, s_cv = sem("up_ready"), sem("conv_middle"), sem("conv_left"), sem("conv_done")
        s_sg, s_h, s_hhi, s_hlo = sem("gate_silu"), sem("hidden_ready"), sem("hidden_hi"), sem("hidden_lo")
        s_dn, s_ya = sem("down_ready"), sem("down_added")
        s_uph, s_cih, s_th = sem("last_up_half_ready"), sem("conv_half_middle"), sem("conv_half_step")
        s_hp, s_hhip, s_hlop = sem("hidden_part_ready"), sem("hidden_part_hi"), sem("hidden_part_lo")
        s_warm, s_whp = sem("table_loaded"), sem("w_hi_half_split")
        s_gf, s_out = sem("final_gain_landed"), sem("output_written")

        block = ctx.enter_context(nc.Block())

        def await_(eng, semaphore, value):
            eng.wait_ge(semaphore, value)
            eng.sem_inc(s_passed, 1)


        def end(eng):
            eng.drain().then_inc(s_phase, 1)

        BODY = [(0, 3, "round", 3), (0, 4, "osum", 0), (0, 5, "round", 0), (0, 6, "osum", 1),
                (0, 7, "round", 1), (1, 0, "osum", 2), (1, 1, "round", 2), (1, 2, "osum", 3)]
        FIRST = 7

        PART = 3 * P
        H = S // 2

        HEAD0 = (0, 2, 3, 1)

        def steps(n, left):
            m = n * 8 + (FIRST if left else FIRST - 3)
            for off, t, use, a in BODY:
                here = left >= (1 if a == 3 else 2) if use == "round" else True
                if here or left or not off:
                    yield off, t, use if here else None, a, m
                if here:
                    m = m + 1

        @block.sync
        def _(sp):
            def begin(s, ph):
                await_(sp, s_phase, s * (PHASES * ENGINES) + (ph * ENGINES + ONE))

            w_in_v = w_in.rearrange("(k p) n -> p k n", p=P)
            w_o_v = w_o.rearrange("(k p) n -> p k n", p=P)
            w_up_v = w_up.rearrange("(k p) n -> p k n", p=P)
            x_v = x_seqs.rearrange("(t p) n -> t p n", p=P)
            out_v = out.rearrange("(t p) n -> t p n", p=P)

            def stage(h, src, dst, width, n):
                if n == "v":
                    sp.dma_start(dst[n][:], src[:, :, bass.ds(h * width, width)]).then_inc(s_st[n], 16)
                    return
                for i in range(2):
                    if width == HA:
                        to, t = dst[n][:, :, i * HA:(i + 1) * HA], slice(0, NT)
                    else:
                        t = slice(i * NT // 2, (i + 1) * NT // 2)
                        to = dst[n][:, t, :]
                    sp.dma_start(to, src[:, t, bass.ds(h * width, width)]).then_inc(s_st[n], 16)

            def load_first(row):
                sp.dma_start(xt[0][:], x_v[row]).then_inc(s_x[0], 16)
                sp.dma_start(gin[:], g_attn.partition_broadcast(P)).then_inc(s_gin, 16)

            def load_input_weights(row):
                sp.dma_start(wst[:], w_in_v[:, :, 3 * WA:3 * WA + RQ]).then_inc(s_wst, 16)
                sp.dma_start(xt[1][:], x_v[row + 1]).then_inc(s_x[1], 16)
                sp.dma_start(cosa[:], cos_a).then_inc(s_inw, 16)
                sp.dma_start(sina[:], sin_a).then_inc(s_inw, 16)

            load_first(0)
            sp.dma_start(idn[:], ident).then_inc(s_idn, 16)
            load_input_weights(0)
            sp.dma_start(stk[:], stack_ident).then_inc(s_const, 16)
            sp.dma_start(cosb[:], cos_b).then_inc(s_const, 16)
            sp.dma_start(sinb[:], sin_b).then_inc(s_const, 16)

            with sp.Fori(0, N_SEQ) as s:
                await_(sp, s_out, s * (16 * NT) + ONE)
                sp.dma_start(glora[:, 0:RQ], g_q.partition_broadcast(P)).then_inc(s_inw, 16)
                sp.dma_start(glora[:, RQ:RC], g_kv.partition_broadcast(P)).then_inc(s_inw, 16)
                for t in range(2, NT):
                    await_(sp, s_tr, s * (3 * NT) + t - 1)
                    sp.dma_start(xt[t % 2][:], x_v[s * NT + t]).then_inc(s_x[t % 2], 16)
                    if t in (2, 4, 7):
                        u = t // 2
                        await_(sp, s_wlo, s * U_ALL + u)
                        if u == 1:
                            sp.dma_start(wst[:, :, 0:KV_COLS], w_in_v[:, :, 3 * WA + RQ:3 * WA + RC + ROT]).then_inc(s_wst, 16)
                        else:
                            sp.dma_start(wst[:], w_in_v[:, :, (u - 2) * COL:(u - 1) * COL]).then_inc(s_wst, 16)
                with sp.Fori(2, U_QK + U_V) as j:
                    await_(sp, s_wlo, s * U_ALL + j + U_C)
                    sp.dma_start(wst[:], w_in_v[:, :, bass.ds(j * COL, COL)]).then_inc(s_wst, 16)
                for i, n in enumerate("qkv"):
                    await_(sp, s_evd, s * EV_SEQ + (2 * (i + 1) if i < 2 else 2 * i + 1) * NT + EV_CREDIT)
                    if n == "v":
                        sp.dma_start(logc[:], log_count).then_inc(s_logc, 16)
                    stage(0, va if n == "v" else qk[:, :, i * WA:(i + 1) * WA], st_a, HA, n)
                end(sp)

                def attention(mixer, src_q, src_k, src_v, dst, width):
                    n0 = s * (2 * HEADS) + mixer * HEADS
                    srcs = dict(q=(src_q, width), k=(src_k, width), v=(src_v, HA))
                    if mixer == 0:
                        await_(sp, s_mi, n0 * 8 + 4)
                    for n in "qk":
                        stage(1, srcs[n][0], dst, srcs[n][1], n)
                    if mixer == 0:
                        await_(sp, s_vlo, n0 + 1)
                    stage(1, srcs["v"][0], dst, srcs["v"][1], "v")
                    with sp.Fori(0, HEADS - 2) as h:
                        n = n0 + h
                        await_(sp, s_mi, n * 8 + (FIRST - 1))
                        stage(h + 2, srcs["q"][0], dst, srcs["q"][1], "q")
                        await_(sp, s_vlo, n + 2)
                        stage(h + 2, srcs["v"][0], dst, srcs["v"][1], "v")
                        await_(sp, s_mi, n * 8 + (FIRST + 1))
                        stage(h + 2, srcs["k"][0], dst, srcs["k"][1], "k")

                def heads_landed(mixer):
                    for n, k in (("q", 32), ("k", 32), ("v", 16)):
                        await_(sp, s_st[n], (s * (2 * HEADS) + (mixer + 1) * HEADS) * k)

                begin(s, 1)
                attention(0, qk, qk[:, :, WA:2 * WA], va, st_a, HA)
                heads_landed(0)
                sp.dma_start(uq_st[:], w_uq.rearrange("(k p) n -> p k n", p=P)).then_inc(s_bw, 16)
                sp.dma_start(ukv_st[:], w_ukv).then_inc(s_bw, 16)
                end(sp)

                begin(s, 2)
                end(sp)

                begin(s, 3)
                for n, k in (("q", 32), ("k", 32), ("v", 16)):
                    sp.sem_inc(s_st[n], k)
                for i in range(3):
                    sp.dma_start(x1[:, i, :], x_v[s * NT + i]).then_inc(s_x1[i], 16)
                sp.dma_start(gout[:], g_out.partition_broadcast(P)).then_inc(s_og, 16)
                attention(1, qb, kb, vb, st_b, HB)
                heads_landed(1)
                await_(sp, s_mi, (s * (2 * HEADS) + (2 * HEADS - 1)) * 8 + (FIRST - 3))
                await_(sp, s_vlo, s * (2 * HEADS) + 2 * HEADS)
                sp.dma_start(wost[:], w_o_v[:, :, 0:COL]).then_inc(s_wst, 16)
                end(sp)

                begin(s, 4)
                await_(sp, s_wlo, s * U_ALL + (U_IN + 1))
                sp.dma_start(wost[:], w_o_v[:, :, COL:2 * COL]).then_inc(s_wst, 16)
                for i in range(3, NT):
                    sp.dma_start(x1[:, i, :], x_v[s * NT + i]).then_inc(s_x1[i], 16)
                sp.dma_start(gffn[:], g_ffn.partition_broadcast(P)).then_inc(s_gf2, 16)
                with sp.Fori(2, U_O) as j:
                    await_(sp, s_wlo, s * U_ALL + j + U_IN)
                    sp.dma_start(wost[:], w_o_v[:, :, bass.ds(j * COL, COL)]).then_inc(s_wst, 16)

                def slot_free(u):
                    await_(sp, s_ulo, s * (6 * NCH) + u - 2)

                def load_up(b, c, slot):
                    col = (b % 2) * F + (b // 2) * P
                    sp.dma_start(ust[slot][:].rearrange("p (k n) -> p k n", k=NK),
                                 w_up_v[:, :, bass.ds(c * (2 * P) + col, P)]).then_inc(s_ust[slot], 16)

                def load_taps(b, c):
                    sp.dma_start(cw[b][:], conv_wb[:, bass.ds(c * 16 + 4 * b, 4)]).then_inc(s_cw[b], 16)

                def load_down(f, c, slot):
                    sp.dma_start(ust[slot][:], w_down[bass.ds(c * (2 * P) + f * P, P), :]).then_inc(s_ust[slot], 16)

                await_(sp, s_xn, s * (4 * NT) + 2 * NT)
                for b in range(3):
                    load_up(b, 0, b % 3)
                    load_taps(b, 0)
                end(sp)

                begin(s, 5)
                slot_free(3)
                load_up(3, 0, 0)
                load_taps(3, 0)
                sp.dma_start(gfin[:], g_final.partition_broadcast(P)).then_inc(s_gf, 16)
                with sp.Fori(0, NCH - 1) as c:
                    for k, what in enumerate(("u0", "d0", "d1", "u1", "u2", "u3")):
                        slot_free(c * 6 + 4 + k)
                        if what[0] == "u":
                            b = int(what[1])
                            load_up(b, c + 1, (4 + k) % 3)
                            await_(sp, s_cv, (s * NCH + c) * 4 + b + 1)
                            load_taps(b, c + 1)
                        else:
                            load_down(int(what[1]), c, (4 + k) % 3)
                load_first(s * (-NT) + NT)
                for f in range(2):
                    slot_free(6 * NCH - 2 + f)
                    load_down(f, NCH - 1, (6 * NCH - 2 + f) % 3)
                await_(sp, s_up, (s * NCH + NCH) * 4)
                load_input_weights(s * (-NT) + NT)
                for t in range(NT):
                    await_(sp, s_xn, s * (4 * NT) + 3 * NT + t + 1)
                    sp.dma_start(out_v[s * NT + t], x1[:, t, :]).then_inc(s_out, 16)
                end(sp)
            sp.wait_ge(s_out, N_SEQ * 16 * NT + ONE)
            for t in range(2):
                sp.wait_ge(s_x[t], 16 * (N_SEQ * NT // 2 + 1))
            sp.wait_ge(s_gin, 16 * (N_SEQ + 1))
            sp.wait_ge(s_wst, 16 * (N_SEQ * U_ALL + 1))
            sp.wait_ge(s_inw, 16 * (N_SEQ * 4 + 2))

        @block.tensor
        def _(pe):
            def product(dst, passes):
                n = len(passes)
                for i, (lhs, rhs) in enumerate(passes):
                    mm = pe.matmul(dst, lhs, rhs, start=(i == 0), stop=(i == n - 1))
                return mm

            def transpose_tile(src, dst):
                for k in range(NK):
                    tr = pe.transpose(dst[:, k * P:(k + 1) * P], src[:, k * P:(k + 1) * P], idn[:])
                tr.then_inc(s_tr, 1)

            def unit(t, whi, wlo, n, dst, at_hi, at_lo):
                tok = slice(t * P, (t + 1) * P)
                passes = []
                for k in range(NK):
                    passes += [(at_hi[:, k, tok], whi[:, k, 0:n]), (at_hi[:, k, tok], wlo[:, k, 0:n]),
                               (at_lo[:, k, tok], whi[:, k, 0:n])]
                product(dst[:, 0:n], passes).then_inc(s_mm, 1)

            pe.wait_ge(s_idn, 16)
            with pe.Fori(0, N_SEQ) as s:
                def c_transposed(tc):
                    pe.wait_ge(s_cn, s * NT + tc + 1)
                    if tc >= 1:
                        pe.wait_ge(s_clo, s * NT + tc)
                    for k in range(3):
                        tr = pe.transpose(bank(6)[:, k * P:(k + 1) * P], cr[tc % 2][:, k * P:(k + 1) * P], idn[:])
                    tr.then_inc(s_ctr, 1)

                pe.wait_ge(s_ya, s * (NCH * NT) + YA_CREDIT)
                pe.wait_ge(s_xn, s * (4 * NT) + 1)
                transpose_tile(xt[0], pair[2])
                for t in range(NT):
                    pe.wait_ge(s_alo, s * (3 * NT) + t + 1)
                    for u in range(U_C):
                        if t + 1 < NT and u == (1 if t == 0 else 0):
                            pe.wait_ge(s_xn, s * (4 * NT) + t + 2)
                            transpose_tile(xt[(t + 1) % 2], pair[2])
                        if t == 0:
                            pe.wait_ge(s_wlo, s * U_ALL + u + 1)
                        if t >= 2:
                            pe.wait_ge(s_eva, s * (U_C * NT) + (t - 2) * U_C + u + 1)
                        unit(t, wc_hi[u], wc_lo[u], COL if u == 0 else KV_COLS, bank((t * U_C + u) % 4), at_hi, at_lo)
                    if t >= 1:
                        c_transposed(t - 1)
                with pe.Fori(0, (U_QK + U_V) // 2) as j:
                    for e in range(2):
                        pe.wait_ge(s_wlo, s * U_ALL + j * 2 + U_C + e + 1)
                        for t in range(NT):
                            if e == 0 and t == 0:
                                pe.wait_ge(s_eva, s * (U_C * NT) + U_C * NT)
                            pe.wait_ge(s_evd, s * EV_SEQ + j * (2 * NT) + e * NT + t - 3 + EV_CREDIT)
                            unit(t, w_hi[e], w_lo[e], COL, bank(t % 4), at_hi, at_lo)

                def first_rounds(src_q, src_k, rows, ready=None):
                    for i, r in enumerate(HEAD0):
                        if ready and i in (0, 2):
                            pe.wait_ge(ready[0], ready[1 + i // 2])
                        src = src_q if r < 2 else src_k
                        if i == 2:
                            pe.wait_ge(s_clo, s * NT + NT)
                        for k in range(4):
                            tr = pe.transpose(bank(4 + i)[0:rows, k * P:(k + 1) * P], src[:, 4 * (r % 2) + k, 0:rows], idn[:])
                        tr.then_inc(s_mi, 1)

                c_transposed(NT - 1)
                pe.wait_ge(s_const, 16 * 3)
                for n in "qk":
                    pe.wait_ge(s_st[n], s * (2 * HEADS * 32) + 32)
                first_rounds(st_a["q"], st_a["k"], P)
                end(pe)

                def attention(mixer, prep_q, prep_k, score_passes, v2, ot, prob, st, pt_hi, pt_lo):
                    n0 = s * (2 * HEADS) + mixer * HEADS

                    def scores(e, t):
                        q = slice(t * P, (t + 1) * P)
                        for half in range(2):
                            k = slice(half * 512, half * 512 + 512)
                            mm = product(pair[t % 2][:, k], score_passes(e, q, k))
                        mm.then_inc(s_sc, 1)

                    def round_(r, m, heads_staged):
                        pe.wait_ge(s_mid, m + ONE)
                        if r % 2 == 0:
                            pe.wait_ge(s_st["q" if r < 2 else "k"], heads_staged * 32)
                        (prep_q if r < 2 else prep_k)(r % 2)

                    def pv(e, n, g, half):
                        if half != 1:
                            pe.wait_ge(s_ptlo, n * 16 + 4 * g + 4 + LO_CREDIT)
                            if g == 0:
                                pe.wait_ge(s_vlo, n + 1)
                            pe.wait_ge(s_ot, n * 4 + (g + ONE))
                        keys = range(NT) if half is None else range(half * NT // 2, (half + 1) * NT // 2)
                        for k in keys:
                            pe.matmul(bank(6)[:, 0:2 * P], v2[e][:, k, :], pt_hi[g % 2][:, k, :],
                                      start=(k == 0), stop=False)
                            mm = pe.matmul(bank(6)[:, 0:2 * P], v2[e][:, k, :], pt_lo[g % 2][:, k, :],
                                           start=False, stop=(k == NT - 1))
                        if half != 0:
                            mm.then_inc(s_pv, 1)

                    def osum(n, g, m):
                        pe.wait_ge(s_ot, n * 4 + (g + 1 + ONE))
                        pe.wait_ge(s_mid, m + ONE)
                        for i in range(2):
                            mm = pe.matmul(bank(7)[:, i * HA:(i + 1) * HA], ot[:, i * P:(i + 1) * P], stk[:],
                                           start=True, stop=True)
                        mm.then_inc(s_mi, 1)

                    def step(e, n, t, left):
                        pe.wait_ge(s_pr, n * 8 + t + 1)
                        for hb in range(2):
                            pe.wait_ge(s_ptlo, n * 16 + 2 * t + hb - 1 + LO_CREDIT)
                            for k in range(4):
                                c = (4 * hb + k) * P
                                tr = pe.transpose(bank(4 + hb)[:, k * P:(k + 1) * P], prob[t % 2][:, c:c + P], idn[:])
                            tr.then_inc(s_pt, 1)
                        if t + 3 < NT or left:
                            pe.wait_ge(s_pr, n * 8 + t + 2)
                        if t + 3 < NT:
                            scores(e, t + 3)
                        elif left:
                            if t + 3 == NT:
                                pe.wait_ge(s_mid, n * 8 + (FIRST + 1 + ONE))
                            scores(1 - e, t + 3 - NT)

                    def body(e, n, left):
                        for off, t, use, a, m in steps(n, left):
                            if left or not off:
                                step((e + off) % 2, n + off, t, left - off)
                            if use == "round":
                                round_(a, m, n + (2 if a == 3 else 3))
                            if use == "osum" and not (a == 3 and not left):
                                osum(n, a, m)
                            if off == 0:
                                pv(e, n, t // 2 - 1, t % 2)
                            elif t < 2 and left:
                                pv(e, n, 3, t)
                            elif t < 2:
                                pv(e, n, 3, None)
                            elif left:
                                pv(1 - e, n + 1, 0, 0)

                    pe.wait_ge(s_mid, n0 * 8 + (3 + ONE))
                    scores(0, 0)
                    scores(0, 1)
                    pe.wait_ge(s_pr, n0 * 8 + 1)
                    scores(0, 2)
                    for t in range(3):
                        step(0, n0, t, HEADS - 1)
                        round_(t, n0 * 8 + 4 + t, n0 + 2)
                    pv(0, n0, 0, 0)
                    with pe.Fori(0, HEADS // 2 - 1) as j:
                        for e in range(2):
                            body(e, j * 2 + (n0 + e), 2)
                    body(0, n0 + (HEADS - 2), 1)
                    body(1, n0 + (HEADS - 1), 0)
                    return lambda: osum(n0 + (HEADS - 1), 3, n0 * 8 + (8 * HEADS - 1))

                def prep(dst_rows, src):
                    def go(half):
                        for i in range(4):
                            tr = pe.transpose(bank(7)[0:dst_rows, i * P:(i + 1) * P], src[:, 4 * half + i, :], idn[:])
                        tr.then_inc(s_mi, 1)
                    return go

                last_osum = attention(0, prep(P, st_a["q"]), prep(P, st_a["k"]),
                          lambda e, q, k: [(q2[e][:, q], khh[e][:, k]), (q2[e][:, q], kll[e][:, k])],
                          v2_a, ot_a, pr_a, st_a, pt_hi_a, pt_lo_a)
                end(pe)

                pe.wait_ge(s_blo, s * 2 + 2)
                for t in range(NT):
                    tok = slice(t * P, (t + 1) * P)
                    if t == 1:
                        last_osum()
                        pe.wait_ge(s_mid, s * (16 * HEADS) + (8 * HEADS + ONE))
                    if t >= 2:
                        pe.wait_ge(s_bed, s * (2 * NT) + 2 * (t - 2) + 2)
                    for a, b in ((0, 512), (512, NUQ)):
                        passes = []
                        for k in range(2):
                            passes += [(ct_hi[:, k, tok], uq_hi[:, k, a:b]), (ct_hi[:, k, tok], uq_lo[:, k, a:b]),
                                       (ct_lo[:, k, tok], uq_hi[:, k, a:b])]
                        mm = product(pair[t % 2][:, a:b], passes)
                    mm.then_inc(s_bmm, 1)
                    for a, b in ((0, 512), (512, 1024)):
                        mm = product(pair[2 + t % 2][:, a:b], [
                            (ct_hi[:, 2, tok], ukv_hi[:, a:b]), (ct_hi[:, 2, tok], ukv_lo[:, a:b]),
                            (ct_lo[:, 2, tok], ukv_hi[:, a:b])])
                    mm.then_inc(s_bmm, 1)
                first_rounds(qb, kb, HB, (s_bed, s * (2 * NT) + (2 * NT - 2), s * (2 * NT) + 2 * NT))
                end(pe)

                last_osum = attention(1, prep(HB, st_b["q"]), prep(HB, st_b["k"]),
                          lambda e, q, k: [(qh[e][0:HB, q], kh[e][0:HB, k]), (qh[e][0:HB, q], kl[e][0:HB, k]),
                                           (ql[e][0:HB, q], kh[e][0:HB, k])],
                          v2_b, ot_b, pr_b, st_b, pt_hi_b, pt_lo_b)
                last_osum()
                end(pe)


                def up_half(b, half):
                    tok = slice(half * H, half * H + H)
                    passes = []
                    for k in range(NK):
                        passes += [(wu_hi[b][:, k, :], at2_hi[:, k, tok]), (wu_hi[b][:, k, :], at2_lo[:, k, tok]),
                                   (wu_lo[b][:, k, :], at2_hi[:, k, tok])]
                    return product(pair[b % 2][:, tok], passes)

                def up(b, c, first, last=False):
                    K = (s * NCH + c) * 4 + b
                    if first:
                        pe.wait_ge(s_ulo, s * (6 * NCH) + b + 1)
                        if b >= 2:
                            pe.wait_ge(s_cv, K - 1)
                    else:
                        pe.wait_ge(s_ulo, s * (6 * NCH) + (c - 1) * 6 + 5 + (0, 3, 4, 5)[b])
                        pe.wait_ge(s_cv, K - 1)
                    mm = up_half(b, 0)
                    if b == 3 and last:
                        mm.then_inc(s_uph, 1)
                    up_half(b, 1).then_inc(s_up, 1)

                def mlp_input(t):
                    pe.wait_ge(s_xn, s * (4 * NT) + 2 * NT + t + 1)
                    if t >= 2:
                        pe.wait_ge(s_alo, s * (3 * NT) + 2 * NT + t - 1)
                    transpose_tile(xn[t % 2], pair[2 + t % 2])

                def wo_input(t):
                    pe.wait_ge(s_xn, s * (4 * NT) + NT + t + 1)
                    if t == 1:
                        pe.wait_ge(s_mid, s * (16 * HEADS) + (16 * HEADS + ONE))
                    if t >= 2:
                        pe.wait_ge(s_alo, s * (3 * NT) + NT + t - 1)
                    transpose_tile(xn[t % 2], pair[2 + t % 2])

                wo_input(0)
                for u in range(U_O):
                    pe.wait_ge(s_wlo, s * U_ALL + U_IN + u + 1)
                    for t in range(NT):
                        if u == 0:
                            if t + 1 < NT:
                                wo_input(t + 1)
                            pe.wait_ge(s_alo, s * (3 * NT) + NT + t + 1)
                        pe.wait_ge(s_evd, s * EV_SEQ + (U_QK + U_V + u) * NT + t - 3 + EV_CREDIT)
                        unit(t, wo_hi[u % 2], wo_lo[u % 2], COL, bank(t % 4), at2_hi, at2_lo)
                        if u == U_O - 1 and t >= 3:
                            mlp_input(t - 3)
                mlp_input(NT - 3)
                pe.wait_ge(s_ulo, s * (6 * NCH) + 1)
                pe.wait_ge(s_alo, s * (3 * NT) + 2 * NT + NT // 2)
                pe.wait_ge(s_evd, s * EV_SEQ + (U_ALL - U_C) * NT - 2 + EV_CREDIT)
                up_half(0, 0)
                mlp_input(NT - 2)
                mlp_input(NT - 1)
                pe.wait_ge(s_alo, s * (3 * NT) + 3 * NT)
                up_half(0, 1).then_inc(s_up, 1)
                end(pe)


                def down(c, tail):
                    n = 6 * NCH if tail else (c * 6 + 7)
                    pe.wait_ge(s_ulo, s * (6 * NCH) + n)
                    if tail:
                        pe.wait_ge(s_hlop, s + 1)
                    for t in range(NT):
                        if t == (PART // P if tail else 0):
                            pe.wait_ge(s_hlo, (s * NCH + c) * 2 + (2 + ONE))
                        tok = slice(t * P, (t + 1) * P)
                        pe.wait_ge(s_ya, (s * NCH + c) * NT + t - 1 + YA_CREDIT)
                        for half in range(2):
                            col = slice(half * 512, half * 512 + 512)
                            passes = []
                            for f in range(2):
                                passes += [(h_hi[f][:, tok], wd_hi[f][:, col]), (h_hi[f][:, tok], wd_lo[f][:, col]),
                                           (h_lo[f][:, tok], wd_hi[f][:, col])]
                            mm = product(pair[2 + t % 2][:, col], passes)
                        mm.then_inc(s_dn, 1)

                for b in range(1, 4):
                    up(b, 0, True)
                def next_chunk(c, last):
                    up(0, c, False)
                    down(c - 1, False)
                    for b in range(1, 4):
                        up(b, c, False, last)

                with pe.Fori(1, NCH - 1) as c:
                    next_chunk(c, False)
                next_chunk(NCH - 1, True)
                down(NCH - 1, True)
                end(pe)


        @block.scalar
        def _(act):
            def squares(src, n_cols, junk_buf, col, done, j0=0):
                act.activation(junk_buf[:, j0:j0 + n_cols], src, ACT.Square, accum_out=ss[:, col:col + 1]).then_inc(done, 1)

            def rms(col, n, n_cols, done, inc=True):
                op = act.activation(sd[:, col:col + n], ss[:, col:col + n], ACT.Sqrt, bias=eps[:, 0:1], scale=1.0 / n_cols)
                if inc:
                    op.then_inc(done, 1)

            def act_hi(t, src, idx, at_hi):
                act.wait_ge(s_tr, idx + 1)
                act.copy(at_hi[:, :, t * P:(t + 1) * P], src[:].rearrange("p (k n) -> p k n", k=NK)).then_inc(s_ahi, 1)

            def load_table(func):
                act.activation(warm[:], eps[:], func).then_inc(s_warm, 1)

            act.wait_ge(s_eps, 1)
            def tile_stats(t, s):
                act.wait_ge(s_x[t % 2], s * (16 * NT // 2) + 16 * (t // 2 + 1))
                squares(xt[t % 2][:], D, junk, 2 * t, s_ss)
                act.wait_ge(s_ss, s * (4 * NT) + t + 1)
                rms(2 * t, 1, D, s_std)

            def unit_hi(i, src, dst):
                act.wait_ge(s_wst, (i + 1) * 16)
                act.copy(dst, src).then_inc(s_whi, 1)

            load_table(ACT.Sqrt)
            tile_stats(0, 0)
            unit_hi(0, wst[:], wc_hi[0][:])
            tile_stats(1, 0)
            with act.Fori(0, N_SEQ) as s:
                xb = s * (4 * NT)
                tb = s * (3 * NT)

                def w_split(u, src, dst):
                    unit_hi(s * U_ALL + u, src, dst)

                def stats(t):
                    tile_stats(t, s)

                def c_hi(tc):
                    act.wait_ge(s_ctr, s * NT + tc + 1)
                    act.copy(ct_hi[:, :, tc * P:(tc + 1) * P],
                             bank(6)[:, 0:3 * P].rearrange("p (k n) -> p k n", k=3)).then_inc(s_chi, 1)

                act_hi(0, pair[2], tb, at_hi)
                w_split(1, wst[:, :, 0:KV_COLS], wc_hi[1][:])
                act.wait_ge(s_out, s * (16 * NT) + ONE)
                for t in range(NT):
                    if t + 1 < NT:
                        act_hi(t + 1, pair[2], tb + t + 1, at_hi)
                    if t + 2 < NT:
                        stats(t + 2)
                    c = cr[t % 2]
                    if t >= 2:
                        act.wait_ge(s_ctr, s * NT + t - 1)
                    act.wait_ge(s_mm, s * (U_ALL * NT) + 2 * t + 1)
                    act.copy(c[:, 0:RQ], bank(2 * t % 4)[:, 0:RQ]).then_inc(s_eva, 1)
                    act.wait_ge(s_mm, s * (U_ALL * NT) + 2 * t + 2)
                    act.copy(c[:, RQ:RC + ROT], bank((2 * t + 1) % 4)[:, 0:KV_COLS]).then_inc(s_eva, 1)
                    act.wait_ge(s_eva, s * (U_C * NT) + 2 * t + 2)
                    squares(c[:, 0:RQ], RQ, junk, 16 + 2 * t, s_css)
                    squares(c[:, RQ:RC], RKV, junk, 17 + 2 * t, s_css, RQ)
                    act.wait_ge(s_css, s * (2 * NT) + 2 * t + 2)
                    rms(16 + 2 * t, 1, RQ, s_cstd)
                    rms(17 + 2 * t, 1, RKV, s_cstd)
                    if t == 4:
                        act.wait_ge(s_wst, (s * U_ALL + U_C + 1) * 16)
                        act.copy(w_hi[0][:, 0:NK // 2], wst[:, 0:NK // 2]).then_inc(s_whp, 1)
                    if t == 5:
                        act.copy(w_hi[0][:, NK // 2:NK], wst[:, NK // 2:NK]).then_inc(s_whi, 1)
                    if t == 7:
                        w_split(U_C + 1, wst[:], w_hi[1][:])
                    if t >= 1:
                        c_hi(t - 1)
                with act.Fori(0, U_QK // 2) as j:
                    for e in range(2):
                        act.wait_ge(s_mm, s * (U_ALL * NT) + j * (2 * NT) + (U_C + e + 1) * NT)
                        w_split(j * 2 + 4 + e, wst[:], w_hi[e][:])
                c_hi(NT - 1)
                end(act)

                def attention(mixer, hi_q, hi_k, v2, ot, prob, st, scale, pt_hi, v_first, between, near_end):
                    n0 = s * (2 * HEADS) + mixer * HEADS

                    def prob_tile(e, n, t):
                        act.wait_ge(s_nm, n * 8 + t + 1)
                        act.activation(prob[t % 2][:], pair[t % 2][:], ACT.Exp, bias=nm[:, t % 4:t % 4 + 1],
                                       scale=scale, accum_out=den[:, e, t:t + 1]).then_inc(s_pr, 1)

                    def round_(r, m, e):
                        act.wait_ge(s_mi, m + 1)
                        (hi_q if r < 2 else hi_k)(e, r % 2)

                    def v_split(e, heads_staged):
                        act.wait_ge(s_st["v"], heads_staged * 16)
                        act.copy(v2[e][:, :, 0:HA], st["v"][:]).then_inc(s_vhi, 1)

                    def first_round(i, r):
                        act.wait_ge(s_mi, n0 * 8 + i + 1)
                        (hi_q if r < 2 else hi_k)(0, r % 2, bank(4 + i))

                    def evict(n, g):
                        act.wait_ge(s_pv, n * 4 + g + 1)
                        act.copy(ot[:], bank(6)[:, 0:2 * P]).then_inc(s_ot, 1)

                    def next_probs(e, n, t, left):
                        if t + 1 < NT:
                            prob_tile(e, n, t + 1)
                        elif left:
                            prob_tile(1 - e, n + 1, 0)

                    def step(n, t):
                        for hb in range(2):
                            act.wait_ge(s_pt, n * 16 + 2 * t + hb + 1)
                            act.copy(pt_hi[t // 2 % 2][:, 4 * hb:4 * hb + 4, t % 2 * P:(t % 2 + 1) * P],
                                     bank(4 + hb).rearrange("p (k n) -> p k n", k=4)).then_inc(s_pthi, 1)

                    def body(e, n, left):
                        for off, t, use, a, m in steps(n, left):
                            if left or not off:
                                next_probs((e + off) % 2, n + off, t, left - off)
                            if use == "osum":
                                evict(n, a)
                            if left or not off:
                                step(n + off, t)
                            if use == "round":
                                round_(a, m, 1 - e if a == 3 else e)
                            if t == 5 and not left:
                                between()
                            if t == 0 and not left:
                                near_end()
                            if off and t == 2 and left > 1:
                                v_split(e, n + 3)

                    for i, r in enumerate(HEAD0):
                        first_round(i, r)
                    act.copy(v2[0][:, :, 0:HA], v_first).then_inc(s_vhi, 1)
                    prob_tile(0, n0, 0)
                    for t in range(3):
                        prob_tile(0, n0, t + 1)
                        step(n0, t)
                        round_(t, n0 * 8 + 4 + t, 1)
                    v_split(1, n0 + 2)
                    with act.Fori(0, HEADS // 2 - 1) as j:
                        for e in range(2):
                            body(e, j * 2 + (n0 + e), 2)
                    body(0, n0 + (HEADS - 2), 1)
                    body(1, n0 + (HEADS - 1), 0)

                def hi_of(dst, rows):
                    def go(e, half, src=bank(7)):
                        act.copy(dst[e][0:rows, half * 512:half * 512 + 512], src[0:rows, :]).then_inc(s_mihi, 1)
                    return go

                load_table(ACT.Exp)
                act.wait_ge(s_st["v"], s * (2 * HEADS * 16) + 16)

                def b_weights_hi():
                    act.wait_ge(s_bw, (s * 2 + 2) * 16)
                    act.copy(uq_hi[:], uq_st[:]).then_inc(s_bhi, 1)
                    act.copy(ukv_hi[:], ukv_st[:]).then_inc(s_bhi, 1)

                attention(0, hi_of(q2, P), hi_of(khh, P), v2_a, ot_a, pr_a, st_a, SCALE_A, pt_hi_a, st_a["v"][:],
                          b_weights_hi, lambda: None)
                end(act)

                for t in range(NT):
                    act.wait_ge(s_bmm, s * (2 * NT) + 2 * t + 1)
                    act.copy(qb[:, t, :].rearrange("p (h x) -> p h x", x=HB)[:, :, 0:HA],
                             pair[t % 2][:, 0:NUQ].rearrange("p (h x) -> p h x", x=HB)[:, :, 0:HA]).then_inc(s_bea, 1)
                    act.wait_ge(s_bmm, s * (2 * NT) + 2 * t + 2)
                    act.copy(kb[:, t, :].rearrange("p (h x) -> p h x", x=HB)[:, :, 0:HA],
                             pair[2 + t % 2][:].rearrange("p (h x) -> p h x", x=2 * HA)[:, :, 0:HA]).then_inc(s_bea, 1)
                end(act)

                def o_stats(t):
                    act.activation(junk2[:, 0:WA], o[:, t, 0:WA], ACT.Square, accum_out=ss[:, 2 * t:2 * t + 1])
                    act.activation(junk2[:, WA:D], o[:, t, WA:D], ACT.Square, accum_out=ss[:, 2 * t + 1:2 * t + 2]).then_inc(s_ss, 1)
                    act.wait_ge(s_ss, xb + NT + t + 1)
                    rms(2 * t, 2, WA, s_std)

                load_table(ACT.Exp)
                def first_o_stats():
                    act.wait_ge(s_mid, (s * (2 * HEADS) + (2 * HEADS - 1)) * 8 + (FIRST - 3 + 1 + ONE))
                    o_stats(0)

                attention(1, hi_of(qh, HB), hi_of(kh, HB), v2_b, ot_b, pr_b, st_b, SCALE_B, pt_hi_b, vb[:, :, 0:HA],
                          lambda: w_split(U_IN, wost[:], wo_hi[0][:]), first_o_stats)
                o_stats(1)
                end(act)

                for t in range(NT):
                    act_hi(t, pair[2 + t % 2], tb + NT + t, at2_hi)
                    if t + 2 < NT:
                        o_stats(t + 2)
                    if t == 3:
                        w_split(U_IN + 1, wost[:], wo_hi[1][:])
                for u in range(2, U_O):
                    act.wait_ge(s_mm, s * (U_ALL * NT) + (U_IN + u - 1) * NT)
                    w_split(U_IN + u, wost[:], wo_hi[u % 2][:])

                def split(u3, slot, dst):
                    act.wait_ge(s_ust[slot], (s * (2 * NCH) + u3) * 16)
                    act.copy(dst, ust[slot][:]).then_inc(s_uhi, 1)

                def split_up(b, c_next, u3, slot):
                    split(u3, slot, wu_hi[b][:].rearrange("p k n -> p (k n)"))

                for b in range(2):
                    split_up(b, 0, 1, b)

                def x1_stats(t, base):
                    squares(x1[:, t, :], D, junk2 if base == 2 * NT else junk3, 2 * t, s_ss)
                    act.wait_ge(s_ss, xb + base + t + 1)
                    rms(2 * t, 1, D, s_std)

                for t in range(NT):
                    act.wait_ge(s_evd, s * EV_SEQ + (U_ALL - U_C - 1) * NT + t + 1 + EV_CREDIT)
                    x1_stats(t, 2 * NT)
                    if t >= 3:
                        act_hi(t - 3, pair[2 + (t - 3) % 2], tb + 2 * NT + t - 3, at2_hi)
                for t in range(NT - 3, NT):
                    act_hi(t, pair[2 + t % 2], tb + 2 * NT + t, at2_hi)
                end(act)


                def conv(b, c):
                    K = (s * NCH + c) * 4 + b
                    act.wait_ge(s_up, K + 1)
                    act.wait_ge(s_cw[b], (s * NCH + c + 1) * 16)
                    dst = cg if b % 2 == 0 else cv
                    if b == 3:
                        act.wait_ge(s_hlo, (s * NCH + c) * 2 + (1 + ONE))
                    if b == 1:
                        act.wait_ge(s_hlo, (s * NCH + c) * 2 + ONE)
                    act.activation(dst[:], pair[b % 2][:], ACT.Identity, bias=cw[b][:, 3:4], scale=cw[b][:, 1:2]).then_inc(s_ci, 1)

                def conv_half(c, half):
                    K = (s * NCH + c) * 4 + 3
                    tok = slice(half * H, half * H + H)
                    if half == 0:
                        act.wait_ge(s_uph, s + 1)
                        act.wait_ge(s_cw[3], (s * NCH + c + 1) * 16)
                        act.wait_ge(s_hlo, (s * NCH + c) * 2 + (1 + ONE))
                    else:
                        act.wait_ge(s_up, K + 1)
                    act.activation(cv[:, tok], pair[1][:, tok], ACT.Identity, bias=cw[3][:, 3:4],
                                   scale=cw[3][:, 1:2]).then_inc(s_cih if half == 0 else s_ci, 1)

                def silu(f, c):
                    act.wait_ge(s_cv, (s * NCH + c) * 4 + 2 * f + 1)
                    act.activation(cg[:], cg[:], ACT.Silu).then_inc(s_sg, 1)

                def hidden_hi(f, c):
                    act.wait_ge(s_h, (s * NCH + c) * 2 + f + 1)
                    act.copy(h_hi[f][:], cv[:]).then_inc(s_hhi, 1)

                def chunk(c, first, last):
                    def next_up(b, k):
                        if not last:
                            split_up(b, c + 1, c * 2 + (4 + k) // 3 + 1, (4 + k) % 3)
                    conv(0, c)
                    next_up(0, 0)
                    silu(0, c)
                    if not first:
                        act.wait_ge(s_dn, (s * NCH + c) * NT)
                    for f in range(2):
                        k = f if last else f + 1
                        split(c * 2 + (4 + k) // 3 + 1, (4 + k) % 3, wd_hi[f][:])
                    conv(1, c)
                    hidden_hi(0, c)
                    next_up(1, 3)
                    conv(2, c)
                    next_up(2, 4)
                    silu(1, c)
                    if last:
                        conv_half(c, 0)
                        act.wait_ge(s_hp, s + 1)
                        act.copy(h_hi[1][:, 0:PART], cv[:, 0:PART]).then_inc(s_hhip, 1)
                        conv_half(c, 1)
                        act.wait_ge(s_h, (s * NCH + c) * 2 + 2)
                        act.copy(h_hi[1][:, PART:S], cv[:, PART:S]).then_inc(s_hhi, 1)
                    else:
                        conv(3, c)
                        hidden_hi(1, c)
                    next_up(3, 5)

                for b in range(2, 4):
                    split_up(b, 0, b // 3 + 1, b % 3)
                chunk(0, True, False)
                with act.Fori(1, NCH - 1) as c:
                    chunk(c, False, False)
                chunk(NCH - 1, False, True)
                load_table(ACT.Sqrt)
                unit_hi((s + 1) * U_ALL, wst[:], wc_hi[0][:])
                for t in range(NT):
                    act.wait_ge(s_ya, (s * NCH + NCH - 1) * NT + t + 1 + YA_CREDIT)
                    x1_stats(t, 3 * NT)
                for t in range(2):
                    tile_stats(t, s + 1)
                end(act)

        @block.vector
        def _(dve):
            def normalise(dst, src, gain, col, idx, halves=1):
                dve.wait_ge(s_std, idx + 1)
                dve.reciprocal(rs[:, col:col + halves], sd[:, col:col + halves]).then_inc(s_rs, 1)
                dve.wait_ge(s_rs, idx + 1)
                w = D // halves
                for i in range(halves):
                    c = slice(i * w, (i + 1) * w)
                    op = dve.scalar_tensor_tensor(dst[:, c], src[:, c], rs[:, col + i:col + i + 1], gain[:, c], ALU.mult, ALU.mult)
                op.then_inc(s_xn, 1)

            def act_lo(t, src, idx, at_hi, at_lo):
                dve.wait_ge(s_ahi, idx + 1)
                tok = slice(t * P, (t + 1) * P)
                dve.tensor_tensor(at_lo[:, :, tok], src[:].rearrange("p (k n) -> p k n", k=NK),
                                  at_hi[:, :, tok].bitcast(F32), ALU.subtract).then_inc(s_alo, 1)

            def rotate(dst, src, cos, sin, heads, width, ta, tb_, idx, done):
                h = width // 2
                bc = lambda a, n: a.unsqueeze(1).to_broadcast([P, heads, n])
                dve.tensor_tensor(ta, src, bc(cos, width), ALU.mult)
                dve.tensor_tensor(tb_[:, :, 0:h], src[:, :, h:width], bc(sin[:, 0:h], h), ALU.mult)
                dve.tensor_tensor(tb_[:, :, h:width], src[:, :, 0:h], bc(sin[:, h:width], h), ALU.mult).then_inc(s_rot, 1)
                dve.wait_ge(s_rot, idx + 1)
                dve.tensor_tensor(dst, ta, tb_, ALU.add).then_inc(done, 1)

            dve.memset(eps[:], EPS).then_inc(s_eps, 1)
            for s_free, n in ((s_ptlo, LO_CREDIT), (s_evd, EV_CREDIT), (s_ya, YA_CREDIT), (s_mid, ONE), (s_ot, ONE),
                              (s_hlo, ONE), (s_phase, ONE), (s_out, ONE)):
                for _ in range(n):
                    dve.sem_inc(s_free, 1)
            def unit_lo(i, src, hi, lo):
                dve.wait_ge(s_whi, i + 1)
                dve.tensor_tensor(lo, src, hi.bitcast(F32), ALU.subtract).then_inc(s_wlo, 1)

            def first_tile(s):
                dve.wait_ge(s_gin, (s + 1) * 16)
                normalise(xt[0][:], xt[0][:], gin[:], 0, s * (4 * NT))

            first_tile(0)
            unit_lo(0, wst[:], wc_hi[0][:], wc_lo[0][:])
            dve.wait_ge(s_const, 16 * 3)
            with dve.Fori(0, N_SEQ) as s:
                xb = s * (4 * NT)
                tb = s * (3 * NT)

                def w_split(u, src, hi, lo):
                    unit_lo(s * U_ALL + u, src, hi, lo)

                def xnorm(t):
                    normalise(xt[t % 2][:], xt[t % 2][:], gin[:], 2 * t, xb + t)

                def c_lo(tc):
                    dve.wait_ge(s_chi, s * NT + tc + 1)
                    tok = slice(tc * P, (tc + 1) * P)
                    dve.tensor_tensor(ct_lo[:, :, tok], bank(6)[:, 0:3 * P].rearrange("p (k n) -> p k n", k=3),
                                      ct_hi[:, :, tok].bitcast(F32), ALU.subtract).then_inc(s_clo, 1)

                act_lo(0, pair[2], tb, at_hi, at_lo)
                xnorm(1)
                w_split(1, wst[:, :, 0:KV_COLS], wc_hi[1][:], wc_lo[1][:])
                dve.wait_ge(s_inw, (s + 1) * 64)
                for t in range(NT):
                    if t + 1 < NT:
                        act_lo(t + 1, pair[2], tb + t + 1, at_hi, at_lo)
                    if t + 2 < NT:
                        xnorm(t + 2)
                    c = cr[t % 2]
                    q0 = 16 + 2 * t
                    dve.wait_ge(s_cstd, s * (2 * NT) + 2 * t + 2)
                    dve.reciprocal(rs[:, q0:q0 + 2], sd[:, q0:q0 + 2]).then_inc(s_crs, 1)
                    dve.wait_ge(s_crs, s * NT + t + 1)
                    dve.scalar_tensor_tensor(c[:, 0:RQ], c[:, 0:RQ], rs[:, q0:q0 + 1], glora[:, 0:RQ], ALU.mult, ALU.mult)
                    dve.scalar_tensor_tensor(c[:, RQ:RC], c[:, RQ:RC], rs[:, q0 + 1:q0 + 2], glora[:, RQ:RC], ALU.mult, ALU.mult)
                    rotate(krot[:, t, :].unsqueeze(1), c[:, RC:RC + ROT].unsqueeze(1), cosb[:, t, :], sinb[:, t, :], 1, ROT,
                           pra[t % 2][:, 0:ROT].unsqueeze(1), prb[t % 2][:, 0:ROT].unsqueeze(1), s * ROT_SEQ + t, s_cn)
                    if t == 4:
                        dve.wait_ge(s_whp, s + 1)
                        dve.tensor_tensor(w_lo[0][:, 0:NK // 2], wst[:, 0:NK // 2],
                                          w_hi[0][:, 0:NK // 2].bitcast(F32), ALU.subtract)
                    if t == 5:
                        dve.wait_ge(s_whi, s * U_ALL + U_C + 1)
                        dve.tensor_tensor(w_lo[0][:, NK // 2:NK], wst[:, NK // 2:NK],
                                          w_hi[0][:, NK // 2:NK].bitcast(F32), ALU.subtract).then_inc(s_wlo, 1)
                    if t == 7:
                        w_split(U_C + 1, wst[:], w_hi[1][:], w_lo[1][:])
                    if t >= 1:
                        c_lo(t - 1)
                heads4 = lambda a: a.rearrange("p (h x) -> p h x", x=HA)
                with dve.Fori(0, U_QK // 2) as j:
                    for e in range(2):
                        for t in range(NT):
                            dve.wait_ge(s_mm, s * (U_ALL * NT) + j * (2 * NT) + (U_C + e) * NT + t + 1)
                            rotate(heads4(qk[:, t, bass.ds(j * (2 * COL) + e * COL, COL)]), heads4(bank(t % 4)[:, 0:COL]),
                                   cosa[:, t, :], sina[:, t, :], COL // HA, HA, heads4(pra[t % 2][:]), heads4(prb[t % 2][:]),
                                   s * ROT_SEQ + j * (2 * NT) + (e + 1) * NT + t, s_evd)
                        w_split(j * 2 + 4 + e, wst[:], w_hi[e][:], w_lo[e][:])
                for u in range(U_V):
                    for t in range(NT):
                        dve.wait_ge(s_mm, s * (U_ALL * NT) + (U_C + U_QK + u) * NT + t + 1)
                        dve.tensor_copy(va[:, t, u * COL:(u + 1) * COL], bank(t % 4)[:, 0:COL]).then_inc(s_evd, 1)
                c_lo(NT - 1)
                end(dve)

                def attention(mixer, lo_q, lo_k, v2, st, scale, pt_hi, pt_lo, v_first, between, near_end):
                    n0 = s * (2 * HEADS) + mixer * HEADS

                    def row_max(t, idx):
                        m, n = mx[:, t % 4:t % 4 + 1], nm[:, t % 4:t % 4 + 1]
                        sc = pair[t % 2][:]
                        if mixer == 0:
                            await_(dve, s_sc, idx + 1)
                            u0 = (NT - 1 - t) * P
                            dve.tensor_tensor_reduce(sc, sc, logc[:, u0:u0 + S], 1.0, -3e38, ALU.add, ALU.max, m).then_inc(s_max, 1)
                        else:
                            dve.wait_ge(s_sc, idx + 1)
                            dve.tensor_reduce(m, sc, AXX, ALU.max).then_inc(s_max, 1)
                        dve.wait_ge(s_max, idx + 1)
                        dve.tensor_scalar(n, m, -scale, None, ALU.mult).then_inc(s_nm, 1)

                    def round_(r, e, idx):
                        dve.wait_ge(s_mihi, idx + 1)
                        (lo_q if r < 2 else lo_k)(e, r % 2)

                    def v_split(e, idx):
                        dve.wait_ge(s_vhi, idx + 1)
                        dve.tensor_tensor(v2[e][:, :, HA:P], st["v"][:], v2[e][:, :, 0:HA].bitcast(F32), ALU.subtract).then_inc(s_vlo, 1)

                    def sums(e, g):
                        dve.reciprocal(rden[:, g % 2 * 2:g % 2 * 2 + 2], den[:, e, 2 * g:2 * g + 2]).then_inc(s_rden, 1)

                    def osum(e, n, g, col, m):
                        r2 = slice(g % 2 * 2, g % 2 * 2 + 2)
                        dve.wait_ge(s_mi, m + 1)
                        dve.wait_ge(s_rden, n * 4 + g + 1)
                        dve.tensor_tensor(o[:, 2 * g:2 * g + 2, bass.ds(col, HA)],
                                          bank(7)[:, 0:2 * HA].rearrange("p (i x) -> p i x", i=2),
                                          rden[:, r2].unsqueeze(2).to_broadcast([P, 2, HA]), ALU.mult).then_inc(s_mid, 1)

                    def step(n, t):
                        for hb in range(2):
                            dve.wait_ge(s_pthi, n * 16 + 2 * t + hb + 1)
                            dst = (slice(None), slice(4 * hb, 4 * hb + 4), slice(t % 2 * P, (t % 2 + 1) * P))
                            dve.tensor_tensor(pt_lo[t // 2 % 2][dst], bank(4 + hb).rearrange("p (k n) -> p k n", k=4),
                                              pt_hi[t // 2 % 2][dst].bitcast(F32), ALU.subtract).then_inc(s_ptlo, 1)

                    def body(e, n, col, left):
                        for off, t, use, a, m in steps(n, left):
                            if use == "osum":
                                sums(e, a)
                            if left or not off:
                                step(n + off, t)
                                if t + 3 < NT or left - off:
                                    row_max((t + 3) % NT, (n + off) * 8 + t + 3)
                            if t == 5 and not left:
                                between()
                            if use == "round":
                                round_(a, 1 - e if a == 3 else e, n * 4 + (7 if a == 3 else 8 + a))
                            if use == "osum":
                                osum(e, n, a, col, m)
                            if t == 0 and not left:
                                near_end()
                            if off and t == 2 and left > 1:
                                v_split(e, n + 2)

                    def first_round(i, r):
                        dve.wait_ge(s_mihi, n0 * 4 + i + 1)
                        (lo_q if r < 2 else lo_k)(0, r % 2, bank(4 + i))

                    for i, r in enumerate(HEAD0[:3]):
                        first_round(i, r)
                    row_max(0, n0 * 8)
                    first_round(3, HEAD0[3])
                    row_max(1, n0 * 8 + 1)
                    dve.wait_ge(s_vhi, n0 + 1)
                    dve.tensor_tensor(v2[0][:, :, HA:P], v_first, v2[0][:, :, 0:HA].bitcast(F32), ALU.subtract).then_inc(s_vlo, 1)
                    row_max(2, n0 * 8 + 2)
                    for t in range(3):
                        step(n0, t)
                        row_max(t + 3, n0 * 8 + t + 3)
                        round_(t, 1, n0 * 4 + 4 + t)
                    v_split(1, n0 + 1)
                    with dve.Fori(0, HEADS // 2 - 1) as j:
                        for e in range(2):
                            body(e, j * 2 + (n0 + e), j * (2 * HA) + (mixer * WA + e * HA), 2)
                    body(0, n0 + (HEADS - 2), mixer * WA + (HEADS - 2) * HA, 1)
                    body(1, n0 + (HEADS - 1), mixer * WA + (HEADS - 1) * HA, 0)

                def lo_of(dst, hi, r0, r1):
                    def go(e, half, src=bank(7)):
                        c = slice(half * 512, half * 512 + 512)
                        dve.tensor_tensor(dst[e][r0:r1, c], src[r0:r1, :], hi[e][r0:r1, c].bitcast(F32),
                                          ALU.subtract).then_inc(s_mid, 1)
                    return go

                dve.wait_ge(s_logc, (s + 1) * 16)

                def b_weights_lo():
                    dve.wait_ge(s_bhi, s * 2 + 1)
                    dve.tensor_tensor(uq_lo[:], uq_st[:], uq_hi[:].bitcast(F32), ALU.subtract).then_inc(s_blo, 1)
                    dve.wait_ge(s_bhi, s * 2 + 2)
                    dve.tensor_tensor(ukv_lo[:], ukv_st[:], ukv_hi[:].bitcast(F32), ALU.subtract).then_inc(s_blo, 1)

                attention(0, lo_of(q2, q2, HA, P), lo_of(kll, khh, 0, P), v2_a, st_a, SCALE_A, pt_hi_a, pt_lo_a,
                          st_a["v"][:], b_weights_lo, lambda: None)
                end(dve)

                for t in range(NT):
                    by_head = lambda a, x: a.rearrange("p (h x) -> p h x", x=x)
                    dve.wait_ge(s_bea, s * (2 * NT) + 2 * t + 1)
                    rotate(by_head(qb[:, t, :], HB)[:, :, HA:HB], by_head(pair[t % 2][:, 0:NUQ], HB)[:, :, HA:HB],
                           cosb[:, t, :], sinb[:, t, :], HEADS, ROT, pba[t % 2][:], pbb[t % 2][:],
                           s * ROT_SEQ + (1 + U_QK) * NT + t, s_bed)
                    dve.tensor_copy(by_head(kb[:, t, :], HB)[:, :, HA:HB], krot[:, t, :].unsqueeze(1).to_broadcast([P, HEADS, ROT]))
                    dve.wait_ge(s_bea, s * (2 * NT) + 2 * t + 2)
                    dve.tensor_copy(by_head(vb[:, t, :], HA), by_head(pair[2 + t % 2][:], 2 * HA)[:, :, HA:2 * HA]).then_inc(s_bed, 1)
                end(dve)

                def onorm(t):
                    if t >= 2:
                        dve.wait_ge(s_tr, tb + NT + t - 1)
                    normalise(xn[t % 2], o[:, t, :], gout, 2 * t, xb + NT + t, halves=2)

                def first_onorm():
                    dve.wait_ge(s_og, (s + 1) * 16)
                    onorm(0)

                attention(1, lo_of(ql, qh, 0, HB), lo_of(kl, kh, 0, HB), v2_b, st_b, SCALE_B, pt_hi_b, pt_lo_b,
                          vb[:, :, 0:HA], lambda: w_split(U_IN, wost[:], wo_hi[0][:], wo_lo[0][:]), first_onorm)
                onorm(1)
                end(dve)


                def add_unit(u, t):
                    if u == 0:
                        dve.wait_ge(s_x1[t], (s + 1) * 16)
                    dve.wait_ge(s_mm, s * (U_ALL * NT) + (U_IN + u) * NT + t + 1)
                    col = slice(u * COL, (u + 1) * COL)
                    dve.tensor_tensor(x1[:, t, col], bank(t % 4)[:, 0:COL], x1[:, t, col], ALU.add).then_inc(s_evd, 1)

                def split(u, slot, hi, lo):
                    dve.wait_ge(s_uhi, s * (6 * NCH) + u + 1)
                    dve.tensor_tensor(lo, ust[slot][:], hi.bitcast(F32), ALU.subtract).then_inc(s_ulo, 1)

                def split_up(b, u, slot):
                    split(u, slot, wu_hi[b][:].rearrange("p k n -> p (k n)"), wu_lo[b][:].rearrange("p k n -> p (k n)"))

                for t in range(NT):
                    act_lo(t, pair[2 + t % 2], tb + NT + t, at2_hi, at2_lo)
                    if t + 2 < NT:
                        onorm(t + 2)
                    if t >= 1:
                        add_unit(0, t - 1)
                    if t == 3:
                        w_split(U_IN + 1, wost[:], wo_hi[1][:], wo_lo[1][:])
                add_unit(0, NT - 1)
                w_split(U_IN + 2, wost[:], wo_hi[0][:], wo_lo[0][:])

                def xnorm2(t):
                    dve.wait_ge(s_tr, tb + (2 * NT + t - 1 if t >= 2 else 2 * NT))
                    normalise(xn[t % 2], x1[:, t, :], gffn, 2 * t, xb + 2 * NT + t)

                for t in range(NT):
                    add_unit(1, t)
                w_split(U_IN + 3, wost[:], wo_hi[1][:], wo_lo[1][:])
                for b in range(2):
                    split_up(b, b, b)
                for t in range(NT):
                    add_unit(2, t)
                dve.wait_ge(s_gf2, (s + 1) * 16)
                for t in range(NT):
                    add_unit(3, t)
                    if t >= 1:
                        xnorm2(t - 1)
                    if t >= 3:
                        act_lo(t - 3, pair[2 + (t - 3) % 2], tb + 2 * NT + t - 3, at2_hi, at2_lo)
                xnorm2(NT - 1)
                act_lo(NT - 3, pair[2 + (NT - 3) % 2], tb + 3 * NT - 3, at2_hi, at2_lo)
                for t in range(NT - 2, NT):
                    act_lo(t, pair[2 + t % 2], tb + 2 * NT + t, at2_hi, at2_lo)
                end(dve)


                def conv(b, c):
                    K = (s * NCH + c) * 4 + b
                    buf, u = (cg if b % 2 == 0 else cv), pair[b % 2]
                    dve.wait_ge(s_ci, K + 1)
                    dve.scalar_tensor_tensor(buf[:, 1:S], u[:, 0:S - 1], cw[b][:, 0:1], buf[:, 1:S], ALU.mult, ALU.add).then_inc(s_c0, 1)
                    dve.wait_ge(s_c0, K + 1)
                    dve.scalar_tensor_tensor(buf[:, 0:S - 1], u[:, 1:S], cw[b][:, 2:3], buf[:, 0:S - 1], ALU.mult, ALU.add).then_inc(s_cv, 1)

                def hidden(f, c):
                    i = (s * NCH + c) * 2 + f
                    dve.wait_ge(s_sg, i + 1)
                    dve.wait_ge(s_cv, (s * NCH + c) * 4 + 2 * f + 2)
                    dve.tensor_tensor(cv[:], cg[:], cv[:], ALU.mult).then_inc(s_h, 1)
                    dve.wait_ge(s_hhi, i + 1)
                    dve.tensor_tensor(h_lo[f][:], cv[:], h_hi[f][:].bitcast(F32), ALU.subtract).then_inc(s_hlo, 1)

                def hidden_halves(c):
                    K = (s * NCH + c) * 4 + 3
                    i = (s * NCH + c) * 2 + 1
                    u, left, right = pair[1], cw[3][:, 0:1], cw[3][:, 2:3]
                    dve.wait_ge(s_cih, s + 1)
                    dve.scalar_tensor_tensor(cv[:, 1:H], u[:, 0:H - 1], left, cv[:, 1:H], ALU.mult, ALU.add).then_inc(s_th, 1)
                    dve.wait_ge(s_th, 2 * s + 1)
                    dve.scalar_tensor_tensor(cv[:, 0:H - 1], u[:, 1:H], right, cv[:, 0:H - 1], ALU.mult, ALU.add).then_inc(s_th, 1)
                    dve.wait_ge(s_sg, i + 1)
                    dve.wait_ge(s_th, 2 * s + 2)
                    dve.tensor_tensor(cv[:, 0:PART], cg[:, 0:PART], cv[:, 0:PART], ALU.mult).then_inc(s_hp, 1)
                    dve.wait_ge(s_hhip, s + 1)
                    dve.tensor_tensor(h_lo[1][:, 0:PART], cv[:, 0:PART], h_hi[1][:, 0:PART].bitcast(F32), ALU.subtract).then_inc(s_hlop, 1)
                    dve.wait_ge(s_ci, K + 1)
                    dve.scalar_tensor_tensor(cv[:, H:S], u[:, H - 1:S - 1], left, cv[:, H:S], ALU.mult, ALU.add).then_inc(s_c0, 1)
                    dve.wait_ge(s_c0, K + 1)
                    dve.scalar_tensor_tensor(cv[:, H - 1:S - 1], u[:, H:S], right, cv[:, H - 1:S - 1], ALU.mult, ALU.add).then_inc(s_cv, 1)
                    dve.wait_ge(s_cv, K + 1)
                    dve.tensor_tensor(cv[:, PART:S], cg[:, PART:S], cv[:, PART:S], ALU.mult).then_inc(s_h, 1)
                    dve.wait_ge(s_hhi, i + 1)
                    dve.tensor_tensor(h_lo[1][:, PART:S], cv[:, PART:S], h_hi[1][:, PART:S].bitcast(F32), ALU.subtract).then_inc(s_hlo, 1)

                def add_down(t, c):
                    dve.wait_ge(s_dn, (s * NCH + c) * NT + t + 1)
                    dve.tensor_tensor(x1[:, t, :], pair[2 + t % 2][:], x1[:, t, :], ALU.add).then_inc(s_ya, 1)

                def chunk(c, first, last):
                    def next_up(b, k):
                        if not last:
                            split_up(b, c * 6 + 4 + k, (4 + k) % 3)
                    conv(0, c)
                    for t in range(NT):
                        if not first:
                            add_down(t, c - 1)
                        if t == 2:
                            next_up(0, 0)
                    for f in range(2):
                        k = f if last else f + 1
                        split(c * 6 + 4 + k, (4 + k) % 3, wd_hi[f][:], wd_lo[f][:])
                    conv(1, c)
                    hidden(0, c)
                    next_up(1, 3)
                    conv(2, c)
                    next_up(2, 4)
                    if last:
                        hidden_halves(c)
                    else:
                        conv(3, c)
                        hidden(1, c)
                    next_up(3, 5)

                for b in range(2, 4):
                    split_up(b, b, b % 3)
                chunk(0, True, False)
                with dve.Fori(1, NCH - 1) as c:
                    chunk(c, False, False)
                chunk(NCH - 1, False, True)
                dve.wait_ge(s_gf, (s + 1) * 16)
                for t in range(NT):
                    add_down(t, NCH - 1)
                    if t >= 1:
                        normalise(x1[:, t - 1, :], x1[:, t - 1, :], gfin, 2 * (t - 1), xb + 3 * NT + t - 1)
                normalise(x1[:, NT - 1, :], x1[:, NT - 1, :], gfin, 2 * (NT - 1), xb + 4 * NT - 1)
                first_tile(s + 1)
                unit_lo((s + 1) * U_ALL, wst[:], wc_hi[0][:], wc_lo[0][:])
                end(dve)


def tables():
    import numpy as np

    def rotary(width):
        half = width // 2
        inv = (np.float32(10000.0) ** (-np.arange(half, dtype=np.float32) * np.float32(2.0 / width))).astype(np.float32)
        ang = np.arange(S, dtype=np.float32)[:, None] * inv[None, :]
        cos, sin = np.cos(ang).astype(np.float32), np.sin(ang).astype(np.float32)
        per_tile = lambda a: np.ascontiguousarray(a.reshape(NT, P, width).transpose(1, 0, 2))
        return per_tile(np.concatenate([cos, cos], 1)), per_tile(np.concatenate([-sin, sin], 1))

    ca, sa = rotary(HA)
    cb, sb = rotary(ROT)
    d = np.arange(MASK_W)[None, :] - (S - P) - np.arange(P)[:, None]
    count = sum(((np.abs(d) <= window // 2) & (d % dil == 0)).astype(np.int64)
                for window, dil in ((128, 1), (512, 4), (2048, 16)))
    logc = np.where(count > 0, np.log(np.maximum(count, 1)) / SCALE_A, NEG_HUGE).astype(np.float32)
    eye = np.eye(P, dtype=np.float32)
    return dict(ident=eye, stack_ident=np.concatenate([np.eye(HA, dtype=np.float32)] * 2, 0),
                cos_a=ca, sin_a=sa, cos_b=cb, sin_b=sb, log_count=logc)


def kernel(x_prompt, x_sample, g_attn, w_in, g_q_lora, w_uq, g_kv_lora, w_ukv, g_out_a, g_out_b, w_o,
           g_ffn, w_up, w_conv, b_conv, w_down, g_final):
    import numpy as np
    import concourse.bacc as bacc
    from concourse.bass_utils import run_bass_kernel_spmd

    a = lambda v: np.ascontiguousarray(v)
    conv = np.concatenate([np.asarray(w_conv)[0], np.asarray(b_conv)], 0).reshape(4, 2, NCH, 2, P)
    conv = conv.transpose(4, 2, 3, 1, 0).reshape(P, NCH * 16)
    arrays = dict(
        x_seqs=np.concatenate([np.asarray(x_prompt).reshape(S, D), np.asarray(x_sample).reshape(S, D)], 0),
        g_attn=np.asarray(g_attn)[0], w_in=np.asarray(w_in)[0], g_q=np.asarray(g_q_lora)[0],
        w_uq=np.asarray(w_uq)[0], g_kv=np.asarray(g_kv_lora)[0], w_ukv=np.asarray(w_ukv)[0],
        g_out=np.concatenate([np.asarray(g_out_a)[0], np.asarray(g_out_b)[0]], 0),
        w_o=np.asarray(w_o)[0], g_ffn=np.asarray(g_ffn)[0], w_up=np.asarray(w_up)[0], conv_wb=conv,
        w_down=np.asarray(w_down)[0], g_final=np.asarray(g_final), **tables())
    nc = bacc.Bacc("TRN2", target_bir_lowering=False, num_devices=1)
    args = {}
    for name, v in arrays.items():
        arrays[name] = v = a(v)
        args[name] = nc.dram_tensor(f"in_{name}", v.shape, mybir.dt.from_np(v.dtype), kind="ExternalInput").ap()
    args["out"] = nc.dram_tensor("out_y", (N_SEQ * S, D), F32, kind="ExternalOutput").ap()
    encoder_kernel(nc, **args)
    r = run_bass_kernel_spmd(nc, [{f"in_{k}": v for k, v in arrays.items()}], core_ids=[0])
    y = r.results[0]["out_y"]
    return y[0:S].reshape(np.asarray(x_prompt).shape), y[S:].reshape(np.asarray(x_sample).shape)
```
